# Optimizing a Trainium2 kernel written in Bass

```python
import jax, jax.numpy as jnp
from jax import lax
import numpy as np

D_MODEL = 1024
BATCH = 1
SEQ = 1024
DEPTH = 2
DEC_BATCH = 8
DEC_SEQ = 4
PAST_LEN = 2048
PAGE_SIZE = 128

N_META = 16
D_CONV = D_MODEL // 2
CONV_W = 3
HEAD_DIM = 64
N_HEADS = (D_MODEL // 2) // HEAD_DIM
N_KV = 2
GROUP = N_HEADS // N_KV
WINDOW = 128
BLOCK = 128
Q_DIM = N_HEADS * HEAD_DIM
KV_DIM = N_KV * HEAD_DIM
POOL_WINDOWS = (2, 4, 8, 16)
N_POOL_GROUPS = len(POOL_WINDOWS)
POOL_GROUP_DIM = D_MODEL // N_POOL_GROUPS
POOL_MAX = 16
D_FF = 4 * D_MODEL
EPS = 1e-6
NEG = -1e30
N_EVEN = (DEPTH + 1) // 2
N_ODD = DEPTH // 2
D_IN_EVEN = 3 * D_CONV + Q_DIM + 2 * KV_DIM
D_MIX_EVEN = D_CONV + Q_DIM
SPLITS = (D_CONV, 2 * D_CONV, 3 * D_CONV, 3 * D_CONV + Q_DIM, 3 * D_CONV + Q_DIM + KV_DIM)

kernel_name = 'hybrid_conv_swa_pool_decoder'

def rmsnorm(x, g):
    xf = x.astype(jnp.float32)
    y = xf * lax.rsqrt(jnp.mean(xf * xf, axis=-1, keepdims=True) + EPS)
    return (y * g.astype(jnp.float32)).astype(x.dtype)

def short_conv(xa, gc, gb, buf, conv_w):
    u = gc * xa
    ue = jnp.concatenate([buf.astype(u.dtype), u], axis=1)
    T = u.shape[1]
    y = ue[:, 0:T] * conv_w[0]
    for j in range(1, CONV_W):
        y = y + ue[:, j:j + T] * conv_w[j]
    return gb * y, ue[:, -(CONV_W - 1):]

def sink_softmax_weights(s, sk, dtype):
    m = jnp.maximum(jnp.max(s, axis=-1, keepdims=True), sk)
    p = jnp.exp(s - m)
    denom = jnp.sum(p, axis=-1, keepdims=True) + jnp.exp(sk - m)
    return (p / denom).astype(dtype)

def swa_prompt(q, k, v, sinks):
    B, L = q.shape[:2]
    pad_front = (-N_META) % BLOCK
    lp0 = pad_front + L
    pad_back = (-lp0) % BLOCK
    lp = lp0 + pad_back
    nb = lp // BLOCK
    qp = jnp.pad(q, ((0, 0), (pad_front, pad_back), (0, 0), (0, 0)))
    qp = qp.reshape(B, nb, BLOCK, N_KV, GROUP, HEAD_DIM)
    kvpad = ((0, 0), (pad_front + BLOCK, pad_back), (0, 0), (0, 0))
    kp = jnp.pad(k, kvpad).reshape(B, nb + 1, BLOCK, N_KV, HEAD_DIM)
    vp = jnp.pad(v, kvpad).reshape(B, nb + 1, BLOCK, N_KV, HEAD_DIM)
    kb = jnp.concatenate([kp[:, :-1], kp[:, 1:]], axis=2)
    vb = jnp.concatenate([vp[:, :-1], vp[:, 1:]], axis=2)
    s = jnp.einsum('bnqkgd,bnskd->bnkgqs', qp, kb, preferred_element_type=jnp.float32) * (HEAD_DIM ** -0.5)
    qi = jnp.arange(nb)[:, None] * BLOCK + jnp.arange(BLOCK)[None, :]
    kj = jnp.arange(nb)[:, None] * BLOCK - BLOCK + jnp.arange(2 * BLOCK)[None, :]
    d = qi[:, :, None] - kj[:, None, :]
    valid = (d >= 0) & (d <= WINDOW) & (kj[:, None, :] >= pad_front)
    s = jnp.where(valid[None, :, None, None], s, NEG)
    sk = sinks.astype(jnp.float32).reshape(N_KV, GROUP)[None, None, :, :, None, None]
    p = sink_softmax_weights(s, sk, v.dtype)
    o = jnp.einsum('bnkgqs,bnskd->bnqkgd', p, vb)
    return o.reshape(B, lp, Q_DIM)[:, pad_front:pad_front + L]

def swa_sample(q, k, v, ck, cv, sinks):
    Bd, T = q.shape[:2]
    wb = ck.shape[1]
    ke = jnp.concatenate([ck.astype(k.dtype), k], axis=1)
    ve = jnp.concatenate([cv.astype(v.dtype), v], axis=1)
    qg = q.reshape(Bd, T, N_KV, GROUP, HEAD_DIM)
    s = jnp.einsum('btkgd,bskd->bkgts', qg, ke, preferred_element_type=jnp.float32) * (HEAD_DIM ** -0.5)
    d = (wb + jnp.arange(T))[:, None] - jnp.arange(wb + T)[None, :]
    valid = (d >= 0) & (d <= WINDOW)
    s = jnp.where(valid[None, None, None], s, NEG)
    sk = sinks.astype(jnp.float32).reshape(N_KV, GROUP)[None, :, :, None, None]
    p = sink_softmax_weights(s, sk, v.dtype)
    o = jnp.einsum('bkgts,bskd->btkgd', p, ve).reshape(Bd, T, Q_DIM)
    return o, ke[:, -wb:], ve[:, -wb:]

def pool_mix(h, buf, pos0, w_pool, scale):
    B, T, D = h.shape
    P = POOL_MAX - 1
    he = jnp.concatenate([buf.astype(h.dtype), h], axis=1)
    cs = jnp.cumsum(he.astype(jnp.float32), axis=1)
    cs = jnp.pad(cs, ((0, 0), (1, 0), (0, 0)))
    end = cs[:, P + 1:]
    pos = pos0 + jnp.arange(T)
    groups = []
    for gi, w in enumerate(POOL_WINDOWS):
        sl = slice(gi * POOL_GROUP_DIM, (gi + 1) * POOL_GROUP_DIM)
        start = cs[:, P + 1 - w:P + 1 - w + T, sl]
        cnt = jnp.minimum(w, pos + 1).astype(jnp.float32)[None, :, None]
        groups.append((end[..., sl] - start) / cnt)
    pooled = jnp.concatenate(groups, axis=-1)
    dlt = (pooled - h.astype(jnp.float32)).astype(h.dtype).reshape(B, T, N_POOL_GROUPS, POOL_GROUP_DIM)
    y = jnp.einsum('btgc,gce->btge', dlt, w_pool).reshape(B, T, D)
    return y * scale, he[:, -P:]

def sqrelu_mlp(x, w_up, w_down):
    return jnp.square(jax.nn.relu(x @ w_up)) @ w_down

def trunk(x, pos0, conv_st, k_st, v_st, pool_st, is_prompt, norm_mix, norm_mlp, w_in_even, conv_w,
          q_norm, k_norm, attn_sinks, w_out_even, w_pool, pool_scale, w_up, w_down):
    B, T, _ = x.shape
    conv_new, k_new, v_new, pool_new = [], [], [], []
    for layer in range(DEPTH):
        i = layer // 2
        h = rmsnorm(x, norm_mix[layer])
        if layer % 2 == 0:
            z = h @ w_in_even[i]
            xa, gc, gb, q, k, v = jnp.split(z, SPLITS, axis=-1)
            ya, cbuf = short_conv(xa, gc, gb, conv_st[i], conv_w[i])
            q = rmsnorm(q.reshape(B, T, N_HEADS, HEAD_DIM), q_norm[i])
            k = rmsnorm(k.reshape(B, T, N_KV, HEAD_DIM), k_norm[i])
            v = v.reshape(B, T, N_KV, HEAD_DIM)
            if is_prompt:
                yb = swa_prompt(q, k, v, attn_sinks[i])
                kbuf, vbuf = k[:, -WINDOW:], v[:, -WINDOW:]
            else:
                yb, kbuf, vbuf = swa_sample(q, k, v, k_st[i], v_st[i], attn_sinks[i])
            x = x + jnp.concatenate([ya, yb], axis=-1) @ w_out_even[i]
            conv_new.append(cbuf)
            k_new.append(kbuf)
            v_new.append(vbuf)
        else:
            yc, pbuf = pool_mix(h, pool_st[i], pos0, w_pool[i], pool_scale[i])
            x = x + yc
            pool_new.append(pbuf)
        x = x + sqrelu_mlp(rmsnorm(x, norm_mlp[layer]), w_up[layer], w_down[layer])
    return x, jnp.stack(conv_new), jnp.stack(k_new), jnp.stack(v_new), jnp.stack(pool_new)

def setup_inputs(seed: int = 0) -> dict:
    key = jax.random.key(seed)
    ks = jax.random.split(key, 20)
    f32 = jnp.float32

    def nrm(k, shape, scale):
        return jax.random.normal(k, shape, f32) * scale

    win_rows = min(WINDOW, PAST_LEN)
    return {
        'x_prompt': nrm(ks[0], (BATCH, SEQ, D_MODEL), 1.0),
        'x_sample': nrm(ks[1], (DEC_BATCH, DEC_SEQ, D_MODEL), 1.0),
        'state_conv': nrm(ks[2], (N_EVEN, DEC_BATCH, CONV_W - 1, D_CONV), 1.0),
        'cache_k_win': nrm(ks[3], (N_EVEN, DEC_BATCH, win_rows, N_KV, HEAD_DIM), 1.0),
        'cache_v_win': nrm(ks[4], (N_EVEN, DEC_BATCH, win_rows, N_KV, HEAD_DIM), 1.0),
        'state_pool': nrm(ks[5], (N_ODD, DEC_BATCH, POOL_MAX - 1, D_MODEL), 1.0),
        'meta_tokens': nrm(ks[6], (N_META, D_MODEL), 1.0),
        'norm_mix': 1.0 + nrm(ks[7], (DEPTH, D_MODEL), 0.02),
        'norm_mlp': 1.0 + nrm(ks[8], (DEPTH, D_MODEL), 0.02),
        'w_in_even': nrm(ks[9], (N_EVEN, D_MODEL, D_IN_EVEN), D_MODEL ** -0.5),
        'conv_w': nrm(ks[10], (N_EVEN, CONV_W, D_CONV), CONV_W ** -0.5),
        'q_norm': 1.0 + nrm(ks[11], (N_EVEN, HEAD_DIM), 0.02),
        'k_norm': 1.0 + nrm(ks[12], (N_EVEN, HEAD_DIM), 0.02),
        'attn_sinks': nrm(ks[13], (N_EVEN, N_HEADS), 0.5),
        'w_out_even': nrm(ks[14], (N_EVEN, D_MIX_EVEN, D_MODEL), D_MIX_EVEN ** -0.5),
        'w_pool': nrm(ks[15], (N_ODD, N_POOL_GROUPS, POOL_GROUP_DIM, POOL_GROUP_DIM), POOL_GROUP_DIM ** -0.5),
        'pool_scale': 1.0 + nrm(ks[16], (N_ODD, D_MODEL), 0.1),
        'w_up': nrm(ks[17], (DEPTH, D_MODEL, D_FF), D_MODEL ** -0.5),
        'w_down': nrm(ks[18], (DEPTH, D_FF, D_MODEL), D_FF ** -0.5),
    }

def reference(x_prompt, x_sample, state_conv, cache_k_win, cache_v_win, state_pool, meta_tokens,
              norm_mix, norm_mlp, w_in_even, conv_w, q_norm, k_norm, attn_sinks, w_out_even,
              w_pool, pool_scale, w_up, w_down):
    weights = (norm_mix, norm_mlp, w_in_even, conv_w, q_norm, k_norm, attn_sinks, w_out_even,
               w_pool, pool_scale, w_up, w_down)
    B = x_prompt.shape[0]
    dt = x_prompt.dtype
    meta = jnp.broadcast_to(meta_tokens.astype(dt)[None], (B, N_META, D_MODEL))
    xp = jnp.concatenate([meta, x_prompt], axis=1)
    zero_conv = jnp.zeros((N_EVEN, B, CONV_W - 1, D_CONV), dt)
    zero_pool = jnp.zeros((N_ODD, B, POOL_MAX - 1, D_MODEL), dt)
    hp, conv_p, k_p, v_p, pool_p = trunk(xp, 0, zero_conv, None, None, zero_pool, True, *weights)
    y_prompt = hp[:, N_META:]
    y_sample, conv_s, k_s, v_s, pool_s = trunk(x_sample, PAST_LEN, state_conv, cache_k_win, cache_v_win,
                                               state_pool, False, *weights)
    return (y_prompt, y_sample, conv_p, conv_s, k_p, k_s, v_p, v_s, pool_p, pool_s)


_drawn_inputs = setup_inputs


def setup_inputs(seed=0):
    import zlib

    import numpy as np

    out = dict(_drawn_inputs(seed))
    spreads = {}
    factors = {'norm_mlp': 2.687, 'q_norm': 8.0, 'k_norm': 3.144, 'attn_sinks': 64.0, 'pool_scale': 5.679}
    for name, (base, spread) in spreads.items():
        noise = np.random.default_rng([zlib.crc32(name.encode()), seed]).standard_normal(out[name].shape)
        drawn = base * np.exp(spread * noise) if base else spread * noise
        out[name] = __import__('jax').numpy.asarray(drawn.astype(out[name].dtype))
    for name, factor in factors.items():
        out[name] = (out[name] * factor).astype(out[name].dtype)
    return out
```

```python
from contextlib import ExitStack

import numpy as np

import concourse.bass as bass
from concourse import mybir

F32 = mybir.dt.float32
F32R = mybir.dt.float32r
ALU = mybir.AluOpType
ACT = mybir.ActivationFunctionType
AX_X = mybir.AxisListType.X

P = 128
D = 1024
KC = D // P
SEQ, N_META, NB_S, T_S = 1024, 16, 8, 4
NS = NB_S * T_S
NPR = N_META + SEQ
NT = NPR + NS
DH, N_HEADS, N_KV = 64, 8, 2
W = 128
EPS = 1e-6
QK_SCALE = DH ** -0.5
POOL_W = (2, 4, 8, 16)
PM = 15
D_FF = 4096
GROUPS = D_FF // 512

PIECES = ((0, 368), (368, 720), (720, NT))
PIECES1 = ((N_META, 368), (368, 720), (720, NT))
PW = 368

W_OUT, W_MLP0, W_POOL, W_MLP1, W_END = 18, 26, 90, 92, 156
M_OUT, M_MLP0, M_POOL, M_MLP1 = 54, 102, 390, 414
UP_OUTS, GROUP_OUTS = 12, 36

IN_COLS = [2048, 2176] + [1536 + P * c for c in range(4)]
for _j in range(4):
    IN_COLS += [P * _j, 512 + P * _j, 1024 + P * _j]

N_HALF, N_SAMPLE_HALF = 18, 2
HALVES = N_HALF + N_SAMPLE_HALF
SLOTS = 36
START = [int(1.7 * h) for h in range(HALVES)]
T_LAG, PV_LAG = 2, 3
SK = 4 * W + 16


def last_output(w):
    if w < W_OUT:
        return 9 * (w // 3) + 6 + w % 3
    if w < W_MLP0:
        half, s = divmod(w - W_OUT, 4)
        return M_OUT + 24 * half + 16 + 2 * s + 1
    if W_POOL <= w < W_MLP1:
        return M_POOL + 16 + 4 * (w - W_POOL) + 3
    wb, mb = (W_MLP0, M_MLP0) if w < W_POOL else (W_MLP1, M_MLP1)
    g, s = divmod(w - wb, 8)
    if s < 4:
        return mb + GROUP_OUTS * g + 6 * (s // 2) + 4 + s % 2
    return mb + GROUP_OUTS * g + UP_OUTS + 16 + 2 * (s - 4) + 1


def constants():
    ident = np.eye(P)
    mean_all = np.full((P, P), 1.0 / D)
    mean_head = np.kron(np.eye(2), np.full((DH, DH), 1.0 / DH))
    i, j = np.arange(P)[:, None], np.arange(P)[None, :]
    prompt = np.concatenate([np.where(j >= i, 0, -1e30), np.where(j <= i, 0, -1e30)], 1)
    b, t = (np.arange(P) % 16) // T_S, np.arange(P) % T_S
    cb, cs = np.arange(4 * W) // W, np.arange(4 * W) % W
    cache = np.where((cb[None] == b[:, None]) & (cs[None] >= t[:, None]), 0, -1e30)
    nb, nt = np.arange(16) // T_S, np.arange(16) % T_S
    new = np.where((nb[None] == b[:, None]) & (nt[None] <= t[:, None]), 0, -1e30)
    return np.concatenate([ident, mean_all, mean_head, prompt, cache, new], 1).astype(np.float32)


C_ID, C_MEAN, C_HEAD, C_MASK, C_SMASK = 0, 128, 256, 384, 640
C_COLS = C_SMASK + SK

R_NMIX, R_NMLP, R_CONV, R_SCALE, R_Q, R_K, R_ALL = 0, 16, 32, 44, 52, 53, 54


def trunk_kernel(nc, ins, outs):
    x_prompt, x_sample, meta = ins["x_prompt"], ins["x_sample"], ins["meta_tokens"]
    w_in, w_out = ins["w_in_even"], ins["w_out_even"]
    w_pool, w_up, w_down = ins["w_pool"], ins["w_up"], ins["w_down"]

    ctx = ExitStack()
    with ctx:
        def sem(name):
            return ctx.enter_context(nc.semaphore(name))

        base = (nc.sbuf_base + 63) // 64 * 64

        def place(name, shape, dtype, at):
            at = (at + 31) // 32 * 32
            n = 4
            for s in shape[1:]:
                n *= s
            return nc.alloc_sbuf_tensor_at(name, shape, dtype, offset=at), at + n

        xT, at = place("residual", [P, KC, NT], F32, base)
        act_hi, at = place("act_hi", [P, KC, NT], F32R, at)
        act_lo, at = place("act_lo", [P, KC, NT], F32R, at)
        w_hi, at = place("w_hi", [P, 4, D], F32R, at)
        w_lo, at = place("w_lo", [P, 4, D], F32R, at)
        raw, at = place("raw", [P, 2, D], F32, at)
        const, at = place("const", [P, C_COLS], F32, at)
        prm, at = place("prm", [P, R_ALL + 2], F32, at)
        pool_state, shared = place("pool_state", [P, KC, NB_S * PM], F32, at)

        conv_out, _ = place("conv_out", [P, 4, NT], F32, base)
        n_keys = NT + NB_S * W
        kT, a = place("kT", [P, n_keys], F32, base + 4 * 4 * NT)
        kT_swapped, a = place("kT_swapped", [P, n_keys], F32, a)
        assert a <= base + 4 * KC * NT
        qT, a = place("qT", [P, 4, NT], F32, shared)
        x_again, a = place("x_again", [P, KC, PW], F32, a)
        scores_sb, a = place("scores_sb", [P, 2, D], F32, a)
        v_blocks, vb_at = place("v_blocks", [P, 11, P], F32, a)
        v_cache, a = place("v_cache", [P, NB_S, P], F32, vb_at)
        probsT, pt_end = place("probsT", [P, D], F32, a)
        U_S = 2 + NPR
        conv_u, a = place("conv_u", [P, U_S + NB_S * 6], F32, pt_end)
        xa_sb, a = place("xa_sb", [P, PW], F32, a)
        conv_y, a = place("conv_y", [P, PW], F32, a)
        sink, a = place("sink", [P, 2, 4], F32, a)
        sink_heads, a = place("sink_heads", [P, N_HEADS], F32, a)
        nsink, a = place("nsink", [P, 2, 4], F32, a)
        ssink, a = place("ssink", [P, 2], F32, a)
        conv_state, a = place("conv_state", [P, 4, 16], F32, a)
        conv_tail, a = place("conv_tail", [P, 4, 18], F32, a)
        q_samples, a = place("q_samples", [P, 2, 4, 16], F32, a)
        soft, a = place("soft", [P, 2, 6, 4], F32, a)
        MX, NM, DS, ES, RS, RC = range(6)
        assert a <= nc.sbuf_usable_end, (a, nc.sbuf_usable_end)
        x_rows, a = place("x_rows", [P, 9, D], F32, shared)
        assert a <= vb_at
        cache_rows, a = place("cache_rows", [P, NB_S, P], F32, shared + 4 * 4 * NT)
        pool_rows, a = place("pool_rows", [P, D], F32, a)
        conv_rows, a = place("conv_rows", [P, 512], F32, a)
        k_tail, a = place("k_tail", [P, 2, P], F32, a)
        assert a <= shared + 4 * 4 * NT + 4 * KC * PW
        head_sq, a = place("head_sq", [P, 2, PW], F32, shared + 4 * 4 * NT + 4 * KC * PW)
        head_rs, a = place("head_rs", [P, 2, PW], F32, a)
        v_flat, _ = place("v_flat", [P, NT], F32, pt_end)
        param_rows, _ = place("param_rows", [P, P], F32, pt_end + 4 * 4 * PW)
        conv_tail_rows, a = place("conv_tail_rows", [P, 512], F32, shared + 4 * 4 * NT + 4 * D)

        norm_buf0, a = place("norm_buf0", [P, KC, PW], F32, vb_at - 4 * 11 * P)
        assert a <= pt_end
        norm_sum0, a = place("norm_sum0", [P, PW], F32, pt_end)
        norm_rs0, a = place("norm_rs0", [P, PW], F32, a)

        h_at = shared
        hid_hi, hid_lo = [], []
        for p in range(3):
            t, h_at = place(f"hid_hi{p}", [P, 4, PW], F32R, h_at)
            hid_hi.append(t)
            t, h_at = place(f"hid_lo{p}", [P, 4, PW], F32R, h_at)
            hid_lo.append(t)
        relu, a = place("relu", [P, 2, PW], F32, h_at)
        sq, a = place("sq", [P, 2, PW], F32, a)
        HW_ = 16 + 320 + NB_S * (PM + T_S)
        win, a2 = place("win", [P, 2, 2, HW_], F32, h_at)
        norm_buf, a = place("norm_buf", [P, KC, PW], F32, max(a, a2))
        norm_sum, a = place("norm_sum", [P, PW], F32, a)
        norm_rs, a = place("norm_rs", [P, PW], F32, a)
        pool_tail, _ = place("pool_tail", [P, KC, 47], F32, a)
        a += 4 * KC * 47
        assert a <= nc.sbuf_usable_end, (a, nc.sbuf_usable_end)
        normed01, a = place("normed01", [P, KC, PW], F32, shared)
        normed2, a = place("normed2", [P, KC, HW_], F32, a)
        assert a <= h_at
        tail_rows, _ = place("tail_rows", [P, D], F32, shared)
        y_rows, a = place("y_rows", [P, 9, D], F32, shared)
        assert a <= h_at + 4 * 4 * PW

        ident = const[:, C_ID:C_ID + P]

        out_bank = [ctx.enter_context(nc.psum_tensor(f"out{i}", [P, 512], F32)) for i in range(4)]
        scores = ctx.enter_context(nc.psum_tensor("scores", [P, 2, 512], F32))
        turned = ctx.enter_context(nc.psum_tensor("turned", [P, 512], F32))
        turned2 = ctx.enter_context(nc.psum_tensor("turned2", [P, 512], F32))
        fin_bank = [scores[:, 0, :], scores[:, 1, :], turned[:, :], turned2[:, :]]

        const_in = sem("const_in")
        params_in = sem("params_in")
        sinks_in = sem("sinks_in")
        x_in = [sem(f"x_in{t}") for t in range(9)]
        raw_in = [sem(f"raw_in{i}") for i in range(2)]
        kcache_in, vcache_in = sem("kcache_in"), sem("vcache_in")
        conv_state_in, pool_state_in = sem("conv_state_in"), sem("pool_state_in")
        x_spilled = sem("x_spilled")
        x_again_in = [sem(f"x_again_in{c}") for c in range(KC)]
        k_swapped = sem("k_swapped")
        stored_pool, stored_sp = sem("stored_pool"), sem("stored_sp")
        w_hi_done, w_lo_done = sem("w_hi_done"), sem("w_lo_done")
        out_ready, out_freed = sem("out_ready"), sem("out_freed")
        prm_turned, prm_ready = sem("prm_turned"), sem("prm_ready")
        nsink_ready = sem("nsink_ready")
        x_turned = [sem(f"x_turned{i}") for i in range(2)]
        xT_copied = [sem(f"xT_copied{i}") for i in range(2)]
        norm_sq, norm_summed, norm_mean = sem("norm_sq"), sem("norm_summed"), sem("norm_mean")
        norm_root, norm_rs_done = sem("norm_root"), sem("norm_rs_done")
        norm_scaled, norm_hi = sem("norm_scaled"), sem("norm_hi")
        act_ready = sem("act_ready")
        head_sq_done, head_mean = sem("head_sq_done"), sem("head_mean")
        head_root, head_rs_done = sem("head_root"), sem("head_rs_done")
        eps_ready = sem("eps_ready")
        setup_turned, setup_copied = sem("setup_turned"), sem("setup_copied")
        q_packed = sem("q_packed")
        qk_ready, scores_read = sem("qk_ready"), sem("scores_read")
        soft_in, exp_done, probs_ready = sem("soft_in"), sem("exp_done"), sem("probs_ready")
        probs_turned = sem("probs_turned")
        probsT_dve, probsT_act = sem("probsT_dve"), sem("probsT_act")
        pv_ready, attn_copied = sem("pv_ready"), sem("attn_copied")
        tail_gathered, tail_turned, tail_copied = sem("tail_gathered"), sem("tail_turned"), sem("tail_copied")
        mix_hi, mix_ready = sem("mix_hi"), sem("mix_ready")
        relu_done, hid_hi_done, hid_ready = sem("relu_done"), sem("hid_hi_done"), sem("hid_ready")
        pool_gathered, pool_turned, pool_copied = sem("pool_gathered"), sem("pool_turned"), sem("pool_copied")
        fin_turned = sem("fin_turned")
        fin_dve, fin_act = sem("fin_dve"), sem("fin_act")
        dve_step = sem("dve_step")
        act_step = sem("act_step")

        x_spill = nc.dram_tensor("x_spill", (P, KC, NT), F32, kind="Internal").ap()

        def norm_pieces(n):
            return PIECES if n < 3 else PIECES1

        def norm_tensors(n):
            return (norm_buf0, norm_sum0, norm_rs0) if n == 0 else (norm_buf, norm_sum, norm_rs)

        def gain(n, c):
            row = (R_NMIX, R_NMLP, R_NMIX + KC, R_NMLP + KC)[n] + c
            return prm[:, row:row + 1]

        def half(h):
            n, kv = divmod(h, 2)
            q0 = 0 if n == 0 else N_META + W * (n - 1)
            nq = N_META if n == 0 else W
            k0 = (0, N_META)[n] if n < 2 else W
            return kv, q0, nq, q0 - k0, k0, nq

        def qk_count(h):
            return h + 1 + max(0, h - N_HALF + 1)

        def v_block(n):
            return v_blocks[0:N_META, 8, :] if n == 0 else v_blocks[:, n - 1, :]

        block = ctx.enter_context(nc.Block())

        @block.sync
        def _(sp):
            def load_x(t):
                if t == 0:
                    sp.dma_start(x_rows[0:N_META, 0, :], meta).then_inc(x_in[0], 16)
                    sp.dma_start(x_rows[N_META:P, 0, :], x_prompt[0, 0:P - N_META, :]).then_inc(x_in[0], 16)
                elif t < 8:
                    sp.dma_start(x_rows[:, t, :], x_prompt[0, P * t - N_META:P * (t + 1) - N_META, :])\
                        .then_inc(x_in[t], 16)
                else:
                    sp.dma_start(x_rows[0:N_META, 8, :], x_prompt[0, SEQ - N_META:SEQ, :]).then_inc(x_in[8], 16)
                    sp.dma_start(x_rows[N_META:N_META + NS, 8, :], x_sample.rearrange("b t d -> (b t) d"))\
                        .then_inc(x_in[8], 16)

            def load_step(src, w, g=0, per_group=0):
                if w >= 2:
                    sp.wait_ge(w_lo_done, g * per_group + (w - 1))
                n = src.shape[-1]
                sp.dma_start(raw[:, w % 2, :].rearrange("p (k n) -> p k n", n=n), src).then_inc(raw_in[w % 2], 16)

            def unit_src(weights, col):
                return weights[:, col].rearrange("(k p) n -> p k n", p=P)

            sp.dma_start(const[:, :], ins["const"]).then_inc(const_in, 16)
            for t in range(6):
                load_x(t)
            for w in range(2):
                load_step(unit_src(w_in[0], slice(IN_COLS[w], IN_COLS[w] + P)), w)
            for t in range(6, 9):
                load_x(t)
            for w in range(2, W_OUT):
                load_step(unit_src(w_in[0], slice(IN_COLS[w], IN_COLS[w] + P)), w)
            for i in range(8):
                hh, s = divmod(i, 4)
                load_step(unit_src(w_out[0][512 * hh:512 * (hh + 1), :], slice(256 * s, 256 * (s + 1))), W_OUT + i)

            def load_mlp(layer, wb):
                with sp.Fori(0, GROUPS) as g:
                    for u in range(4):
                        load_step(unit_src(w_up[layer], bass.ds(g * 512 + P * u, P)), wb + u, g, 8)
                    for s in range(4):
                        load_step(unit_src(w_down[layer][bass.ds(g * 512, 512), :], slice(256 * s, 256 * (s + 1))),
                                  wb + 4 + s, g, 8)

            load_mlp(0, W_MLP0)
            for i in range(2):
                load_step(w_pool[0].rearrange("g c e -> (g c) e")[512 * i:512 * (i + 1), :]
                          .rearrange("(k p) n -> p k n", p=P), W_POOL + i)
            load_mlp(1, W_MLP1)

            for t in range(9):
                sp.wait_ge(fin_dve, t + 1)
                sp.wait_ge(fin_act, t + 1)
                if t < 8:
                    sp.dma_start(outs["y_prompt"][0, P * t:P * (t + 1), :], y_rows[:, t, :]).then_inc(stored_sp, 16)
                else:
                    sp.dma_start(outs["y_sample"].rearrange("b t d -> (b t) d"), y_rows[0:NS, 8, :])\
                        .then_inc(stored_sp, 16)
            sp.wait_ge(stored_sp, 16 * 9)

        @block.gpsimd
        def _(pool):
            n_stored = [0]

            def store(dst, src):
                pool.dma_start(dst, src).then_inc(stored_pool, 16)
                n_stored[0] += 1

            rows = [(R_NMIX, ins["norm_mix"].rearrange("l (c p) -> (l c) p", p=P)),
                    (R_NMLP, ins["norm_mlp"].rearrange("l (c p) -> (l c) p", p=P)),
                    (R_CONV, ins["conv_w"][0].rearrange("j (c p) -> (j c) p", p=P)),
                    (R_SCALE, ins["pool_scale"].rearrange("l (c p) -> (l c) p", p=P))]
            for r, src in rows:
                pool.dma_start(param_rows[r:r + src.shape[0], :], src).then_inc(params_in, 16)
            for r, name in ((R_Q, "q_norm"), (R_K, "k_norm")):
                for i in range(2):
                    pool.dma_start(param_rows[r:r + 1, DH * i:DH * (i + 1)], ins[name]).then_inc(params_in, 16)
            pool.dma_start(sink_heads[:, :], ins["attn_sinks"].broadcast_to([P, N_HEADS])).then_inc(sinks_in, 16)
            for kv in range(N_KV):
                for par in range(2):
                    h = 4 * kv + par
                    for j in range(2):
                        r = 32 * (2 * par + kv) + 16 * j
                        pool.dma_start(ssink[r:r + 16, 0:1],
                                       ins["attn_sinks"][0:1, h + 2 * j:h + 2 * j + 1].broadcast_to([16, 1]))\
                            .then_inc(sinks_in, 16)
            for p, (c0, c1) in enumerate(PIECES):
                tiles = (3, 6, 9)[p]
                pool.wait_ge(xT_copied[0], tiles)
                pool.wait_ge(xT_copied[1], tiles)
                pool.dma_start(x_spill[:, :, c0:c1], xT[:, :, c0:c1]).then_inc(x_spilled, 16)
            pool.dma_start(cache_rows[:, :, :], ins["cache_k_win"][0].rearrange("b s k d -> s b (k d)"))\
                .then_inc(kcache_in, 16)
            pool.dma_start(conv_rows[0:2 * NB_S, :], ins["state_conv"][0].rearrange("b r d -> (b r) d"))\
                .then_inc(conv_state_in, 16)
            pool.dma_start(pool_rows[0:NB_S * PM, :], ins["state_pool"][0].rearrange("b r d -> (b r) d"))\
                .then_inc(pool_state_in, 16)
            pool.wait_ge(act_ready, 12)
            pool.dma_start(v_cache[:, :, :], ins["cache_v_win"][0].rearrange("b s k d -> s b (k d)"))\
                .then_inc(vcache_in, 16)
            store(outs["k_sample"][0, :, 0:W - T_S], ins["cache_k_win"][0, :, T_S:W])
            store(outs["v_sample"][0, :, 0:W - T_S], ins["cache_v_win"][0, :, T_S:W])
            store(outs["pool_sample"][0, :, 0:PM - T_S, :], ins["state_pool"][0, :, T_S:PM, :])
            pool.wait_ge(out_freed, 7)
            pool.wait_ge(setup_copied, 2)
            for i in range(2):
                pool.dma_start(kT_swapped[DH * i:DH * (i + 1), :], kT[DH * (1 - i):DH * (2 - i), :])\
                    .then_inc(k_swapped, 16)
            pool.wait_ge(setup_copied, 9)
            store(outs["v_prompt"][0, 0].rearrange("s k d -> s (k d)"), v_blocks[:, 7, :])
            store(outs["k_prompt"][0, 0].rearrange("s k d -> s (k d)"), k_tail[:, 0, :])
            for b in range(NB_S):
                store(outs["k_sample"][0, b, W - T_S:W].rearrange("t k d -> t (k d)"),
                      k_tail[T_S * b:T_S * (b + 1), 1, :])
                a, bb = divmod(b, 4)
                store(outs["v_sample"][0, b, W - T_S:W].rearrange("t k d -> t (k d)"),
                      v_blocks[T_S * bb:T_S * (bb + 1), 9 + a, :])
            for p, (c0, c1) in enumerate(PIECES):
                if p == 0:
                    pool.wait_ge(x_spilled, 48)
                    pool.wait_ge(stored_pool, 16 * n_stored[0])
                for oc in range(KC):
                    if p:
                        pool.wait_ge(out_freed, M_OUT + 8 * (p - 1) + oc + 1)
                    pool.dma_start(x_again[:, oc, 0:c1 - c0], x_spill[:, oc, c0:c1]).then_inc(x_again_in[oc], 16)
            pool.wait_ge(tail_copied, 1)
            store(outs["conv_prompt"][0, 0], conv_tail_rows[0:2, :])
            store(outs["conv_sample"][0].rearrange("b r d -> (b r) d"), conv_tail_rows[2:18, :])
            pool.wait_ge(pool_copied, 2)
            store(outs["pool_prompt"][0, 0], tail_rows[0:PM, :])
            for b in range(NB_S):
                store(outs["pool_sample"][0, b, PM - T_S:PM, :], tail_rows[PM + T_S * b:PM + T_S * (b + 1), :])
            pool.wait_ge(stored_pool, 16 * n_stored[0])

        @block.tensor
        def _(pe):
            def product(out, lhs, rhs, first, last):
                nc.tensor.matmul(out, lhs[0], rhs[0], start=first, stop=False)
                nc.tensor.matmul(out, lhs[0], rhs[1], start=False, stop=False)
                return nc.tensor.matmul(out, lhs[1], rhs[0], start=False, stop=last)

            def stationary(slot, at):
                return w_hi[:, slot, at:at + P], w_lo[:, slot, at:at + P]

            def acts(k, piece):
                c0, c1 = piece
                return act_hi[:, k, c0:c1], act_lo[:, k, c0:c1]

            def take_bank(m, g=0, per_group=0):
                if m >= 4:
                    pe.wait_ge(out_freed, g * per_group + (m - 3))
                return out_bank[m % 4]

            def wait_step(w, g=0, per_group=0):
                pe.wait_ge(w_lo_done, g * per_group + (w + 1))

            def unit_output(m, w, piece, g=0, normed_k=None):
                out = take_bank(m, g, GROUP_OUTS)[:, 0:piece[1] - piece[0]]
                for k in range(KC):
                    if normed_k is not None and k % 2 == 0:
                        pe.wait_ge(act_ready, 4 * normed_k + k // 2 + 1)
                    ins_ = product(out, stationary(w % 4, P * k), acts(k, piece), k == 0, k == KC - 1)
                ins_.then_inc(out_ready, 1)

            def down_output(m, w0, oc, n, rhs, g=0):
                out = take_bank(m, g, GROUP_OUTS)[:, 0:n]
                for k in range(4):
                    ins_ = product(out, stationary((w0 + oc // 2) % 4, 256 * k + P * (oc % 2)), rhs(k), k == 0, k == 3)
                ins_.then_inc(out_ready, 1)

            def norm_stats(n, p):
                k = 3 * n + p
                c0, c1 = norm_pieces(n)[p]
                pe.wait_ge(norm_summed, k + 1)
                if k:
                    pe.wait_ge(norm_root, k)
                nc.tensor.matmul(turned2[:, 0:c1 - c0], const[:, C_MEAN:C_MEAN + P], norm_tensors(n)[1][:, 0:c1 - c0],
                                 start=True, stop=True).then_inc(norm_mean, 1)

            def head_stats(i):
                pe.wait_ge(head_sq_done, i + 1)
                if i:
                    pe.wait_ge(head_root, i)
                p = HEAD_NORMS[i][1]
                n = PIECES[p][1] - PIECES[p][0]
                nc.tensor.matmul(turned[:, 0:n], const[:, C_HEAD:C_HEAD + P], head_sq[:, i % 2, 0:n],
                                 start=True, stop=True).then_inc(head_mean, 1)

            pe.wait_ge(const_in, 16)
            pe.wait_ge(params_in, 16 * 8)
            nc.tensor.transpose(turned[:, 0:R_ALL], param_rows[0:R_ALL, :], ident[0:R_ALL, 0:R_ALL])\
                .then_inc(prm_turned, 1)

            def turn_x(t):
                nr = P if t < 8 else N_META + NS
                pe.wait_ge(x_in[t], 32 if t in (0, 8) else 16)
                for half_ in range(2):
                    if t:
                        pe.wait_ge(xT_copied[half_], t)
                    for c in range(4):
                        cc = 4 * half_ + c
                        ins_ = nc.tensor.transpose(scores[:, half_, P * c:P * c + nr], x_rows[0:nr, t, P * cc:P * (cc + 1)],
                                                   ident[0:nr, 0:nr])
                    ins_.then_inc(x_turned[half_], 1)

            for t in range(3):
                turn_x(t)
            for t in range(3, 6):
                turn_x(t)
            norm_stats(0, 0)
            for t in range(6, 9):
                turn_x(t)
            norm_stats(0, 1)

            HEAD_NORMS = [(m, (m % 9) // 3) for m in range(18) if m < 9 and m % 3 != 1 or m >= 9]

            def setup_round(r, turns):
                if r == 0:
                    pe.wait_ge(xT_copied[0], 9)
                    pe.wait_ge(xT_copied[1], 9)
                if r >= 2:
                    pe.wait_ge(setup_copied, r - 1)
                for at_, in_ in turns:
                    k, m_ = in_.partition_size(), in_.free_size()
                    ins_ = nc.tensor.transpose(scores[0:m_, r % 2, at_:at_ + k], in_, ident[0:k, 0:k])
                ins_.then_inc(setup_turned, 1)

            done_heads = 0
            for m in range(18):
                grp, p, i = m // 9, (m % 9) // 3, m % 3
                w = 3 * grp + i
                if p == 0:
                    wait_step(w)
                unit_output(m, w, PIECES[p], normed_k=p if m < 9 and i == 0 else None)
                if m == 0:
                    norm_stats(0, 2)
                while done_heads < len(HEAD_NORMS) and HEAD_NORMS[done_heads][0] < m:
                    head_stats(done_heads)
                    done_heads += 1
                if m == 8:
                    pe.wait_ge(kcache_in, 16)
                    for r in range(2):
                        setup_round(r, [(P * b, cache_rows[:, 4 * r + b, :]) for b in range(4)])
                if m == 11:
                    pe.wait_ge(out_freed, 8)
                    for r in range(2):
                        setup_round(2 + r, [(P * b, v_flat[:, N_META + W * (4 * r + b):N_META + W * (4 * r + b + 1)])
                                            for b in range(4)])
                if m == 12:
                    pe.wait_ge(setup_copied, 3)
                    for at_, c in ((0, 0), (P, NPR), (2 * P, NPR + 16)):
                        ins_ = nc.tensor.transpose(scores[0:16, 0, at_:at_ + P], v_flat[:, c:c + 16], ident)
                    ins_.then_inc(setup_turned, 1)
                if m == 14:
                    pe.wait_ge(conv_state_in, 16)
                    pe.wait_ge(pool_state_in, 16)
                    pe.wait_ge(setup_copied, 4)
                    for c in range(4):
                        ins_ = nc.tensor.transpose(scores[:, 1, 16 * c:16 * (c + 1)], conv_rows[0:16, P * c:P * (c + 1)],
                                                   ident[0:16, 0:16])
                    ins_.then_inc(setup_turned, 1)
                    for r in range(2):
                        pe.wait_ge(setup_copied, 5 + r)
                        for c in range(4):
                            cc = 4 * r + c
                            ins_ = nc.tensor.transpose(scores[:, r, 120 * c:120 * (c + 1)],
                                                       pool_rows[0:120, P * cc:P * (cc + 1)], ident[0:120, 0:120])
                        ins_.then_inc(setup_turned, 1)
                if m == 16:
                    pe.wait_ge(setup_copied, 7)
                    nc.tensor.transpose(scores[:, 0, 0:P], kT[:, NPR - W:NPR], ident)
                    nc.tensor.transpose(scores[0:NS, 0, P:2 * P], kT[:, NPR:NT], ident).then_inc(setup_turned, 1)
            while done_heads < len(HEAD_NORMS):
                head_stats(done_heads)
                done_heads += 1

            def keys(kv, par, c0, c1):
                return (kT if kv == par else kT_swapped)[DH * par:DH * (par + 1), c0:c1]

            def attn_scores(h):
                if h == 0:
                    pe.wait_ge(out_freed, 18)
                    pe.wait_ge(k_swapped, 32)
                    pe.wait_ge(setup_copied, 8)
                else:
                    pe.wait_ge(scores_read, h)
                if h < N_HALF:
                    kv, q0, nq, key0, k0, k1 = half(h)
                    for par in range(2):
                        for j in range(2):
                            ins_ = nc.tensor.matmul(scores[0:nq, par, 256 * j:256 * j + k0 + k1],
                                                    qT[DH * par:DH * (par + 1), 2 * kv + j, q0:q0 + nq],
                                                    keys(kv, par, key0, key0 + k0 + k1), start=True, stop=True)
                    ins_.then_inc(qk_ready, 1)
                    return
                a = h - N_HALF
                if a == 0:
                    pe.wait_ge(q_packed, 1)
                new = NPR + 16 * a
                for par in range(2):
                    for kv in range(N_KV):
                        r = 32 * (2 * par + kv)
                        q = q_samples[DH * par:DH * (par + 1), a, 2 * kv:2 * kv + 2, :].rearrange("p c n -> p (c n)")
                        nc.tensor.matmul(scores[r:r + 32, 0, :], q, keys(kv, par, NT + 4 * W * a, NT + 4 * W * (a + 1)),
                                         start=True, stop=True)
                        ins_ = nc.tensor.matmul(scores[r:r + 32, 1, 0:16], q, keys(kv, par, new, new + 16),
                                                start=True, stop=True)
                    ins_.then_inc(qk_ready, 1)
                    if par == 0:
                        pe.wait_ge(qk_ready, qk_count(h - 1) + 1)

            def turn_probs(h):
                pe.wait_ge(probs_ready, h + 1)
                if h == 0:
                    pe.wait_ge(head_root, len(HEAD_NORMS))
                    pe.wait_ge(norm_root, 3)
                else:
                    pe.wait_ge(attn_copied, h)
                    pe.wait_ge(probsT_act, h)
                if h < N_HALF:
                    kv, q0, nq, key0, k0, k1 = half(h)
                    for bank, at_, n in ((turned, 0, k0), (turned2, k0, k1)):
                        for e in range(4 if n else 0):
                            ins_ = nc.tensor.transpose(bank[0:n, e * nq:(e + 1) * nq],
                                                       scores_sb[0:nq, h % 2, 256 * e + at_:256 * e + at_ + n],
                                                       ident[0:nq, 0:nq])
                else:
                    for b in range(4):
                        nc.tensor.transpose(turned[:, P * b:P * (b + 1)], scores_sb[:, h % 2, P * b:P * (b + 1)], ident)
                    ins_ = nc.tensor.transpose(turned2[0:16, 0:P], scores_sb[:, h % 2, 4 * P:4 * P + 16], ident)
                ins_.then_inc(probs_turned, 1)

            def attn_values(h):
                if h >= 2:
                    pe.wait_ge(probsT_dve, h - 1)
                pe.wait_ge(probsT_act, h + 1)
                if h < N_HALF:
                    kv, q0, nq, key0, k0, k1 = half(h)
                    n = h // 2
                    for par in range(2):
                        parts = ([(v_block(n - 1), k0, 0)] if k0 else []) + [(v_block(n), k1, 512)]
                        for i, (vb, kn, at_) in enumerate(parts):
                            ins_ = nc.tensor.matmul(turned[DH * par:DH * (par + 1), 0:2 * nq],
                                                    vb[0:kn, DH * kv:DH * (kv + 1)],
                                                    probsT[0:kn, at_ + 2 * par * nq:at_ + 2 * (par + 1) * nq],
                                                    start=i == 0, stop=i == len(parts) - 1)
                else:
                    a = h - N_HALF
                    if a == 0:
                        pe.wait_ge(vcache_in, 16)
                    for par in range(2):
                        for kv in range(N_KV):
                            r = 32 * (2 * par + kv)
                            out = turned[DH * par:DH * (par + 1), 32 * kv:32 * (kv + 1)]
                            for b in range(4):
                                nc.tensor.matmul(out, v_cache[:, 4 * a + b, DH * kv:DH * (kv + 1)],
                                                 probsT[:, P * b + r:P * b + r + 32], start=b == 0, stop=False)
                            ins_ = nc.tensor.matmul(out, v_blocks[0:16, 9 + a, DH * kv:DH * (kv + 1)],
                                                    probsT[0:16, 512 + r:512 + r + 32], start=False, stop=True)
                ins_.then_inc(pv_ready, 1)

            for s in range(SLOTS):
                for h in range(HALVES):
                    if START[h] == s:
                        attn_scores(h)
                m = 18 + s
                w = 6 + 3 * (s // 9) + s % 3
                if (s % 9) // 3 == 0:
                    wait_step(w)
                unit_output(m, w, PIECES[(s % 9) // 3])
                for h in range(HALVES):
                    if START[h] + PV_LAG == s:
                        attn_values(h)
                for h in range(HALVES):
                    if START[h] + T_LAG == s:
                        turn_probs(h)
            for h in range(HALVES):
                if START[h] + PV_LAG >= SLOTS:
                    attn_values(h)

            def w_out_half(half_, hook):
                for p, piece in enumerate(PIECES):
                    pe.wait_ge(mix_ready, 3 * half_ + p + 1)
                    for oc in range(KC):
                        m = M_OUT + 24 * half_ + 8 * p + oc
                        if p == 0 and oc % 2 == 0:
                            wait_step(W_OUT + 4 * half_ + oc // 2)
                        down_output(m, W_OUT + 4 * half_, oc, piece[1] - piece[0],
                                    lambda k: acts(4 * half_ + k, piece))
                        hook(p, oc)

            def conv_tail_turn(p, oc):
                if (p, oc) == (0, 7):
                    pe.wait_ge(tail_gathered, 4)
                    for c in range(4):
                        ins_ = nc.tensor.transpose(scores[0:18, 0, P * c:P * (c + 1)], conv_tail[:, c, :], ident)
                    ins_.then_inc(tail_turned, 1)

            w_out_half(0, conv_tail_turn)

            def stats_hook(n):
                def hook(p, oc):
                    if p and oc == 1:
                        norm_stats(n, p - 1)
                return hook

            w_out_half(1, stats_hook(1))

            def up(layer, mb, wb, g, after=None, normed=None):
                pieces = (PIECES, PIECES1)[layer]
                for u in range(2):
                    for p, piece in enumerate(pieces):
                        for i in range(2):
                            if p == 0:
                                wait_step(wb + 2 * u + i, g, 8)
                            unit_output(mb + 6 * u + 2 * p + i, wb + 2 * u + i, piece, g,
                                        3 * normed + p if normed is not None and u == 0 and i == 0 else None)
                        if after:
                            after(u, p)

            def down(layer, mb, wb, hb, g, hook=None):
                pieces = (PIECES, PIECES1)[layer]
                for p, (c0, c1) in enumerate(pieces):
                    pe.wait_ge(hid_ready, g * UP_OUTS + (hb + 6 + 2 * p + 2))
                    for oc in range(KC):
                        if p == 0 and oc % 2 == 0:
                            wait_step(wb + 4 + oc // 2, g, 8)
                        down_output(mb + UP_OUTS + 8 * p + oc, wb + 4, oc, c1 - c0,
                                    lambda k: (hid_hi[p][:, k, 0:c1 - c0], hid_lo[p][:, k, 0:c1 - c0]), g)
                        if hook:
                            hook(p, oc)

            def at_group(mb, wb, hb, g):
                return mb + GROUP_OUTS * g, wb + 8 * g, hb + UP_OUTS * g

            def mlp(layer, mb, wb, hb, after, normed, hook):
                m0, w0, h0 = mb, wb, hb
                up(layer, m0, w0, 0, after, normed)
                down(layer, m0, w0, h0, 0)
                with pe.Fori(1, GROUPS - 1) as g:
                    up(layer, mb, wb, g)
                    down(layer, mb, wb, hb, g)
                m0, w0, h0 = at_group(mb, wb, hb, GROUPS - 1)
                up(layer, m0, w0, 0)
                down(layer, m0, w0, h0, 0, hook)

            mlp(0, M_MLP0, W_MLP0, 0, lambda u, p: norm_stats(1, 2) if (u, p) == (0, 0) else None, 1, stats_hook(2))

            def pool_outputs(p):
                c0, c1 = PIECES1[p]
                for oc in range(KC):
                    gi = oc // 2
                    m = M_POOL + 8 * p + oc
                    if p == 0 and oc % 4 == 0:
                        wait_step(W_POOL + oc // 4)
                    pe.wait_ge(act_ready, 4 * (6 + p) + gi + 1)
                    out = take_bank(m)[:, 0:c1 - c0]
                    for k in range(2):
                        ins_ = product(out, stationary((W_POOL + gi // 2) % 4, 512 * (gi % 2) + 256 * k + P * (oc % 2)),
                                       acts(2 * gi + k, (c0, c1)), k == 0, k == 1)
                    ins_.then_inc(out_ready, 1)

            pool_outputs(0)
            norm_stats(2, 2)
            pool_outputs(1)
            pool_outputs(2)
            pe.wait_ge(pool_gathered, 1)
            for half_ in range(2):
                for c in range(4):
                    ins_ = nc.tensor.transpose(scores[0:47, half_, P * c:P * (c + 1)], pool_tail[:, 4 * half_ + c, :], ident)
                ins_.then_inc(pool_turned, 1)
            norm_stats(3, 0)

            def turn_y(t):
                c0 = N_META + P * t
                n = P if t < 8 else NS
                for half_ in range(2):
                    i = 2 * t + half_
                    if i >= 4:
                        pe.wait_ge((fin_dve, fin_act)[half_], t - 1)
                    if half_ == 0:
                        last_piece = 0 if c0 + n <= 368 else 1 if c0 + n <= 720 else 2
                        pe.wait_ge(out_freed, M_MLP1 + GROUP_OUTS * (GROUPS - 1) + UP_OUTS + 8 * (last_piece + 1))
                    for c in range(4):
                        cc = 4 * half_ + c
                        ins_ = nc.tensor.transpose(fin_bank[i % 4][0:n, P * c:P * (c + 1)], xT[:, cc, c0:c0 + n], ident)
                    ins_.then_inc(fin_turned, 1)

            def y_hook(p, oc):
                if oc == 3 and p == 1:
                    pe.wait_ge(norm_root, 12)
                    pe.wait_ge(pool_copied, 2)
                    turn_y(0)
                    turn_y(1)
                if p == 2 and oc in (1, 3, 5):
                    turn_y(2 + oc // 2)

            mlp(1, M_MLP1, W_MLP1, 96, lambda u, p: norm_stats(3, p + 1) if u == 0 and p < 2 else None, 3, y_hook)
            for t in range(5, 9):
                turn_y(t)

        @block.scalar
        def _(act):
            def split_hi(w, g=0, per_group=0, last=None):
                act.wait_ge(raw_in[w % 2], g * (8 * per_group) + 16 * (w // 2 + 1))
                if w >= 4:
                    act.wait_ge(out_ready, g * (GROUP_OUTS if per_group else 0) + (last_output(w - 4) + 1))
                nc.scalar.activation(w_hi[:, w % 4, :], raw[:, w % 2, :], ACT.Copy).then_inc(w_hi_done, 1)

            def norm_square(n, p):
                k = 3 * n + p
                c0, c1 = norm_pieces(n)[p]
                if n == 0:
                    act.wait_ge(xT_copied[0], 3 * p + 3)
                    act.wait_ge(xT_copied[1], 3 * p + 3)
                else:
                    last = {1: M_OUT + 24, 2: M_POOL - 24, 3: M_POOL}[n] + 8 * p + 8
                    act.wait_ge(out_freed, last)
                if k:
                    act.wait_ge(act_ready, 4 * k)
                nc.scalar.activation(norm_tensors(n)[0][:, :, 0:c1 - c0], xT[:, :, c0:c1], ACT.Square)\
                    .then_inc(norm_sq, 1)

            def norm_sqrt(n, p):
                k = 3 * n + p
                c0, c1 = norm_pieces(n)[p]
                act.wait_ge(norm_mean, k + 1)
                nc.scalar.activation(norm_tensors(n)[2][:, 0:c1 - c0], turned2[:, 0:c1 - c0], ACT.Sqrt,
                                     bias=prm[:, R_ALL:R_ALL + 1]).then_inc(norm_root, 1)

            def norm_split_hi(n, p, pair):
                k = 3 * n + p
                c0, c1 = norm_pieces(n)[p]
                if n == 2:
                    c0, c1 = PIECES1[p]
                act.wait_ge(norm_scaled, 4 * k + pair + 1)
                nc.scalar.activation(act_hi[:, 2 * pair:2 * pair + 2, c0:c1],
                                     norm_tensors(n)[0][:, 2 * pair:2 * pair + 2, 0:c1 - c0], ACT.Copy)\
                    .then_inc(norm_hi, 1)

            act.wait_ge(prm_turned, 1)
            nc.scalar.activation(prm[:, 0:R_ALL], turned[:, 0:R_ALL], ACT.Copy).then_inc(prm_ready, 1)

            def copy_x(t):
                nr = P if t < 8 else N_META + NS
                act.wait_ge(x_turned[1], t + 1)
                nc.scalar.activation(xT[:, 4:8, P * t:P * t + nr],
                                     scores[:, 1, :].rearrange("p (c n) -> p c n", c=4)[:, :, 0:nr], ACT.Copy)\
                    .then_inc(xT_copied[1], 1)

            for t in range(3):
                copy_x(t)
            norm_square(0, 0)
            for t in range(3, 6):
                copy_x(t)
            split_hi(0)
            split_hi(1)
            act.wait_ge(eps_ready, 1)
            norm_sqrt(0, 0)
            for pair in range(4):
                norm_split_hi(0, 0, pair)
            norm_square(0, 1)
            for t in range(6, 9):
                copy_x(t)
            split_hi(2)
            split_hi(3)
            norm_sqrt(0, 1)
            for pair in range(4):
                norm_split_hi(0, 1, pair)
            norm_square(0, 2)

            def setup_copy(r, dst, src):
                act.wait_ge(setup_turned, r + 1)
                nc.scalar.activation(dst, src, ACT.Copy).then_inc(setup_copied, 1)

            head_outputs = [m for m in range(18) if m >= 9 or m % 3 != 1]

            def head_sqrt(i):
                m = head_outputs[i]
                n = PIECES[(m % 9) // 3][1] - PIECES[(m % 9) // 3][0]
                act.wait_ge(head_mean, i + 1)
                if i >= 2:
                    act.wait_ge(out_freed, head_outputs[i - 2] + 1)
                nc.scalar.activation(head_rs[:, i % 2, 0:n], turned[:, 0:n], ACT.Sqrt, bias=prm[:, R_ALL:R_ALL + 1])\
                    .then_inc(head_root, 1)

            i = 0
            for m in range(18):
                grp, p, part = m // 9, (m % 9) // 3, m % 3
                if m in head_outputs:
                    n = PIECES[p][1] - PIECES[p][0]
                    act.wait_ge(out_ready, m + 1)
                    if i >= 2:
                        act.wait_ge(head_mean, i - 1)
                    nc.scalar.activation(head_sq[:, i % 2, 0:n], out_bank[m % 4][:, 0:n], ACT.Square)\
                        .then_inc(head_sq_done, 1)
                    i += 1
                if m - 1 in head_outputs:
                    head_sqrt(head_outputs.index(m - 1))
                if m == 0:
                    norm_sqrt(0, 2)
                    for pair in range(4):
                        norm_split_hi(0, 2, pair)
                if p == 2:
                    split_hi(3 * grp + part + 4)
                if m == 8:
                    act.wait_ge(x_spilled, 48)
                    for r in range(2):
                        setup_copy(r, kT[:, NT + 4 * W * r:NT + 4 * W * (r + 1)], scores[:, r, :])
                if m == 11:
                    act.wait_ge(act_ready, 12)
                    for r in range(2):
                        setup_copy(2 + r, v_blocks[:, 4 * r:4 * (r + 1), :],
                                   scores[:, r, :].rearrange("p (b n) -> p b n", b=4))
                if m == 12:
                    setup_copy(4, v_blocks[0:16, 8:11, :], scores[0:16, 0, 0:3 * P].rearrange("p (b n) -> p b n", b=3))
                if m == 14:
                    setup_copy(5, conv_state[:, :, :], scores[:, 1, 0:64].rearrange("p (c n) -> p c n", c=4))
                    for r in range(2):
                        setup_copy(6 + r, pool_state[:, 4 * r:4 * (r + 1), :],
                                   scores[:, r, 0:480].rearrange("p (c n) -> p c n", c=4))
                if m == 16:
                    act.wait_ge(setup_turned, 9)
                    nc.scalar.activation(k_tail[0:NS, 1, :], scores[0:NS, 0, P:2 * P], ACT.Copy).then_inc(act_step, 1)
                    act.wait_ge(act_step, 1)
                    nc.scalar.activation(k_tail[:, 0, :], scores[:, 0, 0:P], ACT.Copy).then_inc(setup_copied, 1)

            head_sqrt(len(head_outputs) - 1)

            def exps(h):
                act.wait_ge(soft_in, h + 1)
                s = soft[:, h % 2]
                if h < N_HALF:
                    kv, q0, nq, key0, k0, k1 = half(h)
                    for e in range(4):
                        pr = scores_sb[0:nq, h % 2, 256 * e:256 * e + k0 + k1]
                        nc.scalar.activation(pr, pr, ACT.Exp, bias=s[0:nq, NM, e:e + 1],
                                             accum_out=s[0:nq, RS, e:e + 1])
                    nc.scalar.activation(s[0:nq, ES, :], s[0:nq, DS, :], ACT.Exp).then_inc(exp_done, 1)
                else:
                    pr = scores_sb[:, h % 2, 0:SK]
                    nc.scalar.activation(pr, pr, ACT.Exp, bias=s[:, NM, 0:1], accum_out=s[:, RS, 0:1])
                    nc.scalar.activation(s[:, ES, 0:1], s[:, DS, 0:1], ACT.Exp).then_inc(exp_done, 1)

            def copy_own_probs(h):
                act.wait_ge(probs_turned, h + 1)
                if h < N_HALF:
                    kv, q0, nq, key0, k0, k1 = half(h)
                    nc.scalar.activation(probsT[0:k1, 512:512 + 4 * nq], turned2[0:k1, 0:4 * nq], ACT.Copy)\
                        .then_inc(probsT_act, 1)
                else:
                    nc.scalar.activation(probsT[0:16, 512:512 + P], turned2[0:16, 0:P], ACT.Copy).then_inc(probsT_act, 1)

            for s in range(SLOTS):
                for h in range(HALVES):
                    if START[h] == s:
                        exps(h)
                if (s % 9) // 3 == 2:
                    split_hi(6 + 3 * (s // 9) + s % 3 + 4)
                for h in range(HALVES):
                    if START[h] + T_LAG == s:
                        copy_own_probs(h)

            act.wait_ge(out_ready, M_OUT)
            for p, (c0, c1) in enumerate(PIECES):
                act.wait_ge(out_freed, 45 + 3 * p + 3)
                nc.scalar.activation(act_hi[:, 0:4, c0:c1], conv_out[:, :, c0:c1], ACT.Copy).then_inc(mix_hi, 1)
            act.wait_ge(attn_copied, HALVES)
            for c0, c1 in PIECES:
                nc.scalar.activation(act_hi[:, 4:8, c0:c1], qT[:, :, c0:c1], ACT.Copy).then_inc(mix_hi, 1)
            def splits_half0():
                for s in range(4):
                    split_hi(W_OUT + 4 + s)

            splits_half0()
            act.wait_ge(tail_turned, 1)
            act.wait_ge(out_freed, M_OUT + 24)
            nc.scalar.activation(conv_tail_rows[0:18, :], scores[0:18, 0, :], ACT.Copy).then_inc(tail_copied, 1)

            def normed_pass_hi(n, p, w0):
                norm_square(n, p - 1)
                if p == 1:
                    norm_sqrt(n, 0)
                    for pair in range(4):
                        norm_split_hi(n, 0, pair)
                    return
                for what in ("w0", "r", "w1", "n0", "w2", "n1", "n2", "w3", "n3"):
                    if what[0] == "w":
                        if w0 is not None:
                            split_hi(w0 + int(what[1]))
                    elif what == "r":
                        norm_sqrt(n, p - 1)
                    else:
                        norm_split_hi(n, p - 1, int(what[1]))

            normed_pass_hi(1, 1, None)
            normed_pass_hi(1, 2, W_OUT + 8)
            norm_square(1, 2)

            def hidden(layer, mb, hb, g, u, p, i):
                q = 6 * u + 2 * p + i
                m = mb + q
                c0, c1 = (PIECES, PIECES1)[layer][p]
                n = c1 - c0
                act.wait_ge(out_ready, g * GROUP_OUTS + (m + 1))
                if q >= 2:
                    act.wait_ge(out_freed, g * GROUP_OUTS + (m - 1))
                nc.scalar.activation(relu[:, q % 2, 0:n], out_bank[m % 4][:, 0:n], ACT.Relu).then_inc(relu_done, 1)
                act.wait_ge(relu_done, g * UP_OUTS + (hb + q + 1))
                nc.scalar.activation(hid_hi[p][:, 2 * u + i, 0:n], relu[:, q % 2, 0:n], ACT.Square)\
                    .then_inc(hid_hi_done, 1)

            def up(layer, mb, wb, hb, g, after=None):
                for u in range(2):
                    for p in range(3):
                        for i in range(2):
                            hidden(layer, mb, hb, g, u, p, i)
                        if after:
                            after(u, p)
                    for i in range(2):
                        split_hi(wb + 4 + 2 * u + i, g, 8)

            def down_splits(wb, g):
                for s in range(4):
                    split_hi(wb + 8 + s, g, 8)

            def mlp(layer, mb, wb, hb, after):
                up(layer, mb, wb, hb, 0, after)
                down_splits(wb, 0)
                with act.Fori(1, GROUPS - 1) as g:
                    up(layer, mb, wb, hb, g)
                    down_splits(wb, g)
                last = GROUPS - 1
                up(layer, mb + GROUP_OUTS * last, wb + 8 * last, hb + UP_OUTS * last, 0)

            def norm1_tail(u, p):
                if (u, p) == (0, 0):
                    norm_sqrt(1, 2)
                    for pair in range(4):
                        norm_split_hi(1, 2, pair)

            act.wait_ge(stored_pool, 16 * (N_STORES - 1 - NB_S))
            mlp(0, M_MLP0, W_MLP0, 0, norm1_tail)

            normed_pass_hi(2, 1, None)
            normed_pass_hi(2, 2, W_POOL)
            norm_square(2, 2)
            norm_sqrt(2, 2)
            for pair in range(4):
                norm_split_hi(2, 2, pair)
            norm_square(3, 0)
            split_hi(W_MLP1 + 2)
            split_hi(W_MLP1 + 3)
            for half_ in range(2):
                act.wait_ge(pool_turned, half_ + 1)
                nc.scalar.activation(tail_rows[0:47, 512 * half_:512 * (half_ + 1)], scores[0:47, half_, :], ACT.Copy)\
                    .then_inc(pool_copied, 1)
            norm_sqrt(3, 0)
            for pair in range(4):
                norm_split_hi(3, 0, pair)
            norm_square(3, 1)

            def norm3_tail(u, p):
                if u == 0 and p < 2:
                    norm_sqrt(3, p + 1)
                    for pair in range(4):
                        norm_split_hi(3, p + 1, pair)
                    if p == 0:
                        norm_square(3, 2)

            act.wait_ge(stored_pool, 16 * N_STORES)
            mlp(1, M_MLP1, W_MLP1, 96, norm3_tail)

            for t in range(9):
                n = P if t < 8 else NS
                act.wait_ge(fin_turned, 2 * t + 2)
                nc.scalar.activation(y_rows[0:n, t, 512:1024], fin_bank[(2 * t + 1) % 4][0:n, :], ACT.Copy)\
                    .then_inc(fin_act, 1)

        @block.vector
        def _(dve):
            steps = [0]

            def then(ins_):
                ins_.then_inc(dve_step, 1)
                steps[0] += 1
                dve.wait_ge(dve_step, steps[0])

            def f32(t):
                return t.bitcast(F32)

            def split_lo(w, g=0, per_group=0):
                dve.wait_ge(w_hi_done, g * per_group + (w + 1))
                nc.vector.tensor_tensor(w_lo[:, w % 4, :], raw[:, w % 2, :], f32(w_hi[:, w % 4, :]), ALU.subtract)\
                    .then_inc(w_lo_done, 1)

            def norm_reduce(n, p):
                k = 3 * n + p
                c0, c1 = norm_pieces(n)[p]
                buf, total, _ = norm_tensors(n)
                dve.wait_ge(norm_sq, k + 1)
                nc.vector.tensor_reduce(total[:, 0:c1 - c0], buf[:, :, 0:c1 - c0].rearrange("p c n -> p n c"), AX_X,
                                        ALU.add).then_inc(norm_summed, 1)

            def norm_rsqrt(n, p):
                k = 3 * n + p
                c0, c1 = norm_pieces(n)[p]
                rs = norm_tensors(n)[2][:, 0:c1 - c0]
                dve.wait_ge(norm_root, k + 1)
                nc.vector.reciprocal(rs, rs).then_inc(norm_rs_done, 1)
                dve.wait_ge(norm_rs_done, k + 1)

            def norm_scale(n, p, pair):
                c0, c1 = norm_pieces(n)[p]
                buf, _, rs = norm_tensors(n)
                for c in (2 * pair, 2 * pair + 1):
                    ins_ = nc.vector.scalar_tensor_tensor(out=buf[:, c, 0:c1 - c0], in0=xT[:, c, c0:c1],
                                                          scalar=gain(n, c), in1=rs[:, 0:c1 - c0],
                                                          op0=ALU.mult, op1=ALU.mult)
                ins_.then_inc(norm_scaled, 1)

            def norm_split_lo(n, p, pair):
                k = 3 * n + p
                c0, c1 = PIECES1[p] if n == 2 else norm_pieces(n)[p]
                dve.wait_ge(norm_hi, 4 * k + pair + 1)
                ch = slice(2 * pair, 2 * pair + 2)
                nc.vector.tensor_tensor(act_lo[:, ch, c0:c1], norm_tensors(n)[0][:, ch, 0:c1 - c0],
                                        f32(act_hi[:, ch, c0:c1]), ALU.subtract).then_inc(act_ready, 1)

            def norm_rest(n, p):
                norm_rsqrt(n, p)
                norm_scale(n, p, 0)
                for pair in range(1, 4):
                    norm_scale(n, p, pair)
                    norm_split_lo(n, p, pair - 1)
                norm_split_lo(n, p, 3)

            nc.vector.memset(prm[:, R_ALL:R_ALL + 1], EPS).then_inc(eps_ready, 1)

            def copy_x(t):
                nr = P if t < 8 else N_META + NS
                dve.wait_ge(x_turned[0], t + 1)
                nc.vector.tensor_copy(xT[:, 0:4, P * t:P * t + nr],
                                      scores[:, 0, :].rearrange("p (c n) -> p c n", c=4)[:, :, 0:nr])\
                    .then_inc(xT_copied[0], 1)

            for t in range(3):
                copy_x(t)
            norm_reduce(0, 0)
            for t in range(3, 6):
                copy_x(t)
            dve.wait_ge(prm_ready, 1)
            split_lo(0)
            split_lo(1)
            norm_rest(0, 0)
            norm_reduce(0, 1)
            for t in range(6, 9):
                copy_x(t)
            split_lo(2)
            split_lo(3)
            norm_rest(0, 1)
            norm_reduce(0, 2)

            i = 0
            for m in range(18):
                grp, p, part = m // 9, (m % 9) // 3, m % 3
                c0, c1 = PIECES[p]
                n = c1 - c0
                acc = out_bank[m % 4][:, 0:n]
                if m == 0:
                    dve.wait_ge(x_spilled, 48)
                    norm_rest(0, 2)
                if m == 1:
                    dve.wait_ge(act_ready, 12)
                if grp == 0 and part == 1:
                    dve.wait_ge(out_ready, m + 1)
                    nc.vector.tensor_copy(v_flat[:, c0:c1], acc).then_inc(out_freed, 1)
                else:
                    rs = head_rs[:, i % 2, 0:n]
                    dve.wait_ge(head_root, i + 1)
                    nc.vector.reciprocal(rs, rs).then_inc(head_rs_done, 1)
                    dve.wait_ge(head_rs_done, i + 1)
                    if (grp, part) == (0, 0):
                        dst, row = kT[:, c0:c1], R_K
                    else:
                        dst, row = qT[:, 0 if grp == 0 else part + 1, c0:c1], R_Q
                    nc.vector.scalar_tensor_tensor(out=dst, in0=acc, scalar=prm[:, row:row + 1], in1=rs,
                                                   op0=ALU.mult, op1=ALU.mult).then_inc(out_freed, 1)
                    i += 1
                if p == 2:
                    split_lo(3 * grp + part + 4)

            dve.wait_ge(sinks_in, 16 * 9)
            dve.wait_ge(out_freed, 18)
            nc.vector.tensor_copy(q_samples[:, :, :, :].rearrange("p a c n -> p c a n"),
                                  qT[:, :, NPR:NT].rearrange("p c (a n) -> p c a n", a=2)).then_inc(q_packed, 1)
            by_e = sink_heads[:, :].rearrange("p (k j r) -> p k r j", k=2, j=2)
            for kv in range(N_KV):
                nc.vector.tensor_copy(sink[:, kv, :].rearrange("p (r j) -> p r j", r=2), by_e[:, kv])
                nc.vector.tensor_scalar(nsink[:, kv, :].rearrange("p (r j) -> p r j", r=2), by_e[:, kv], -1.0, None,
                                        ALU.mult)
            then(nc.vector.tensor_scalar(ssink[:, 1:2], ssink[:, 0:1], -1.0, None, ALU.mult))
            dve.wait_ge(setup_copied, 9)
            then(nc.vector.memset(conv_u[:, 0:2], 0.0))

            def mask_and_max(h):
                dve.wait_ge(qk_ready, qk_count(h))
                s = soft[:, h % 2]
                if h >= 2:
                    dve.wait_ge(probs_turned, h - 1)
                if h < N_HALF:
                    kv, q0, nq, key0, k0, k1 = half(h)
                    kn = k0 + k1
                    sv = scores_sb[0:nq, h % 2, :].rearrange("p (e n) -> p e n", e=4)[:, :, 0:kn]
                    ps = scores[0:nq].rearrange("p a (j n) -> p (a j) n", j=2)[:, :, 0:kn]
                    mask = const[0:nq, C_MASK + W - k0:C_MASK + W + k1].unsqueeze(1).to_broadcast([nq, 4, kn])
                    ne, nsk, sk = 4, nsink[0:nq, kv, :], sink[0:nq, kv, :]
                else:
                    nq, ne = P, 1
                    sv, ps = scores_sb[:, h % 2, 0:SK], scores.rearrange("p a n -> p (a n)")[:, 0:SK]
                    mask = const[:, C_SMASK:C_SMASK + SK]
                    nsk, sk = ssink[:, 1:2], ssink[:, 0:1]
                nc.vector.scalar_tensor_tensor(out=sv, in0=ps, scalar=QK_SCALE, in1=mask, op0=ALU.mult, op1=ALU.add)\
                    .then_inc(scores_read, 1)
                dve.wait_ge(scores_read, h + 1)
                then(nc.vector.tensor_reduce(s[0:nq, MX, 0:ne], sv, AX_X, ALU.max))
                then(nc.vector.scalar_tensor_tensor(out=s[0:nq, NM, 0:ne], in0=s[0:nq, MX, 0:ne], scalar=-1.0, in1=nsk,
                                                    op0=ALU.mult, op1=ALU.min))
                nc.vector.tensor_tensor(s[0:nq, DS, 0:ne], sk, s[0:nq, NM, 0:ne], ALU.add).then_inc(soft_in, 1)

            def normalise(h):
                s = soft[:, h % 2]
                nq, ne = (half(h)[2], 4) if h < N_HALF else (P, 1)
                dve.wait_ge(exp_done, h + 1)
                then(nc.vector.tensor_tensor(s[0:nq, RC, 0:ne], s[0:nq, RS, 0:ne], s[0:nq, ES, 0:ne], ALU.add))
                then(nc.vector.reciprocal(s[0:nq, RC, 0:ne], s[0:nq, RC, 0:ne]))
                for e in range(ne):
                    kn = sum(half(h)[4:6]) if h < N_HALF else SK
                    pr = scores_sb[0:nq, h % 2, 256 * e:256 * e + kn]
                    ins_ = nc.vector.tensor_scalar(pr, pr, s[0:nq, RC, e:e + 1], None, ALU.mult)
                ins_.then_inc(probs_ready, 1)

            def copy_attn(h):
                dve.wait_ge(pv_ready, h + 1)
                if h < N_HALF:
                    kv, q0, nq = half(h)[:3]
                    dst = qT[:, 2 * kv:2 * kv + 2, q0:q0 + nq]
                    src = turned[:, 0:2 * nq].rearrange("p (j n) -> p j n", j=2)
                else:
                    a = h - N_HALF
                    dst = qT[:, :, NPR + 16 * a:NPR + 16 * (a + 1)]
                    src = turned[:, 0:64].rearrange("p (c n) -> p c n", c=4)
                nc.vector.tensor_copy(dst, src).then_inc(attn_copied, 1)

            def copy_earlier_probs(h):
                if h < 2:
                    return
                dve.wait_ge(probs_turned, h + 1)
                rows, cols = (half(h)[4], 4 * W) if h < N_HALF else (P, 512)
                nc.vector.tensor_copy(probsT[0:rows, 0:cols], turned[0:rows, 0:cols]).then_inc(probsT_dve, 1)

            def sample_u(first, n):
                return conv_u[:, U_S:U_S + 6 * NB_S].rearrange("p (b r) -> p b r", r=6)[:, :, first:first + n]

            def conv(s):
                j, p, part = s // 9, (s % 9) // 3, s % 3
                c0, c1 = PIECES[p]
                n = c1 - c0
                acc = out_bank[(18 + s) % 4][:, 0:n]
                n_pr = min(c1, NPR) - c0
                parts = [(slice(0, n_pr), None)] + ([(slice(n_pr, n), True)] if n > n_pr else [])

                def rows(sl, samples, ap):
                    v = ap[:, sl]
                    return v.rearrange("p (b t) -> p b t", t=T_S) if samples else v

                dve.wait_ge(out_ready, 18 + s + 1)
                if part == 0:
                    if p == 0:
                        nc.vector.tensor_copy(sample_u(0, 2), conv_state[:, j, :].rearrange("p (b r) -> p b r", r=2))
                    nc.vector.tensor_copy(xa_sb[:, 0:n], acc).then_inc(out_freed, 1)
                    dve.wait_ge(out_freed, 18 + s + 1)
                elif part == 1:
                    for sl, samples in parts:
                        dst = sample_u(2, T_S) if samples else conv_u[:, 2 + c0:2 + c0 + n_pr]
                        ins_ = nc.vector.tensor_tensor(dst, rows(sl, samples, acc), rows(sl, samples, xa_sb), ALU.mult)
                    ins_.then_inc(out_freed, 1)
                    dve.wait_ge(out_freed, 18 + s + 1)
                    for tap in range(3):
                        row = R_CONV + 4 * tap + j
                        wt = prm[:, row:row + 1]
                        for sl, samples in parts:
                            src = sample_u(tap, T_S) if samples else conv_u[:, c0 + tap:c0 + tap + n_pr]
                            y = rows(sl, samples, conv_y)
                            if tap == 0:
                                ins_ = nc.vector.tensor_scalar(y, src, wt, None, ALU.mult)
                            else:
                                ins_ = nc.vector.scalar_tensor_tensor(out=y, in0=src, scalar=wt, in1=y, op0=ALU.mult,
                                                                      op1=ALU.add)
                        then(ins_)
                    if p == 2:
                        nc.vector.tensor_copy(conv_tail[:, j, 0:2], conv_u[:, 2 + NPR - 2:2 + NPR])
                        nc.vector.tensor_copy(conv_tail[:, j, 2:18].rearrange("p (b r) -> p b r", r=2), sample_u(4, 2))\
                            .then_inc(tail_gathered, 1)
                else:
                    nc.vector.tensor_tensor(conv_out[:, j, c0:c1], acc, conv_y[:, 0:n], ALU.mult).then_inc(out_freed, 1)
                if p == 2:
                    split_lo(6 + 3 * j + part + 4)

            for s in range(SLOTS):
                for h in range(HALVES):
                    if START[h] == s:
                        mask_and_max(h)
                for h in range(HALVES):
                    if START[h] + T_LAG == s:
                        normalise(h)
                conv(s)
                for h in range(HALVES):
                    if START[h] + PV_LAG == s:
                        copy_attn(h)
                for h in range(HALVES):
                    if START[h] + T_LAG == s:
                        copy_earlier_probs(h)
            for h in range(HALVES):
                if START[h] + PV_LAG >= SLOTS:
                    copy_attn(h)

            for i, (first, src) in enumerate(((0, conv_out), (4, qT))):
                for p, (c0, c1) in enumerate(PIECES):
                    dve.wait_ge(mix_hi, 3 * i + p + 1)
                    nc.vector.tensor_tensor(act_lo[:, first:first + 4, c0:c1], src[:, :, c0:c1],
                                            f32(act_hi[:, first:first + 4, c0:c1]), ALU.subtract)\
                        .then_inc(mix_ready, 1)

            for p, (c0, c1) in enumerate(PIECES):
                for oc in range(KC):
                    m = M_OUT + 8 * p + oc
                    dve.wait_ge(x_again_in[oc], 16 * (p + 1))
                    dve.wait_ge(out_ready, m + 1)
                    nc.vector.tensor_tensor(xT[:, oc, c0:c1], out_bank[m % 4][:, 0:c1 - c0], x_again[:, oc, 0:c1 - c0],
                                            ALU.add).then_inc(out_freed, 1)
                    if p == 2 and oc % 2:
                        split_lo(W_OUT + 4 + oc // 2)

            def add_output(m, oc, piece, g=0):
                c0, c1 = piece
                dve.wait_ge(out_ready, g * GROUP_OUTS + (m + 1))
                nc.vector.tensor_tensor(xT[:, oc, c0:c1], out_bank[m % 4][:, 0:c1 - c0], xT[:, oc, c0:c1], ALU.add)\
                    .then_inc(out_freed, 1)

            def normed_passes(n, mb, pieces, w0, rsqrt, scale, finish):
                for p in range(3):
                    for oc in range(KC):
                        add_output(mb + 8 * p + oc, oc, pieces[p])
                        if p:
                            if oc == 0:
                                norm_reduce(n, p - 1)
                            if oc == 2:
                                rsqrt(p - 1)
                            if 2 <= oc:
                                scale(p - 1, oc - 2)
                            if 5 <= oc:
                                norm_split_lo(n, p - 1, oc - 5)
                        if p == 2 and oc % 2:
                            split_lo(w0 + oc // 2)
                    if p:
                        norm_split_lo(n, p - 1, 3)
                        finish(p - 1)

            def scale1(p, i):
                if i >= 2:
                    norm_scale(1, p, i - 2)

            normed_passes(1, M_OUT + 24, PIECES, W_OUT + 8, lambda p: norm_rsqrt(1, p), scale1, lambda p: None)
            norm_reduce(1, 2)

            def hidden(layer, mb, hb, g, u, p, i):
                q = 6 * u + 2 * p + i
                m = mb + q
                c0, c1 = (PIECES, PIECES1)[layer][p]
                n = c1 - c0
                dve.wait_ge(relu_done, g * UP_OUTS + (hb + q + 1))
                nc.vector.tensor_tensor(sq[:, q % 2, 0:n], out_bank[m % 4][:, 0:n], relu[:, q % 2, 0:n], ALU.mult)\
                    .then_inc(out_freed, 1)
                dve.wait_ge(out_freed, g * GROUP_OUTS + (m + 1))
                dve.wait_ge(hid_hi_done, g * UP_OUTS + (hb + q + 1))
                nc.vector.tensor_tensor(hid_lo[p][:, 2 * u + i, 0:n], sq[:, q % 2, 0:n],
                                        f32(hid_hi[p][:, 2 * u + i, 0:n]), ALU.subtract).then_inc(hid_ready, 1)

            def up(layer, mb, wb, hb, g, after=None):
                for u in range(2):
                    for p in range(3):
                        for i in range(2):
                            hidden(layer, mb, hb, g, u, p, i)
                        if after:
                            after(u, p)
                    for i in range(2):
                        split_lo(wb + 4 + 2 * u + i, g, 8)

            def down(layer, mb, wb, g):
                for p in range(3):
                    for oc in range(KC):
                        add_output(mb + UP_OUTS + 8 * p + oc, oc, (PIECES, PIECES1)[layer][p], g)
                        if p == 2 and oc % 2:
                            split_lo(wb + 8 + oc // 2, g, 8)

            def mlp(layer, mb, wb, hb, after):
                up(layer, mb, wb, hb, 0, after)
                down(layer, mb, wb, 0)
                with dve.Fori(1, GROUPS - 1) as g:
                    up(layer, mb, wb, hb, g)
                    down(layer, mb, wb, g)
                last = GROUPS - 1
                up(layer, mb + GROUP_OUTS * last, wb + 8 * last, hb + UP_OUTS * last, 0)

            def norm1_tail(u, p):
                if (u, p) == (0, 0):
                    norm_rest(1, 2)

            mlp(0, M_MLP0, W_MLP0, 0, norm1_tail)

            def pool_scale(p, c):
                normed = normed2 if p == 2 else normed01
                c0, c1 = PIECES[p]
                at_ = 0 if p == 0 else 16
                n_pr = min(c1, NPR) - c0
                rs = norm_rs
                ins_ = nc.vector.scalar_tensor_tensor(out=normed[:, c, at_:at_ + n_pr], in0=xT[:, c, c0:c0 + n_pr],
                                                      scalar=gain(2, c), in1=rs[:, 0:n_pr], op0=ALU.mult, op1=ALU.mult)
                if p == 2:
                    smp = normed[:, c, 336:336 + 19 * NB_S].rearrange("p (b r) -> p b r", r=19)
                    ins_ = nc.vector.scalar_tensor_tensor(
                        out=smp[:, :, PM:19], in0=xT[:, c, NPR:NT].rearrange("p (b t) -> p b t", t=T_S),
                        scalar=gain(2, c), in1=rs[:, n_pr:n_pr + NS].rearrange("p (b t) -> p b t", t=T_S),
                        op0=ALU.mult, op1=ALU.mult)
                return ins_

            def pool_pair(p, gi):
                normed, width = (normed2, HW_) if p == 2 else (normed01, PW)
                ch = slice(2 * gi, 2 * gi + 2)
                src, src_ch, shift = normed, ch, 1
                dve.wait_ge(norm_scaled, 4 * (6 + p) + gi)
                for i in range(gi + 1):
                    lo = 2 * shift - 1
                    dst = win[:, i % 2, :, :]
                    a = src[:, src_ch, :] if src is normed else src
                    then(nc.vector.tensor_tensor(dst[:, :, lo:width], a[:, :, lo:width], a[:, :, lo - shift:width - shift],
                                                 ALU.add))
                    src, shift = dst, 2 * shift
                n_pr = (352, 352, 320)[p]
                ins_ = nc.vector.scalar_tensor_tensor(out=norm_buf[:, ch, 0:n_pr], in0=src[:, :, 16:16 + n_pr],
                                                      scalar=1.0 / POOL_W[gi], in1=normed[:, ch, 16:16 + n_pr],
                                                      op0=ALU.mult, op1=ALU.subtract)
                if p == 2:
                    def smp(t):
                        return t[:, :, 336:336 + 19 * NB_S].rearrange("p c (b r) -> p c b r", r=19)[:, :, :, PM:19]
                    for c in range(2):
                        ins_ = nc.vector.scalar_tensor_tensor(
                            out=norm_buf[:, 2 * gi + c, n_pr:n_pr + NS].rearrange("p (b t) -> p b t", t=T_S),
                            in0=smp(src)[:, c], scalar=1.0 / POOL_W[gi], in1=smp(normed[:, ch, :])[:, c],
                            op0=ALU.mult, op1=ALU.subtract)
                ins_.then_inc(norm_scaled, 1)

            def scale2(p, i):
                if i == 0:
                    for c in range(4):
                        pool_scale(p, c)
                elif i == 1:
                    for c in range(4, 7):
                        pool_scale(p, c)
                    then(pool_scale(p, 7))
                else:
                    pool_pair(p, i - 2)

            def carry(p):
                then(nc.vector.tensor_copy((normed01, normed2)[p][:, :, 0:16], normed01[:, :, PW - 16:PW]))

            normed_passes(2, M_POOL - 24, PIECES, W_POOL, lambda p: norm_rsqrt(2, p), scale2, carry)

            def add_pooled(p, split=None):
                c0, c1 = PIECES1[p]
                for oc in range(KC):
                    m = M_POOL + 8 * p + oc
                    dve.wait_ge(out_ready, m + 1)
                    nc.vector.scalar_tensor_tensor(out=xT[:, oc, c0:c1], in0=out_bank[m % 4][:, 0:c1 - c0],
                                                   scalar=prm[:, R_SCALE + oc:R_SCALE + oc + 1], in1=xT[:, oc, c0:c1],
                                                   op0=ALU.mult, op1=ALU.add).then_inc(out_freed, 1)
                    if split is not None and oc % 4 == 3:
                        split_lo(split + oc // 4)

            norm_reduce(2, 2)
            add_pooled(0)
            norm_rsqrt(2, 2)
            nc.vector.tensor_copy(normed2[:, :, 336:336 + 19 * NB_S].rearrange("p c (b r) -> p c b r", r=19)[:, :, :, 0:PM],
                                  pool_state[:, :, :].rearrange("p c (b r) -> p c b r", r=PM))
            for i in range(3):
                scale2(2, i)
            for pair in range(1, 4):
                scale2(2, 2 + pair)
                norm_split_lo(2, 2, pair - 1)
            norm_split_lo(2, 2, 3)
            nc.vector.tensor_copy(pool_tail[:, :, 0:PM], normed2[:, :, 336 - PM:336])
            for c in range(KC):
                ins_ = nc.vector.tensor_copy(
                    pool_tail[:, c, PM:PM + NS].rearrange("p (b t) -> p b t", t=T_S),
                    normed2[:, c, 336:336 + 19 * NB_S].rearrange("p (b r) -> p b r", r=19)[:, :, PM:19])
            ins_.then_inc(pool_gathered, 1)
            add_pooled(1)
            norm_reduce(3, 0)
            add_pooled(2, W_MLP1 + 2)
            norm_rest(3, 0)
            norm_reduce(3, 1)

            def norm3_tail(u, p):
                if u == 0 and p < 2:
                    norm_rest(3, p + 1)
                    if p == 0:
                        norm_reduce(3, 2)

            mlp(1, M_MLP1, W_MLP1, 96, norm3_tail)

            def copy_y(t):
                n = P if t < 8 else NS
                dve.wait_ge(fin_turned, 2 * t + 1)
                nc.vector.tensor_copy(y_rows[0:n, t, 0:512], fin_bank[(2 * t) % 4][0:n, :]).then_inc(fin_dve, 1)

            mb = M_MLP1 + GROUP_OUTS * (GROUPS - 1) + UP_OUTS
            for p in range(3):
                for oc in range(KC):
                    add_output(mb + 8 * p + oc, oc, PIECES1[p])
                    if p == 1 and oc == 4:
                        copy_y(0)
                        copy_y(1)
                    if p == 2 and oc in (2, 4, 6):
                        copy_y(1 + oc // 2)
            for t in range(5, 9):
                copy_y(t)


N_STORES = 3 + 2 + 2 * NB_S + 2 + 1 + NB_S

_INS = ["x_prompt", "x_sample", "state_conv", "cache_k_win", "cache_v_win", "state_pool", "meta_tokens", "norm_mix",
        "norm_mlp", "w_in_even", "conv_w", "q_norm", "k_norm", "attn_sinks", "w_out_even", "w_pool", "pool_scale",
        "w_up", "w_down"]
_OUTS = [("y_prompt", (1, SEQ, D)), ("y_sample", (NB_S, T_S, D)), ("conv_prompt", (1, 1, 2, 512)),
         ("conv_sample", (1, NB_S, 2, 512)), ("k_prompt", (1, 1, W, N_KV, DH)), ("k_sample", (1, NB_S, W, N_KV, DH)),
         ("v_prompt", (1, 1, W, N_KV, DH)), ("v_sample", (1, NB_S, W, N_KV, DH)), ("pool_prompt", (1, 1, PM, D)),
         ("pool_sample", (1, NB_S, PM, D))]


def kernel(**inputs):
    import concourse.bacc as _bacc
    from concourse.bass_utils import run_bass_kernel_spmd as _run

    nc = _bacc.Bacc("TRN2", target_bir_lowering=False, num_devices=1)
    arrays = {n: np.ascontiguousarray(inputs[n]) for n in _INS}
    arrays["const"] = constants()
    ins = {n: nc.dram_tensor(f"in_{n}", a.shape, F32, kind="ExternalInput").ap() for n, a in arrays.items()}
    outs = {n: nc.dram_tensor(f"out_{n}", s, F32, kind="ExternalOutput").ap() for n, s in _OUTS}
    trunk_kernel(nc, ins, outs)
    r = _run(nc, [{f"in_{n}": a for n, a in arrays.items()}], core_ids=[0])
    return tuple(r.results[0][f"out_{n}"] for n, _ in _OUTS)
```

```python
from contextlib import ExitStack

import numpy as np

import concourse.bass as bass
from concourse import mybir

F32 = mybir.dt.float32
F32R = mybir.dt.float32r
ALU = mybir.AluOpType
ACT = mybir.ActivationFunctionType
AX_X = mybir.AxisListType.X

P = 128
D = 1024
KC = D // P
SEQ, N_META, NB_S, T_S = 1024, 16, 8, 4
NS = NB_S * T_S
NPR = N_META + SEQ
NT = NPR + NS
DH, N_HEADS, N_KV = 64, 8, 2
W = 128
EPS = 1e-6
QK_SCALE = DH ** -0.5
POOL_W = (2, 4, 8, 16)
PM = 15
D_FF = 4096
GROUPS = D_FF // 512

PIECES = ((0, 368), (368, 720), (720, NT))
PIECES1 = ((N_META, 368), (368, 720), (720, NT))
PW = 368

W_OUT, W_MLP0, W_POOL, W_MLP1, W_END = 18, 26, 90, 92, 156
M_OUT, M_MLP0, M_POOL, M_MLP1 = 54, 102, 390, 414
UP_OUTS, GROUP_OUTS = 12, 36

IN_COLS = [2048, 2176] + [1536 + P * c for c in range(4)]
for _j in range(4):
    IN_COLS += [P * _j, 512 + P * _j, 1024 + P * _j]

N_HALF, N_SAMPLE_HALF = 18, 2
HALVES = N_HALF + N_SAMPLE_HALF
SLOTS = 36
START = [1 + int(1.65 * h) for h in range(HALVES)]
T_LAG, PV_LAG = 2, 3
SK = 4 * W + 16


def last_output(w, in_loop=False):
    if w < W_OUT:
        return 9 * (w // 3) + 6 + w % 3
    if w < W_MLP0:
        half, s = divmod(w - W_OUT, 4)
        return M_OUT + 24 * half + 16 + 2 * s + 1
    if W_POOL <= w < W_MLP1:
        return M_POOL + 16 + 4 * (w - W_POOL) + 3
    wb, mb = (W_MLP0, M_MLP0) if w < W_POOL else (W_MLP1, M_MLP1)
    g, s = divmod(w - wb, 8)
    if s < 4 and w >= W_MLP1 and g == 0 and not in_loop:
        return mb + 8 + s
    if s < 4:
        return mb + GROUP_OUTS * g + 6 * (s // 2) + 4 + s % 2
    return mb + GROUP_OUTS * g + UP_OUTS + 16 + 2 * (s - 4) + 1


def constants():
    ident = np.eye(P)
    mean_all = np.full((P, P), 1.0 / D)
    mean_head = np.kron(np.eye(2), np.full((DH, DH), 1.0 / DH))
    i, j = np.arange(P)[:, None], np.arange(P)[None, :]
    prompt = np.concatenate([np.where(j >= i, 0, -1e30), np.where(j <= i, 0, -1e30)], 1)
    b, t = (np.arange(P) % 16) // T_S, np.arange(P) % T_S
    cb, cs = np.arange(4 * W) // W, np.arange(4 * W) % W
    cache = np.where((cb[None] == b[:, None]) & (cs[None] >= t[:, None]), 0, -1e30)
    nb, nt = np.arange(16) // T_S, np.arange(16) % T_S
    new = np.where((nb[None] == b[:, None]) & (nt[None] <= t[:, None]), 0, -1e30)
    return np.concatenate([ident, mean_all, mean_head, prompt, cache, new], 1).astype(np.float32)


C_ID, C_MEAN, C_HEAD, C_MASK, C_SMASK = 0, 128, 256, 384, 640
C_COLS = C_SMASK + SK

R_NMIX, R_NMLP, R_CONV, R_SCALE, R_Q, R_K, R_ALL = 0, 16, 32, 44, 52, 53, 54


def trunk_kernel(nc, ins, outs):
    x_prompt, x_sample, meta = ins["x_prompt"], ins["x_sample"], ins["meta_tokens"]
    w_in, w_out = ins["w_in_even"], ins["w_out_even"]
    w_pool, w_up, w_down = ins["w_pool"], ins["w_up"], ins["w_down"]

    ctx = ExitStack()
    with ctx:
        def sem(name):
            return ctx.enter_context(nc.semaphore(name))

        base = (nc.sbuf_base + 63) // 64 * 64

        def place(name, shape, dtype, at):
            at = (at + 31) // 32 * 32
            n = 4
            for s in shape[1:]:
                n *= s
            return nc.alloc_sbuf_tensor_at(name, shape, dtype, offset=at), at + n

        xT, at = place("residual", [P, KC, NT], F32, base)
        act_hi, at = place("act_hi", [P, KC, NT], F32R, at)
        act_lo, at = place("act_lo", [P, KC, NT], F32R, at)
        w_hi, at = place("w_hi", [P, 4, D], F32R, at)
        w_lo, at = place("w_lo", [P, 4, D], F32R, at)
        raw, at = place("raw", [P, 2, D], F32, at)
        const, at = place("const", [P, C_COLS], F32, at)
        const_at = at - 4 * C_COLS
        prm, at = place("prm", [P, R_ALL + 2], F32, at)
        rs, shared = place("rs", [P, NT], F32, at)

        conv_out, _ = place("conv_out", [P, 4, NT], F32, base)
        n_keys = NT + NB_S * W
        kT, a = place("kT", [P, n_keys], F32, base + 4 * 4 * NT)
        kT_swapped, a = place("kT_swapped", [P, n_keys], F32, a)
        assert a <= base + 4 * KC * NT
        qT, a = place("qT", [P, 4, NT], F32, shared)
        x_again, a = place("x_again", [P, KC, PW], F32, a)
        scores_sb, a = place("scores_sb", [P, 2, D], F32, a)
        v_blocks, vb_at = place("v_blocks", [P, 11, P], F32, a)
        v_cache, a = place("v_cache", [P, NB_S, P], F32, vb_at)
        probsT, pt_end = place("probsT", [P, D], F32, a)
        U_S = 2 + NPR
        conv_u, a = place("conv_u", [P, U_S + NB_S * 6], F32, pt_end)
        xa_at = a
        xa_sb, a = place("xa_sb", [P, PW], F32, a)
        conv_y, a = place("conv_y", [P, PW], F32, a)
        sink, a = place("sink", [P, 2, 4], F32, a)
        sink_heads, a = place("sink_heads", [P, N_HEADS], F32, a)
        nsink, a = place("nsink", [P, 2, 4], F32, a)
        ssink, a = place("ssink", [P, 2], F32, a)
        conv_state, a = place("conv_state", [P, 4, 16], F32, a)
        conv_tail, a = place("conv_tail", [P, 4, 18], F32, a)
        q_samples, a = place("q_samples", [P, 2, 4, 16], F32, a)
        soft, a = place("soft", [P, 2, 6, 4], F32, a)
        MX, NM, DS, ES, RS, RC = range(6)
        assert a <= nc.sbuf_usable_end, (a, nc.sbuf_usable_end)
        x_rows, a = place("x_rows", [P, 9, D], F32, shared)
        assert a <= vb_at
        cache_rows, a = place("cache_rows", [P, NB_S, P], F32, shared + 4 * 4 * NT)
        rs_squared, a = place("rs_squared", [P, NT], F32, a)
        conv_rows, a = place("conv_rows", [P, 512], F32, a)
        k_tail, a = place("k_tail", [P, 2, P], F32, a)
        assert a <= shared + 4 * 4 * NT + 4 * KC * PW
        v_flat, _ = place("v_flat", [P, NT], F32, pt_end)
        param_rows, _ = place("param_rows", [P, P], F32, pt_end + 4 * 4 * PW)
        conv_tail_rows, a = place("conv_tail_rows", [P, 512], F32, shared + 4 * 4 * NT + 4 * D)

        norm_buf0, a = place("norm_buf0", [P, 4, PW], F32, vb_at - 4 * 11 * P)
        k_flat, a = place("k_flat", [P, NT], F32, a)
        head_sq, a = place("head_sq", [P, 2, PW], F32, a)
        assert a <= pt_end
        norm_sum0, a = place("norm_sum0", [P, 2, PW], F32, xa_at)
        assert a <= xa_at + 4 * 2 * PW + 64

        h_at = shared
        hid_hi, hid_lo = [], []
        for p in range(3):
            width = PIECES[p][1] - PIECES[p][0] if p == 2 else PW
            t, h_at = place(f"hid_hi{p}", [P, 4, width], F32R, h_at)
            hid_hi.append(t)
            t, h_at = place(f"hid_lo{p}", [P, 4, width], F32R, h_at)
            hid_lo.append(t)
        HW_ = 16 + 320 + NB_S * (PM + T_S)
        relu, a = place("relu", [P, 2, PW], F32, h_at)
        sq, a = place("sq", [P, 2, PW], F32, a)
        HW_ = 16 + 320 + NB_S * (PM + T_S)
        norm_buf, a = place("norm_buf", [P, 4, PW], F32, a)
        pool_rows, _ = place("pool_rows", [P, D], F32, a)
        win, a = place("win", [P, 2, 2, HW_], F32, a)
        pool_state_at = a
        pool_state, a = place("pool_state", [P, KC, NB_S * PM], F32, a)
        assert a <= nc.sbuf_usable_end, (a, nc.sbuf_usable_end)
        norm_sum, a = place("norm_sum", [P, 2, PW], F32, const_at + 4 * C_MASK)
        assert a <= const_at + 4 * C_COLS
        z0, a = place("z0", [P, KC, PW], F32, shared)
        z1, a = place("z1", [P, KC, PW], F32, a)
        z2, a = place("z2", [P, KC, 336], F32, a)
        assert a <= h_at
        z = (z0, z1, z2)
        z_samples, a = place("z_samples", [P, KC, 19 * NB_S], F32, pool_state_at)
        assert a <= nc.sbuf_usable_end
        tail_rows, a = place("tail_rows", [P, D], F32, h_at)
        pool_tail, a = place("pool_tail", [P, KC, 47], F32, a)
        assert a <= h_at + 4 * 4 * PW
        y_rows, a = place("y_rows", [P, 9, D], F32, shared)
        assert a <= h_at + 4 * 4 * PW

        ident = const[:, C_ID:C_ID + P]

        out_bank = [ctx.enter_context(nc.psum_tensor(f"out{i}", [P, 512], F32)) for i in range(4)]
        scores = ctx.enter_context(nc.psum_tensor("scores", [P, 2, 512], F32))
        turned = ctx.enter_context(nc.psum_tensor("turned", [P, 512], F32))
        turned2 = ctx.enter_context(nc.psum_tensor("turned2", [P, 512], F32))
        fin_bank = [scores[:, 0, :], scores[:, 1, :], turned[:, :], turned2[:, :]]

        ident_in, mean_in = sem("ident_in"), sem("mean_in")
        params_in = sem("params_in")
        sinks_in = sem("sinks_in")
        x_in = [sem(f"x_in{t}") for t in range(9)]
        raw_in = [sem(f"raw_in{i}") for i in range(2)]
        kcache_in, vcache_in = sem("kcache_in"), sem("vcache_in")
        masks_in = sem("masks_in")
        conv_state_in, pool_state_in = sem("conv_state_in"), sem("pool_state_in")
        x_spilled = sem("x_spilled")
        x_again_in = [sem(f"x_again_in{c}") for c in range(KC)]
        k_moved, k_swapped = sem("k_moved"), sem("k_swapped")
        stored_pool, stored_sp = sem("stored_pool"), sem("stored_sp")
        w_hi_done, w_lo_done = sem("w_hi_done"), sem("w_lo_done")
        out_ready, out_freed = sem("out_ready"), sem("out_freed")
        prm_turned, prm_ready = sem("prm_turned"), sem("prm_ready")
        nsink_ready = sem("nsink_ready")
        x_turned = [sem(f"x_turned{i}") for i in range(2)]
        xT_copied = [sem(f"xT_copied{i}") for i in range(2)]
        norm_sq, norm_summed, norm_mean = sem("norm_sq"), sem("norm_summed"), sem("norm_mean")
        norm_root, norm_rs_done = sem("norm_root"), sem("norm_rs_done")
        norm_hi = sem("norm_hi")
        act_ready = sem("act_ready")
        head_scaled = sem("head_scaled")
        head_sq_done, head_mean = sem("head_sq_done"), sem("head_mean")
        head_root, head_rs_done = sem("head_root"), sem("head_rs_done")
        eps_ready = sem("eps_ready")
        setup_turned, setup_copied = sem("setup_turned"), sem("setup_copied")
        q_packed = sem("q_packed")
        qk_ready, scores_read = sem("qk_ready"), sem("scores_read")
        soft_in, exp_done, probs_ready = sem("soft_in"), sem("exp_done"), sem("probs_ready")
        probs_turned = sem("probs_turned")
        probsT_dve, probsT_act = sem("probsT_dve"), sem("probsT_act")
        pv_ready, attn_copied = sem("pv_ready"), sem("attn_copied")
        tail_gathered, tail_turned, tail_copied = sem("tail_gathered"), sem("tail_turned"), sem("tail_copied")
        mix_hi, mix_ready = sem("mix_hi"), sem("mix_ready")
        hid_sq_done, hid_hi_done, hid_ready = sem("hid_sq_done"), sem("hid_hi_done"), sem("hid_ready")
        pool_state_turned, pool_state_copied = sem("pool_state_turned"), sem("pool_state_copied")
        state_mapped, states_placed = sem("state_mapped"), sem("states_placed")
        x_pooled = sem("x_pooled")
        pool_gathered, pool_turned, pool_copied = sem("pool_gathered"), sem("pool_turned"), sem("pool_copied")
        fin_turned = sem("fin_turned")
        fin_dve, fin_act = sem("fin_dve"), sem("fin_act")
        dve_step = sem("dve_step")
        act_step = sem("act_step")

        x_spill = nc.dram_tensor("x_spill", (P, KC, NT), F32, kind="Internal").ap()

        def norm_pieces(n):
            return PIECES if n < 3 else PIECES1

        def norm_tensors(n):
            return (norm_buf0, norm_sum0) if n == 0 else (norm_buf, norm_sum)

        def gain(n, c):
            row = (R_NMIX, R_NMLP, R_NMIX + KC, R_NMLP + KC)[n] + c
            return prm[:, row:row + 1]

        def half(h):
            n, kv = divmod(h, 2)
            q0 = 0 if n == 0 else N_META + W * (n - 1)
            nq = N_META if n == 0 else W
            k0 = (0, N_META)[n] if n < 2 else W
            return kv, q0, nq, q0 - k0, k0, nq

        def qk_count(h):
            return h + 1 + max(0, h - N_HALF + 1)

        def v_block(n):
            return v_blocks[0:N_META, 8, :] if n == 0 else v_blocks[:, n - 1, :]

        SETUPS = 7
        block = ctx.enter_context(nc.Block())

        @block.sync
        def _(sp):
            def load_x(t):
                if t == 0:
                    sp.dma_start(x_rows[0:N_META, 0, :], meta).then_inc(x_in[0], 16)
                    sp.dma_start(x_rows[N_META:P, 0, :], x_prompt[0, 0:P - N_META, :]).then_inc(x_in[0], 16)
                elif t < 8:
                    sp.dma_start(x_rows[:, t, :], x_prompt[0, P * t - N_META:P * (t + 1) - N_META, :])\
                        .then_inc(x_in[t], 16)
                else:
                    sp.dma_start(x_rows[0:N_META, 8, :], x_prompt[0, SEQ - N_META:SEQ, :]).then_inc(x_in[8], 16)
                    sp.dma_start(x_rows[N_META:N_META + NS, 8, :], x_sample.rearrange("b t d -> (b t) d"))\
                        .then_inc(x_in[8], 16)

            def load_step(src, w, g=0, per_group=0):
                if w >= 2:
                    sp.wait_ge(w_lo_done, g * per_group + (w - 1))
                if W_POOL + 2 <= w < W_POOL + 4 and per_group == 0:
                    sp.wait_ge(state_mapped, w - W_POOL - 1)
                n = src.shape[-1]
                sp.dma_start(raw[:, w % 2, :].rearrange("p (k n) -> p k n", n=n), src).then_inc(raw_in[w % 2], 16)

            def unit_src(weights, col):
                return weights[:, col].rearrange("(k p) n -> p k n", p=P)

            def load_in(w):
                load_step(unit_src(w_in[0], slice(IN_COLS[w], IN_COLS[w] + P)), w)

            for t in range(3):
                load_x(t)
            load_in(0)
            load_in(1)
            for t in range(3, 9):
                load_x(t)
            for w in range(2, W_OUT):
                load_in(w)
            for i in range(8):
                hh, s = divmod(i, 4)
                load_step(unit_src(w_out[0][512 * hh:512 * (hh + 1), :], slice(256 * s, 256 * (s + 1))), W_OUT + i)

            def load_group(layer, wb, g, first=0):
                at_ = (lambda n: slice(0, n)) if g is None else (lambda n: bass.ds(g * 512, n))
                for u in range(first, 4):
                    cols = slice(P * u, P * (u + 1)) if g is None else bass.ds(g * 512 + P * u, P)
                    load_step(unit_src(w_up[layer], cols), wb + u, 0 if g is None else g, 0 if g is None else 8)
                for s in range(4):
                    load_step(unit_src(w_down[layer][at_(512), :], slice(256 * s, 256 * (s + 1))),
                              wb + 4 + s, 0 if g is None else g, 0 if g is None else 8)

            def load_mlp(layer, wb, first):
                load_group(layer, wb, None, first)
                with sp.Fori(1, GROUPS) as g:
                    load_group(layer, wb, g)

            load_mlp(0, W_MLP0, 0)
            for i in range(2):
                load_step(w_pool[0].rearrange("g c e -> (g c) e")[512 * i:512 * (i + 1), :]
                          .rearrange("(k p) n -> p k n", p=P), W_POOL + i)
            for u in range(2):
                load_step(unit_src(w_up[1], slice(P * u, P * (u + 1))), W_MLP1 + u)
            load_mlp(1, W_MLP1, 2)

            for t in range(9):
                sp.wait_ge(fin_dve, t + 1)
                sp.wait_ge(fin_act, t + 1)
                if t < 8:
                    sp.dma_start(outs["y_prompt"][0, P * t:P * (t + 1), :], y_rows[:, t, :]).then_inc(stored_sp, 16)
                else:
                    sp.dma_start(outs["y_sample"].rearrange("b t d -> (b t) d"), y_rows[0:NS, 8, :])\
                        .then_inc(stored_sp, 16)
            sp.wait_ge(stored_sp, 16 * 9)

        @block.gpsimd
        def _(pool):
            n_stored = [0]

            def store(dst, src):
                pool.dma_start(dst, src).then_inc(stored_pool, 16)
                n_stored[0] += 1

            for p, (c0, c1) in enumerate(PIECES):
                tiles = (3, 6, 9)[p]
                pool.wait_ge(xT_copied[0], tiles)
                pool.wait_ge(xT_copied[1], tiles)
                pool.dma_start(x_spill[:, :, c0:c1], xT[:, :, c0:c1]).then_inc(x_spilled, 16)
            pool.dma_start(sink_heads[:, :], ins["attn_sinks"].broadcast_to([P, N_HEADS])).then_inc(sinks_in, 16)
            for kv in range(N_KV):
                for par in range(2):
                    h = 4 * kv + par
                    for j in range(2):
                        r = 32 * (2 * par + kv) + 16 * j
                        pool.dma_start(ssink[r:r + 16, 0:1],
                                       ins["attn_sinks"][0:1, h + 2 * j:h + 2 * j + 1].broadcast_to([16, 1]))\
                            .then_inc(sinks_in, 16)
            pool.dma_start(const[:, C_MASK:C_COLS], ins["const"][:, C_MASK:C_COLS]).then_inc(masks_in, 16)
            pool.dma_start(cache_rows[:, :, :], ins["cache_k_win"][0].rearrange("b s k d -> s b (k d)"))\
                .then_inc(kcache_in, 16)
            pool.dma_start(conv_rows[0:2 * NB_S, :], ins["state_conv"][0].rearrange("b r d -> (b r) d"))\
                .then_inc(conv_state_in, 16)
            store(outs["k_sample"][0, :, 0:W - T_S], ins["cache_k_win"][0, :, T_S:W])
            store(outs["v_sample"][0, :, 0:W - T_S], ins["cache_v_win"][0, :, T_S:W])
            store(outs["pool_sample"][0, :, 0:PM - T_S, :], ins["state_pool"][0, :, T_S:PM, :])
            pool.wait_ge(out_freed, 7)
            pool.wait_ge(norm_summed, 6)
            pool.wait_ge(act_ready, 12)
            pool.wait_ge(x_spilled, 48)
            pool.dma_start(kT[:, 0:NT], k_flat[:, :]).then_inc(k_moved, 16)
            for i in range(2):
                pool.dma_start(kT_swapped[DH * i:DH * (i + 1), 0:NT], k_flat[DH * (1 - i):DH * (2 - i), :])\
                    .then_inc(k_swapped, 16)
            pool.wait_ge(setup_copied, 2)
            for i in range(2):
                pool.dma_start(kT_swapped[DH * i:DH * (i + 1), NT:n_keys], kT[DH * (1 - i):DH * (2 - i), NT:n_keys])\
                    .then_inc(k_swapped, 16)
            pool.wait_ge(k_moved, 16)
            pool.wait_ge(k_swapped, 64)
            pool.dma_start(v_cache[:, :, :], ins["cache_v_win"][0].rearrange("b s k d -> s b (k d)"))\
                .then_inc(vcache_in, 16)
            pool.wait_ge(setup_copied, SETUPS)
            store(outs["v_prompt"][0, 0].rearrange("s k d -> s (k d)"), v_blocks[:, 7, :])
            store(outs["k_prompt"][0, 0].rearrange("s k d -> s (k d)"), k_tail[:, 0, :])
            for b in range(NB_S):
                store(outs["k_sample"][0, b, W - T_S:W].rearrange("t k d -> t (k d)"),
                      k_tail[T_S * b:T_S * (b + 1), 1, :])
                a, bb = divmod(b, 4)
                store(outs["v_sample"][0, b, W - T_S:W].rearrange("t k d -> t (k d)"),
                      v_blocks[T_S * bb:T_S * (bb + 1), 9 + a, :])
            for p, (c0, c1) in enumerate(PIECES):
                if p == 0:
                    pool.wait_ge(x_spilled, 48)
                    pool.wait_ge(stored_pool, 16 * n_stored[0])
                for oc in range(KC):
                    if p:
                        pool.wait_ge(out_freed, M_OUT + 8 * (p - 1) + oc + 1)
                    elif oc == 1:
                        pool.wait_ge(out_freed, 52)
                    pool.dma_start(x_again[:, oc, 0:c1 - c0], x_spill[:, oc, c0:c1]).then_inc(x_again_in[oc], 16)
            pool.wait_ge(tail_copied, 1)
            store(outs["conv_prompt"][0, 0], conv_tail_rows[0:2, :])
            store(outs["conv_sample"][0].rearrange("b r d -> (b r) d"), conv_tail_rows[2:18, :])
            pool.wait_ge(out_freed, M_MLP0)
            pool.wait_ge(stored_pool, 16 * n_stored[0])
            pool.dma_start(pool_rows[0:NB_S * PM, :], ins["state_pool"][0].rearrange("b r d -> (b r) d"))\
                .then_inc(pool_state_in, 16)
            pool.wait_ge(pool_copied, 2)
            store(outs["pool_prompt"][0, 0], tail_rows[0:PM, :])
            for b in range(NB_S):
                store(outs["pool_sample"][0, b, PM - T_S:PM, :], tail_rows[PM + T_S * b:PM + T_S * (b + 1), :])
            pool.wait_ge(stored_pool, 16 * n_stored[0])

        @block.tensor
        def _(pe):
            def product(out, lhs, rhs, first, last):
                nc.tensor.matmul(out, lhs[0], rhs[0], start=first, stop=False)
                nc.tensor.matmul(out, lhs[0], rhs[1], start=False, stop=False)
                return nc.tensor.matmul(out, lhs[1], rhs[0], start=False, stop=last)

            def stationary(slot, at):
                return w_hi[:, slot, at:at + P], w_lo[:, slot, at:at + P]

            def acts(k, piece):
                c0, c1 = piece
                return act_hi[:, k, c0:c1], act_lo[:, k, c0:c1]

            def take_bank(m, g=0, per_group=0):
                if m >= 4:
                    pe.wait_ge(out_freed, g * per_group + (m - 3))
                return out_bank[m % 4]

            def wait_step(w, g=0, per_group=0):
                pe.wait_ge(w_lo_done, g * per_group + (w + 1))

            def unit_output(m, w, piece, g=0, normed_k=None, midway=None):
                out = take_bank(m, g, GROUP_OUTS)[:, 0:piece[1] - piece[0]]
                for k in range(KC):
                    if normed_k is not None and k % 2 == 0:
                        pe.wait_ge(act_ready, 4 * normed_k + k // 2 + 1)
                    if midway and k == KC // 2:
                        midway()
                    ins_ = product(out, stationary(w % 4, P * k), acts(k, piece), k == 0, k == KC - 1)
                ins_.then_inc(out_ready, 1)

            def down_output(m, w0, oc, n, rhs, g=0):
                out = take_bank(m, g, GROUP_OUTS)[:, 0:n]
                for k in range(4):
                    ins_ = product(out, stationary((w0 + oc // 2) % 4, 256 * k + P * (oc % 2)), rhs(k), k == 0, k == 3)
                ins_.then_inc(out_ready, 1)

            def norm_stats(n, p):
                k = 3 * n + p
                c0, c1 = norm_pieces(n)[p]
                pe.wait_ge(norm_summed, 2 * k + 2)
                if k:
                    pe.wait_ge(norm_root, k)
                for half_ in range(2):
                    ins_ = nc.tensor.matmul(turned2[:, 0:c1 - c0], const[:, C_MEAN:C_MEAN + P],
                                            norm_tensors(n)[1][:, half_, 0:c1 - c0], start=half_ == 0, stop=half_ == 1)
                ins_.then_inc(norm_mean, 1)

            def head_stats(i):
                pe.wait_ge(head_sq_done, i + 1)
                if i:
                    pe.wait_ge(head_root, i)
                p = HEAD_NORMS[i][1]
                n = PIECES[p][1] - PIECES[p][0]
                nc.tensor.matmul(turned[:, 0:n], const[:, C_HEAD:C_HEAD + P], head_sq[:, i % 2, 0:n],
                                 start=True, stop=True).then_inc(head_mean, 1)

            pe.wait_ge(ident_in, 16)

            def turn_x(t):
                nr = P if t < 8 else N_META + NS
                pe.wait_ge(x_in[t], 32 if t in (0, 8) else 16)
                for half_ in range(2):
                    if t:
                        pe.wait_ge(xT_copied[half_], t)
                    for c in range(4):
                        cc = 4 * half_ + c
                        ins_ = nc.tensor.transpose(scores[:, half_, P * c:P * c + nr], x_rows[0:nr, t, P * cc:P * (cc + 1)],
                                                   ident[0:nr, 0:nr])
                    ins_.then_inc(x_turned[half_], 1)

            for t in range(3):
                turn_x(t)
            pe.wait_ge(params_in, 16 * 8)
            nc.tensor.transpose(turned[:, 0:R_ALL], param_rows[0:R_ALL, :], ident[0:R_ALL, 0:R_ALL])\
                .then_inc(prm_turned, 1)
            pe.wait_ge(mean_in, 16)

            HEAD_NORMS = [(m, (m % 9) // 3) for m in range(18) if m < 9 and m % 3 != 1 or m >= 9]

            def setup_round(r, turns):
                if r == 0:
                    pe.wait_ge(xT_copied[0], 9)
                    pe.wait_ge(xT_copied[1], 9)
                if r >= 2:
                    pe.wait_ge(setup_copied, r - 1)
                for at_, in_ in turns:
                    k, m_ = in_.partition_size(), in_.free_size()
                    ins_ = nc.tensor.transpose(scores[0:m_, r % 2, at_:at_ + k], in_, ident[0:k, 0:k])
                ins_.then_inc(setup_turned, 1)

            done_heads = 0
            for m in range(18):
                grp, p, i = m // 9, (m % 9) // 3, m % 3
                w = 3 * grp + i
                if p == 0:
                    wait_step(w)
                unit_output(m, w, PIECES[p], normed_k=p if m < 9 and i == 0 else None)
                if m in (3, 6):
                    norm_stats(0, p)
                while done_heads < len(HEAD_NORMS) and HEAD_NORMS[done_heads][0] < m:
                    head_stats(done_heads)
                    done_heads += 1
                if m < 3:
                    turn_x(2 * m + 3)
                    turn_x(2 * m + 4)
                if m == 0:
                    norm_stats(0, 0)
                if m == 8:
                    pe.wait_ge(kcache_in, 16)
                    for r in range(2):
                        setup_round(r, [(P * b, cache_rows[:, 4 * r + b, :]) for b in range(4)])
                if m == 11:
                    pe.wait_ge(out_freed, 8)
                    for r in range(2):
                        setup_round(2 + r, [(P * b, v_flat[:, N_META + W * (4 * r + b):N_META + W * (4 * r + b + 1)])
                                            for b in range(4)])
                if m == 12:
                    pe.wait_ge(setup_copied, 3)
                    for at_, c in ((0, 0), (P, NPR), (2 * P, NPR + 16)):
                        ins_ = nc.tensor.transpose(scores[0:16, 0, at_:at_ + P], v_flat[:, c:c + 16], ident)
                    ins_.then_inc(setup_turned, 1)
                if m == 14:
                    pe.wait_ge(conv_state_in, 16)
                    pe.wait_ge(setup_copied, 4)
                    for c in range(4):
                        ins_ = nc.tensor.transpose(scores[:, 1, 16 * c:16 * (c + 1)], conv_rows[0:16, P * c:P * (c + 1)],
                                                   ident[0:16, 0:16])
                    ins_.then_inc(setup_turned, 1)
                if m == 16:
                    pe.wait_ge(setup_copied, 5)
                    pe.wait_ge(k_moved, 16)
                    nc.tensor.transpose(scores[:, 0, 0:P], kT[:, NPR - W:NPR], ident)
                    nc.tensor.transpose(scores[0:NS, 0, P:2 * P], kT[:, NPR:NT], ident).then_inc(setup_turned, 1)

            def keys(kv, par, c0, c1):
                return (kT if kv == par else kT_swapped)[DH * par:DH * (par + 1), c0:c1]

            def attn_scores(h):
                if h == 0:
                    pe.wait_ge(out_freed, 18)
                    pe.wait_ge(k_moved, 16)
                    pe.wait_ge(k_swapped, 64)
                    pe.wait_ge(setup_copied, SETUPS)
                else:
                    pe.wait_ge(scores_read, h)
                if h < N_HALF:
                    kv, q0, nq, key0, k0, k1 = half(h)
                    for par in range(2):
                        for j in range(2):
                            ins_ = nc.tensor.matmul(scores[0:nq, par, 256 * j:256 * j + k0 + k1],
                                                    qT[DH * par:DH * (par + 1), 2 * kv + j, q0:q0 + nq],
                                                    keys(kv, par, key0, key0 + k0 + k1), start=True, stop=True)
                    ins_.then_inc(qk_ready, 1)
                    return
                a = h - N_HALF
                if a == 0:
                    pe.wait_ge(q_packed, 1)
                new = NPR + 16 * a
                for par in range(2):
                    for kv in range(N_KV):
                        r = 32 * (2 * par + kv)
                        q = q_samples[DH * par:DH * (par + 1), a, 2 * kv:2 * kv + 2, :].rearrange("p c n -> p (c n)")
                        nc.tensor.matmul(scores[r:r + 32, 0, :], q, keys(kv, par, NT + 4 * W * a, NT + 4 * W * (a + 1)),
                                         start=True, stop=True)
                        ins_ = nc.tensor.matmul(scores[r:r + 32, 1, 0:16], q, keys(kv, par, new, new + 16),
                                                start=True, stop=True)
                    ins_.then_inc(qk_ready, 1)
                    if par == 0:
                        pe.wait_ge(qk_ready, qk_count(h - 1) + 1)

            def turn_probs(h):
                pe.wait_ge(probs_ready, h + 1)
                if h == 0:
                    pe.wait_ge(head_root, len(HEAD_NORMS))
                    pe.wait_ge(norm_root, 3)
                else:
                    pe.wait_ge(attn_copied, h)
                    pe.wait_ge(probsT_act, h)
                if h < N_HALF:
                    kv, q0, nq, key0, k0, k1 = half(h)
                    for bank, at_, n in ((turned, 0, k0), (turned2, k0, k1)):
                        for e in range(4 if n else 0):
                            ins_ = nc.tensor.transpose(bank[0:n, e * nq:(e + 1) * nq],
                                                       scores_sb[0:nq, h % 2, 256 * e + at_:256 * e + at_ + n],
                                                       ident[0:nq, 0:nq])
                else:
                    for b in range(4):
                        nc.tensor.transpose(turned[:, P * b:P * (b + 1)], scores_sb[:, h % 2, P * b:P * (b + 1)], ident)
                    ins_ = nc.tensor.transpose(turned2[0:16, 0:P], scores_sb[:, h % 2, 4 * P:4 * P + 16], ident)
                ins_.then_inc(probs_turned, 1)

            def attn_values(h):
                if h >= 2:
                    pe.wait_ge(probsT_dve, h - 1)
                pe.wait_ge(probsT_act, h + 1)
                if h < N_HALF:
                    kv, q0, nq, key0, k0, k1 = half(h)
                    n = h // 2
                    for par in range(2):
                        parts = ([(v_block(n - 1), k0, 0)] if k0 else []) + [(v_block(n), k1, 512)]
                        for i, (vb, kn, at_) in enumerate(parts):
                            ins_ = nc.tensor.matmul(turned[DH * par:DH * (par + 1), 0:2 * nq],
                                                    vb[0:kn, DH * kv:DH * (kv + 1)],
                                                    probsT[0:kn, at_ + 2 * par * nq:at_ + 2 * (par + 1) * nq],
                                                    start=i == 0, stop=i == len(parts) - 1)
                else:
                    a = h - N_HALF
                    if a == 0:
                        pe.wait_ge(vcache_in, 16)
                    for par in range(2):
                        for kv in range(N_KV):
                            r = 32 * (2 * par + kv)
                            out = turned[DH * par:DH * (par + 1), 32 * kv:32 * (kv + 1)]
                            for b in range(4):
                                nc.tensor.matmul(out, v_cache[:, 4 * a + b, DH * kv:DH * (kv + 1)],
                                                 probsT[:, P * b + r:P * b + r + 32], start=b == 0, stop=False)
                            ins_ = nc.tensor.matmul(out, v_blocks[0:16, 9 + a, DH * kv:DH * (kv + 1)],
                                                    probsT[0:16, 512 + r:512 + r + 32], start=False, stop=True)
                ins_.then_inc(pv_ready, 1)

            for s in range(SLOTS):
                for h in range(HALVES):
                    if START[h] == s:
                        attn_scores(h)
                m = 18 + s
                w = 6 + 3 * (s // 9) + s % 3
                if (s % 9) // 3 == 0:
                    wait_step(w)

                def values():
                    for h in range(HALVES):
                        if START[h] + PV_LAG == s:
                            attn_values(h)

                unit_output(m, w, PIECES[(s % 9) // 3], midway=values)
                if s == 0:
                    for i in range(done_heads, len(HEAD_NORMS)):
                        head_stats(i)
                for h in range(HALVES):
                    if START[h] + T_LAG == s:
                        turn_probs(h)
            for h in range(HALVES):
                if START[h] + PV_LAG >= SLOTS:
                    attn_values(h)

            def w_out_half(half_, hook):
                for p, piece in enumerate(PIECES):
                    pe.wait_ge(mix_ready, 3 * half_ + p + 1)
                    for oc in range(KC):
                        m = M_OUT + 24 * half_ + 8 * p + oc
                        if p == 0 and oc % 2 == 0:
                            wait_step(W_OUT + 4 * half_ + oc // 2)
                        down_output(m, W_OUT + 4 * half_, oc, piece[1] - piece[0],
                                    lambda k: acts(4 * half_ + k, piece))
                        hook(p, oc)

            def conv_tail_turn(p, oc):
                if (p, oc) == (0, 7):
                    pe.wait_ge(tail_gathered, 4)
                    for c in range(4):
                        ins_ = nc.tensor.transpose(scores[0:18, 0, P * c:P * (c + 1)], conv_tail[:, c, :], ident)
                    ins_.then_inc(tail_turned, 1)

            w_out_half(0, conv_tail_turn)

            def stats_hook(n):
                def hook(p, oc):
                    if p and oc == 3:
                        norm_stats(n, p - 1)
                    if n == 2 and (p, oc) == (1, 5):
                        for i in range(2):
                            map_pool_state(i)
                return hook

            w_out_half(1, stats_hook(1))

            def turn_pool_state():
                pe.wait_ge(pool_state_in, 16)
                pe.wait_ge(tail_copied, 1)
                for half_ in range(2):
                    for c in range(4):
                        cc = 4 * half_ + c
                        ins_ = nc.tensor.transpose(scores[:, half_, 120 * c:120 * (c + 1)],
                                                   pool_rows[0:120, P * cc:P * (cc + 1)], ident[0:120, 0:120])
                    ins_.then_inc(pool_state_turned, 1)

            def map_pool_state(i):
                pe.wait_ge(raw_in[i], 16 * ((W_POOL + i) // 2 + 1))
                pe.wait_ge(pool_state_copied, 2)
                for o in range(4):
                    gi, c = divmod(o, 2)
                    for k in range(2):
                        ins_ = nc.tensor.matmul(scores[:, i, 120 * o:120 * (o + 1)],
                                                raw[:, i, 512 * gi + 256 * k + P * c:512 * gi + 256 * k + P * c + P],
                                                pool_state[:, 4 * i + 2 * gi + k, :], start=k == 0, stop=k == 1)
                ins_.then_inc(state_mapped, 1)

            def up(layer, mb, wb, g, after=None, normed=None):
                pieces = (PIECES, PIECES1)[layer]
                for u in range(2):
                    for p, piece in enumerate(pieces):
                        for i in range(2):
                            if p == 0:
                                wait_step(wb + 2 * u + i, g, 8)
                            unit_output(mb + 6 * u + 2 * p + i, wb + 2 * u + i, piece, g,
                                        3 * normed + p if normed is not None and u == 0 and i == 0 else None)
                        if after:
                            after(u, p)

            def up_by_piece(mb, wb):
                for p, piece in enumerate(PIECES1):
                    for s in range(4):
                        if p == 0:
                            wait_step(wb + s)
                        unit_output(mb + 4 * p + s, wb + s, piece, 0, 9 + p if s == 0 else None)
                        if s == 0:
                            norm_stats(3, p)

            def down(layer, mb, wb, hb, g, hook=None, by_piece=False):
                pieces = (PIECES, PIECES1)[layer]
                for p, (c0, c1) in enumerate(pieces):
                    pe.wait_ge(hid_ready, g * UP_OUTS + (hb + (4 * p + 4 if by_piece else 6 + 2 * p + 2)))
                    for oc in range(KC):
                        if p == 0 and oc % 2 == 0:
                            wait_step(wb + 4 + oc // 2, g, 8)
                        down_output(mb + UP_OUTS + 8 * p + oc, wb + 4, oc, c1 - c0,
                                    lambda k: (hid_hi[p][:, k, 0:c1 - c0], hid_lo[p][:, k, 0:c1 - c0]), g)
                        if hook:
                            hook(p, oc)

            def at_group(mb, wb, hb, g):
                return mb + GROUP_OUTS * g, wb + 8 * g, hb + UP_OUTS * g

            def mlp(layer, mb, wb, hb, after, normed, hook):
                m0, w0, h0 = mb, wb, hb
                if layer == 0:
                    up(layer, m0, w0, 0, after, normed)
                else:
                    up_by_piece(m0, w0)
                down(layer, m0, w0, h0, 0, None, layer == 1)
                with pe.Fori(1, GROUPS - 1) as g:
                    up(layer, mb, wb, g)
                    down(layer, mb, wb, hb, g)
                m0, w0, h0 = at_group(mb, wb, hb, GROUPS - 1)
                up(layer, m0, w0, 0)
                down(layer, m0, w0, h0, 0, hook)

            def mlp0_hook(u, p):
                if (u, p) == (0, 0):
                    norm_stats(1, 2)
                if (u, p) == (1, 0):
                    turn_pool_state()

            mlp(0, M_MLP0, W_MLP0, 0, mlp0_hook, 1, stats_hook(2))

            def pool_outputs(p):
                c0, c1 = PIECES[p]
                for oc in range(KC):
                    gi = oc // 2
                    m = M_POOL + 8 * p + oc
                    if p == 0 and oc % 4 == 0:
                        wait_step(W_POOL + oc // 4)
                    pe.wait_ge(act_ready, 4 * (6 + p) + gi + 1)
                    out = take_bank(m)[:, 0:c1 - c0]
                    for k in range(2):
                        ins_ = product(out, stationary((W_POOL + gi // 2) % 4, 512 * (gi % 2) + 256 * k + P * (oc % 2)),
                                       acts(2 * gi + k, (c0, c1)), k == 0, k == 1)
                    ins_.then_inc(out_ready, 1)

            pool_outputs(0)
            pool_outputs(1)
            norm_stats(2, 2)
            pool_outputs(2)
            pe.wait_ge(pool_gathered, 1)
            pe.wait_ge(states_placed, 2)
            for half_ in range(2):
                for c in range(4):
                    ins_ = nc.tensor.transpose(scores[0:47, half_, P * c:P * (c + 1)], pool_tail[:, 4 * half_ + c, :], ident)
                ins_.then_inc(pool_turned, 1)

            def turn_y(t):
                c0 = N_META + P * t
                n = P if t < 8 else NS
                for half_ in range(2):
                    i = 2 * t + half_
                    if i >= 4:
                        pe.wait_ge((fin_dve, fin_act)[half_], t - 1)
                    if half_ == 0:
                        last_piece = 0 if c0 + n <= 368 else 1 if c0 + n <= 720 else 2
                        pe.wait_ge(out_freed, M_MLP1 + GROUP_OUTS * (GROUPS - 1) + UP_OUTS + 8 * (last_piece + 1))
                    for c in range(4):
                        cc = 4 * half_ + c
                        ins_ = nc.tensor.transpose(fin_bank[i % 4][0:n, P * c:P * (c + 1)], xT[:, cc, c0:c0 + n], ident)
                    ins_.then_inc(fin_turned, 1)

            def y_hook(p, oc):
                if oc == 3 and p == 1:
                    pe.wait_ge(norm_root, 12)
                    pe.wait_ge(pool_copied, 2)
                    turn_y(0)
                    turn_y(1)
                if p == 2 and oc in (1, 3, 5):
                    turn_y(2 + oc // 2)

            mlp(1, M_MLP1, W_MLP1, 96, None, None, y_hook)
            for t in range(5, 9):
                turn_y(t)

        @block.scalar
        def _(act):
            def split_hi(w, g=0, per_group=0, last=None):
                act.wait_ge(raw_in[w % 2], g * (8 * per_group) + 16 * (w // 2 + 1))
                if w >= 4:
                    act.wait_ge(out_ready, g * (GROUP_OUTS if per_group else 0)
                                + (last_output(w - 4, in_loop=per_group > 0) + 1))
                nc.scalar.activation(w_hi[:, w % 4, :], raw[:, w % 2, :], ACT.Copy).then_inc(w_hi_done, 1)

            def wait_residual(n, p, c):
                if n == 0:
                    act.wait_ge(xT_copied[c // 4], 3 * p + 3)
                elif n == 3:
                    act.wait_ge(x_pooled, 4 * p + c // 2 + 1)
                else:
                    act.wait_ge(out_freed, {1: M_OUT + 24, 2: M_POOL - 24}[n] + 8 * p + c + 1)

            def norm_square(n, p, half_):
                i = 2 * (3 * n + p) + half_
                c0, c1 = norm_pieces(n)[p]
                wait_residual(n, p, 4 * half_ + 3)
                if i:
                    act.wait_ge(norm_summed, i)
                nc.scalar.activation(norm_tensors(n)[0][:, :, 0:c1 - c0], xT[:, 4 * half_:4 * half_ + 4, c0:c1],
                                     ACT.Square).then_inc(norm_sq, 1)

            def norm_sqrt(n, p):
                k = 3 * n + p
                c0, c1 = norm_pieces(n)[p]
                act.wait_ge(norm_mean, k + 1)
                nc.scalar.activation(rs[:, c0:c1], turned2[:, 0:c1 - c0], ACT.Sqrt,
                                     bias=prm[:, R_ALL:R_ALL + 1]).then_inc(norm_root, 1)

            def norm_split_hi(n, p, pair):
                c0, c1 = norm_pieces(n)[p]
                wait_residual(n, p, 7 if n == 1 and pair >= 2 else 2 * pair + 1)
                for c in (2 * pair, 2 * pair + 1):
                    ins_ = nc.scalar.activation(act_hi[:, c, c0:c1], xT[:, c, c0:c1], ACT.Copy, scale=gain(n, c))
                ins_.then_inc(norm_hi, 1)

            def norm_splits(n, p):
                for pair in range(4):
                    norm_split_hi(n, p, pair)
                for half_ in range(2):
                    norm_square(n, p, half_)

            act.dma_start(const[:, 0:C_MEAN], ins["const"][:, 0:C_MEAN]).then_inc(ident_in, 16)
            rows = [(R_NMIX, ins["norm_mix"].rearrange("l (c p) -> (l c) p", p=P)),
                    (R_NMLP, ins["norm_mlp"].rearrange("l (c p) -> (l c) p", p=P)),
                    (R_CONV, ins["conv_w"][0].rearrange("j (c p) -> (j c) p", p=P)),
                    (R_SCALE, ins["pool_scale"].rearrange("l (c p) -> (l c) p", p=P))]
            for r, src in rows:
                act.dma_start(param_rows[r:r + src.shape[0], :], src).then_inc(params_in, 16)
            for r, name in ((R_Q, "q_norm"), (R_K, "k_norm")):
                for i in range(2):
                    act.dma_start(param_rows[r:r + 1, DH * i:DH * (i + 1)], ins[name]).then_inc(params_in, 16)
            act.dma_start(const[:, C_MEAN:C_MASK], ins["const"][:, C_MEAN:C_MASK]).then_inc(mean_in, 16)

            def copy_x(t):
                nr = P if t < 8 else N_META + NS
                act.wait_ge(x_turned[1], t + 1)
                nc.scalar.activation(xT[:, 4:8, P * t:P * t + nr],
                                     scores[:, 1, :].rearrange("p (c n) -> p c n", c=4)[:, :, 0:nr], ACT.Copy)\
                    .then_inc(xT_copied[1], 1)

            for t in range(3):
                copy_x(t)
            act.wait_ge(prm_turned, 1)
            nc.scalar.activation(prm[:, 0:R_ALL], turned[:, 0:R_ALL], ACT.Copy).then_inc(prm_ready, 1)
            split_hi(0)
            act.wait_ge(prm_ready, 1)
            for pair in range(4):
                norm_split_hi(0, 0, pair)
            norm_square(0, 0, 0)
            split_hi(1)
            norm_square(0, 0, 1)
            copy_x(3)
            copy_x(4)
            act.wait_ge(eps_ready, 1)
            norm_sqrt(0, 0)

            def setup_copy(r, dst, src):
                act.wait_ge(setup_turned, r + 1)
                nc.scalar.activation(dst, src, ACT.Copy).then_inc(setup_copied, 1)

            head_outputs = [m for m in range(18) if m >= 9 or m % 3 != 1]

            def head_sqrt(i):
                m = head_outputs[i]
                n = PIECES[(m % 9) // 3][1] - PIECES[(m % 9) // 3][0]
                act.wait_ge(head_mean, i + 1)
                nc.scalar.activation(head_sq[:, i % 2, 0:n], turned[:, 0:n], ACT.Sqrt, bias=prm[:, R_ALL:R_ALL + 1])\
                    .then_inc(head_root, 1)

            i = 0
            for m in range(18):
                grp, p, part = m // 9, (m % 9) // 3, m % 3
                if m in (3, 6):
                    norm_sqrt(0, p)
                if m in head_outputs:
                    n = PIECES[p][1] - PIECES[p][0]
                    act.wait_ge(head_scaled, i + 1)
                    if i >= 2:
                        act.wait_ge(out_freed, head_outputs[i - 2] + 1)
                    nc.scalar.activation(head_sq[:, i % 2, 0:n], out_bank[m % 4][:, 0:n], ACT.Square)\
                        .then_inc(head_sq_done, 1)
                    i += 1
                if m - 1 in head_outputs:
                    head_sqrt(head_outputs.index(m - 1))
                if m < 2:
                    copy_x(2 * m + 5)
                    copy_x(2 * m + 6)
                if m == 0:
                    split_hi(2)
                if m in (1, 4):
                    norm_splits(0, p + 1)
                if m == 3:
                    split_hi(3)
                if p == 2:
                    split_hi(3 * grp + part + 4)
                if m == 8:
                    act.wait_ge(x_spilled, 48)
                    act.wait_ge(norm_summed, 6)
                    act.wait_ge(act_ready, 12)
                    for r in range(2):
                        setup_copy(r, kT[:, NT + 4 * W * r:NT + 4 * W * (r + 1)], scores[:, r, :])
                if m == 11:
                    act.wait_ge(act_ready, 12)
                    for r in range(2):
                        setup_copy(2 + r, v_blocks[:, 4 * r:4 * (r + 1), :],
                                   scores[:, r, :].rearrange("p (b n) -> p b n", b=4))
                if m == 12:
                    setup_copy(4, v_blocks[0:16, 8:11, :], scores[0:16, 0, 0:3 * P].rearrange("p (b n) -> p b n", b=3))
                if m == 14:
                    setup_copy(5, conv_state[:, :, :], scores[:, 1, 0:64].rearrange("p (c n) -> p c n", c=4))
                if m == 16:
                    act.wait_ge(setup_turned, SETUPS)
                    nc.scalar.activation(k_tail[0:NS, 1, :], scores[0:NS, 0, P:2 * P], ACT.Copy).then_inc(act_step, 1)
                    act.wait_ge(act_step, 1)
                    nc.scalar.activation(k_tail[:, 0, :], scores[:, 0, 0:P], ACT.Copy).then_inc(setup_copied, 1)

            head_sqrt(len(head_outputs) - 1)

            def exps(h):
                act.wait_ge(soft_in, h + 1)
                s = soft[:, h % 2]
                if h < N_HALF:
                    kv, q0, nq, key0, k0, k1 = half(h)
                    for e in range(4):
                        pr = scores_sb[0:nq, h % 2, 256 * e:256 * e + k0 + k1]
                        nc.scalar.activation(pr, pr, ACT.Exp, bias=s[0:nq, NM, e:e + 1],
                                             accum_out=s[0:nq, RS, e:e + 1])
                    nc.scalar.activation(s[0:nq, ES, :], s[0:nq, DS, :], ACT.Exp).then_inc(exp_done, 1)
                else:
                    pr = scores_sb[:, h % 2, 0:SK]
                    nc.scalar.activation(pr, pr, ACT.Exp, bias=s[:, NM, 0:1], accum_out=s[:, RS, 0:1])
                    nc.scalar.activation(s[:, ES, 0:1], s[:, DS, 0:1], ACT.Exp).then_inc(exp_done, 1)

            def copy_own_probs(h):
                act.wait_ge(probs_turned, h + 1)
                if h < N_HALF:
                    kv, q0, nq, key0, k0, k1 = half(h)
                    nc.scalar.activation(probsT[0:k1, 512:512 + 4 * nq], turned2[0:k1, 0:4 * nq], ACT.Copy)\
                        .then_inc(probsT_act, 1)
                else:
                    nc.scalar.activation(probsT[0:16, 512:512 + P], turned2[0:16, 0:P], ACT.Copy).then_inc(probsT_act, 1)

            for s in range(SLOTS):
                for h in range(HALVES):
                    if START[h] == s:
                        exps(h)
                if (s % 9) // 3 == 2:
                    split_hi(6 + 3 * (s // 9) + s % 3 + 4)
                for h in range(HALVES):
                    if START[h] + T_LAG == s:
                        copy_own_probs(h)

            act.wait_ge(out_ready, M_OUT)
            for p, (c0, c1) in enumerate(PIECES):
                act.wait_ge(out_freed, 45 + 3 * p + 3)
                nc.scalar.activation(act_hi[:, 0:4, c0:c1], conv_out[:, :, c0:c1], ACT.Copy).then_inc(mix_hi, 1)
            act.wait_ge(attn_copied, HALVES)
            for c0, c1 in PIECES:
                nc.scalar.activation(act_hi[:, 4:8, c0:c1], qT[:, :, c0:c1], ACT.Copy).then_inc(mix_hi, 1)
            def splits_half0():
                for s in range(4):
                    split_hi(W_OUT + 4 + s)

            splits_half0()
            act.wait_ge(tail_turned, 1)
            act.wait_ge(out_freed, M_OUT + 24)
            nc.scalar.activation(conv_tail_rows[0:18, :], scores[0:18, 0, :], ACT.Copy).then_inc(tail_copied, 1)

            def normed_pass_hi(n, p, w0):
                for what in ("w0", "n0", "w1", "n1", "s0", "r", "w2", "w3", "n2", "n3", "s1"):
                    if what[0] == "w":
                        if w0 is not None:
                            split_hi(w0 + int(what[1]))
                    elif what == "r":
                        if p:
                            norm_sqrt(n, p - 1)
                    elif what[0] == "s":
                        norm_square(n, p, int(what[1]))
                    else:
                        norm_split_hi(n, p, int(what[1]))

            normed_pass_hi(1, 0, None)
            normed_pass_hi(1, 1, None)
            normed_pass_hi(1, 2, W_OUT + 8)

            def hidden(layer, mb, hb, g, q, p, chunk):
                m = mb + q
                c0, c1 = (PIECES, PIECES1)[layer][p]
                n = c1 - c0
                act.wait_ge(out_freed, g * GROUP_OUTS + (m + 1))
                if hb + q >= 2:
                    act.wait_ge(hid_ready, g * UP_OUTS + (hb + q - 1))
                nc.scalar.activation(sq[:, q % 2, 0:n], relu[:, q % 2, 0:n], ACT.Square).then_inc(hid_sq_done, 1)
                act.wait_ge(hid_sq_done, g * UP_OUTS + (hb + q + 1))
                nc.scalar.activation(hid_hi[p][:, chunk, 0:n], sq[:, q % 2, 0:n], ACT.Copy)\
                    .then_inc(hid_hi_done, 1)

            def up(layer, mb, wb, hb, g, after=None):
                for u in range(2):
                    for p in range(3):
                        for i in range(2):
                            hidden(layer, mb, hb, g, 6 * u + 2 * p + i, p, 2 * u + i)
                        if after:
                            after(u, p)
                    for i in range(2):
                        split_hi(wb + 4 + 2 * u + i, g, 8)

            def up_by_piece(mb, wb, hb):
                for p in range(3):
                    for s in range(4):
                        if s == 0:
                            if p < 2:
                                norm_split_hi(3, p + 1, s)
                            norm_sqrt(3, p)
                        hidden(1, mb, hb, 0, 4 * p + s, p, s)
                        if p < 2 and s:
                            norm_split_hi(3, p + 1, s)
                            if s % 2:
                                norm_square(3, p + 1, s // 2)
                        if p == 2:
                            split_hi(wb + 4 + s)

            def down_splits(wb, g):
                for s in range(4):
                    split_hi(wb + 8 + s, g, 8)

            def mlp(layer, mb, wb, hb, after):
                if layer == 0:
                    up(layer, mb, wb, hb, 0, after)
                else:
                    up_by_piece(mb, wb, hb)
                down_splits(wb, 0)
                with act.Fori(1, GROUPS - 1) as g:
                    up(layer, mb, wb, hb, g)
                    down_splits(wb, g)
                last = GROUPS - 1
                up(layer, mb + GROUP_OUTS * last, wb + 8 * last, hb + UP_OUTS * last, 0)

            def mlp0_extras(u, p):
                if (u, p) == (0, 0):
                    norm_sqrt(1, 2)
                if (u, p) == (1, 0):
                    for half_ in range(2):
                        act.wait_ge(pool_state_turned, half_ + 1)
                        nc.scalar.activation(pool_state[:, 4 * half_:4 * (half_ + 1), :],
                                             scores[:, half_, 0:480].rearrange("p (c n) -> p c n", c=4), ACT.Copy)\
                            .then_inc(pool_state_copied, 1)

            act.wait_ge(stored_pool, 16 * (N_STORES - 1 - NB_S))
            mlp(0, M_MLP0, W_MLP0, 0, mlp0_extras)

            for p in range(3):
                normed_pass_hi(2, p, W_POOL if p == 2 else None)
            for half_ in range(2):
                act.wait_ge(state_mapped, 2)
                for c in range(4):
                    smp = z_samples[:, 4 * half_ + c, :].rearrange("p (b r) -> p b r", r=19)
                    ins_ = nc.scalar.activation(smp[:, :, 0:PM], scores[:, half_, 120 * c:120 * (c + 1)]
                                                .rearrange("p (b r) -> p b r", r=PM), ACT.Copy)
                ins_.then_inc(states_placed, 1)
            norm_sqrt(2, 2)
            split_hi(W_MLP1 + 2)
            split_hi(W_MLP1 + 3)
            for half_ in range(2):
                act.wait_ge(pool_turned, half_ + 1)
                nc.scalar.activation(tail_rows[0:47, 512 * half_:512 * (half_ + 1)], scores[0:47, half_, :], ACT.Copy)\
                    .then_inc(pool_copied, 1)
            norm_splits(3, 0)

            mlp(1, M_MLP1, W_MLP1, 96, None)

            for t in range(9):
                n = P if t < 8 else NS
                act.wait_ge(fin_turned, 2 * t + 2)
                nc.scalar.activation(y_rows[0:n, t, 512:1024], fin_bank[(2 * t + 1) % 4][0:n, :], ACT.Copy)\
                    .then_inc(fin_act, 1)

        @block.vector
        def _(dve):
            steps = [0]

            def then(ins_):
                ins_.then_inc(dve_step, 1)
                steps[0] += 1
                dve.wait_ge(dve_step, steps[0])

            def f32(t):
                return t.bitcast(F32)

            def split_lo(w, g=0, per_group=0):
                dve.wait_ge(w_hi_done, g * per_group + (w + 1))
                nc.vector.tensor_tensor(w_lo[:, w % 4, :], raw[:, w % 2, :], f32(w_hi[:, w % 4, :]), ALU.subtract)\
                    .then_inc(w_lo_done, 1)

            def norm_reduce(n, p, half_):
                i = 2 * (3 * n + p) + half_
                c0, c1 = norm_pieces(n)[p]
                buf, total = norm_tensors(n)
                dve.wait_ge(norm_sq, i + 1)
                if i >= 2:
                    dve.wait_ge(norm_mean, i // 2)
                nc.vector.tensor_reduce(total[:, half_, 0:c1 - c0], buf[:, :, 0:c1 - c0].rearrange("p c n -> p n c"),
                                        AX_X, ALU.add).then_inc(norm_summed, 1)

            def norm_rsqrt(n, p):
                k = 3 * n + p
                c0, c1 = norm_pieces(n)[p]
                dve.wait_ge(norm_root, k + 1)
                nc.vector.reciprocal(rs[:, c0:c1], rs[:, c0:c1]).then_inc(norm_rs_done, 1)
                dve.wait_ge(norm_rs_done, k + 1)

            def norm_split_lo(n, p, pair):
                c0, c1 = norm_pieces(n)[p]
                dve.wait_ge(norm_hi, 4 * (3 * n + p) + pair + 1)
                for c in (2 * pair, 2 * pair + 1):
                    ins_ = nc.vector.scalar_tensor_tensor(out=act_lo[:, c, c0:c1], in0=xT[:, c, c0:c1],
                                                          scalar=gain(n, c), in1=f32(act_hi[:, c, c0:c1]),
                                                          op0=ALU.mult, op1=ALU.subtract)
                ins_.then_inc(act_ready, 1)

            def norm_splits(n, p):
                for pair in range(4):
                    norm_split_lo(n, p, pair)
                for half_ in range(2):
                    norm_reduce(n, p, half_)

            nc.vector.memset(prm[:, R_ALL:R_ALL + 1], EPS).then_inc(eps_ready, 1)

            def copy_x(t):
                nr = P if t < 8 else N_META + NS
                dve.wait_ge(x_turned[0], t + 1)
                nc.vector.tensor_copy(xT[:, 0:4, P * t:P * t + nr],
                                      scores[:, 0, :].rearrange("p (c n) -> p c n", c=4)[:, :, 0:nr])\
                    .then_inc(xT_copied[0], 1)

            for t in range(3):
                copy_x(t)
            dve.wait_ge(prm_ready, 1)
            split_lo(0)
            for pair in range(4):
                norm_split_lo(0, 0, pair)
            norm_reduce(0, 0, 0)
            split_lo(1)
            norm_reduce(0, 0, 1)
            copy_x(3)
            copy_x(4)
            norm_rsqrt(0, 0)

            heads = [m for m in range(18) if m >= 9 or m % 3 != 1]

            def head_finish(m):
                i = heads.index(m)
                grp, p, part = m // 9, (m % 9) // 3, m % 3
                c0, c1 = PIECES[p]
                head_rs = head_sq[:, i % 2, 0:c1 - c0]
                dve.wait_ge(head_root, i + 1)
                nc.vector.reciprocal(head_rs, head_rs).then_inc(head_rs_done, 1)
                dve.wait_ge(head_rs_done, i + 1)
                if (grp, part) == (0, 0):
                    dst, row = k_flat[:, c0:c1], R_K
                else:
                    dst, row = qT[:, 0 if grp == 0 else part + 1, c0:c1], R_Q
                nc.vector.scalar_tensor_tensor(out=dst, in0=out_bank[m % 4][:, 0:c1 - c0], scalar=prm[:, row:row + 1],
                                               in1=head_rs, op0=ALU.mult, op1=ALU.mult).then_inc(out_freed, 1)

            for m in range(18):
                grp, p, part = m // 9, (m % 9) // 3, m % 3
                c0, c1 = PIECES[p]
                n = c1 - c0
                acc = out_bank[m % 4][:, 0:n]
                if m in (3, 6):
                    norm_rsqrt(0, p)
                if m in heads:
                    dve.wait_ge(out_ready, m + 1)
                    nc.vector.tensor_tensor(acc, acc, rs[:, c0:c1], ALU.mult).then_inc(head_scaled, 1)
                    dve.wait_ge(head_scaled, heads.index(m) + 1)
                if m - 1 in heads:
                    head_finish(m - 1)
                if m not in heads:
                    dve.wait_ge(out_ready, m + 1)
                    nc.vector.tensor_tensor(v_flat[:, c0:c1], acc, rs[:, c0:c1], ALU.mult).then_inc(out_freed, 1)
                if m < 2:
                    copy_x(2 * m + 5)
                    copy_x(2 * m + 6)
                if m == 0:
                    split_lo(2)
                if m in (1, 4):
                    norm_splits(0, p + 1)
                if m == 3:
                    split_lo(3)
                if p == 2:
                    split_lo(3 * grp + part + 4)
                if m == 12:
                    then(nc.vector.tensor_tensor(rs_squared[:, :], rs[:, :], rs[:, :], ALU.mult))
            head_finish(17)

            dve.wait_ge(sinks_in, 16 * 9)
            dve.wait_ge(out_freed, 18)
            nc.vector.tensor_copy(q_samples[:, :, :, :].rearrange("p a c n -> p c a n"),
                                  qT[:, :, NPR:NT].rearrange("p c (a n) -> p c a n", a=2)).then_inc(q_packed, 1)
            by_e = sink_heads[:, :].rearrange("p (k j r) -> p k r j", k=2, j=2)
            for kv in range(N_KV):
                nc.vector.tensor_copy(sink[:, kv, :].rearrange("p (r j) -> p r j", r=2), by_e[:, kv])
                nc.vector.tensor_scalar(nsink[:, kv, :].rearrange("p (r j) -> p r j", r=2), by_e[:, kv], -1.0, None,
                                        ALU.mult)
            then(nc.vector.tensor_scalar(ssink[:, 1:2], ssink[:, 0:1], -1.0, None, ALU.mult))
            dve.wait_ge(masks_in, 16)
            dve.wait_ge(setup_copied, SETUPS)
            then(nc.vector.memset(conv_u[:, 0:2], 0.0))

            def mask_and_max(h):
                dve.wait_ge(qk_ready, qk_count(h))
                s = soft[:, h % 2]
                if h >= 2:
                    dve.wait_ge(probs_turned, h - 1)
                if h < N_HALF:
                    kv, q0, nq, key0, k0, k1 = half(h)
                    kn = k0 + k1
                    sv = scores_sb[0:nq, h % 2, :].rearrange("p (e n) -> p e n", e=4)[:, :, 0:kn]
                    ps = scores[0:nq].rearrange("p a (j n) -> p (a j) n", j=2)[:, :, 0:kn]
                    mask = const[0:nq, C_MASK + W - k0:C_MASK + W + k1].unsqueeze(1).to_broadcast([nq, 4, kn])
                    ne, nsk, sk = 4, nsink[0:nq, kv, :], sink[0:nq, kv, :]
                else:
                    nq, ne = P, 1
                    sv, ps = scores_sb[:, h % 2, 0:SK], scores.rearrange("p a n -> p (a n)")[:, 0:SK]
                    mask = const[:, C_SMASK:C_SMASK + SK]
                    nsk, sk = ssink[:, 1:2], ssink[:, 0:1]
                nc.vector.scalar_tensor_tensor(out=sv, in0=ps, scalar=QK_SCALE, in1=mask, op0=ALU.mult, op1=ALU.add)\
                    .then_inc(scores_read, 1)
                dve.wait_ge(scores_read, h + 1)
                then(nc.vector.tensor_reduce(s[0:nq, MX, 0:ne], sv, AX_X, ALU.max))
                then(nc.vector.scalar_tensor_tensor(out=s[0:nq, NM, 0:ne], in0=s[0:nq, MX, 0:ne], scalar=-1.0, in1=nsk,
                                                    op0=ALU.mult, op1=ALU.min))
                nc.vector.tensor_tensor(s[0:nq, DS, 0:ne], sk, s[0:nq, NM, 0:ne], ALU.add).then_inc(soft_in, 1)

            def normalise(h):
                s = soft[:, h % 2]
                nq, ne = (half(h)[2], 4) if h < N_HALF else (P, 1)
                dve.wait_ge(exp_done, h + 1)
                then(nc.vector.tensor_tensor(s[0:nq, RC, 0:ne], s[0:nq, RS, 0:ne], s[0:nq, ES, 0:ne], ALU.add))
                then(nc.vector.reciprocal(s[0:nq, RC, 0:ne], s[0:nq, RC, 0:ne]))
                for e in range(ne):
                    kn = sum(half(h)[4:6]) if h < N_HALF else SK
                    pr = scores_sb[0:nq, h % 2, 256 * e:256 * e + kn]
                    ins_ = nc.vector.tensor_scalar(pr, pr, s[0:nq, RC, e:e + 1], None, ALU.mult)
                ins_.then_inc(probs_ready, 1)

            def copy_attn(h):
                dve.wait_ge(pv_ready, h + 1)
                if h < N_HALF:
                    kv, q0, nq = half(h)[:3]
                    dst = qT[:, 2 * kv:2 * kv + 2, q0:q0 + nq]
                    src = turned[:, 0:2 * nq].rearrange("p (j n) -> p j n", j=2)
                else:
                    a = h - N_HALF
                    dst = qT[:, :, NPR + 16 * a:NPR + 16 * (a + 1)]
                    src = turned[:, 0:64].rearrange("p (c n) -> p c n", c=4)
                nc.vector.tensor_copy(dst, src).then_inc(attn_copied, 1)

            def copy_earlier_probs(h):
                if h < 2:
                    return
                dve.wait_ge(probs_turned, h + 1)
                rows, cols = (half(h)[4], 4 * W) if h < N_HALF else (P, 512)
                nc.vector.tensor_copy(probsT[0:rows, 0:cols], turned[0:rows, 0:cols]).then_inc(probsT_dve, 1)

            def sample_u(first, n):
                return conv_u[:, U_S:U_S + 6 * NB_S].rearrange("p (b r) -> p b r", r=6)[:, :, first:first + n]

            def conv(s):
                j, p, part = s // 9, (s % 9) // 3, s % 3
                c0, c1 = PIECES[p]
                n = c1 - c0
                acc = out_bank[(18 + s) % 4][:, 0:n]
                n_pr = min(c1, NPR) - c0
                parts = [(slice(0, n_pr), None)] + ([(slice(n_pr, n), True)] if n > n_pr else [])

                def rows(sl, samples, ap):
                    v = ap[:, sl]
                    return v.rearrange("p (b t) -> p b t", t=T_S) if samples else v

                dve.wait_ge(out_ready, 18 + s + 1)
                if part == 0:
                    if p == 0:
                        nc.vector.tensor_copy(sample_u(0, 2), conv_state[:, j, :].rearrange("p (b r) -> p b r", r=2))
                    nc.vector.tensor_tensor(xa_sb[:, 0:n], acc, rs_squared[:, c0:c1], ALU.mult).then_inc(out_freed, 1)
                    dve.wait_ge(out_freed, 18 + s + 1)
                elif part == 1:
                    for sl, samples in parts:
                        dst = sample_u(2, T_S) if samples else conv_u[:, 2 + c0:2 + c0 + n_pr]
                        ins_ = nc.vector.tensor_tensor(dst, rows(sl, samples, acc), rows(sl, samples, xa_sb), ALU.mult)
                    ins_.then_inc(out_freed, 1)
                    dve.wait_ge(out_freed, 18 + s + 1)
                    for tap in range(3):
                        row = R_CONV + 4 * tap + j
                        wt = prm[:, row:row + 1]
                        for sl, samples in parts:
                            src = sample_u(tap, T_S) if samples else conv_u[:, c0 + tap:c0 + tap + n_pr]
                            y = rows(sl, samples, conv_y)
                            if tap == 0:
                                ins_ = nc.vector.tensor_scalar(y, src, wt, None, ALU.mult)
                            else:
                                ins_ = nc.vector.scalar_tensor_tensor(out=y, in0=src, scalar=wt, in1=y, op0=ALU.mult,
                                                                      op1=ALU.add)
                        then(ins_)
                    then(nc.vector.tensor_tensor(conv_y[:, 0:n], conv_y[:, 0:n], rs[:, c0:c1], ALU.mult))
                    if p == 2:
                        nc.vector.tensor_copy(conv_tail[:, j, 0:2], conv_u[:, 2 + NPR - 2:2 + NPR])
                        nc.vector.tensor_copy(conv_tail[:, j, 2:18].rearrange("p (b r) -> p b r", r=2), sample_u(4, 2))\
                            .then_inc(tail_gathered, 1)
                else:
                    nc.vector.tensor_tensor(conv_out[:, j, c0:c1], acc, conv_y[:, 0:n], ALU.mult).then_inc(out_freed, 1)
                if p == 2:
                    split_lo(6 + 3 * j + part + 4)

            for s in range(SLOTS):
                for h in range(HALVES):
                    if START[h] == s:
                        mask_and_max(h)
                for h in range(HALVES):
                    if START[h] + PV_LAG == s:
                        copy_attn(h)
                conv(s)
                for h in range(HALVES):
                    if START[h] + T_LAG == s:
                        copy_earlier_probs(h)
                for h in range(HALVES):
                    if START[h] + T_LAG - 1 == s:
                        normalise(h)
            for h in range(HALVES):
                if START[h] + PV_LAG >= SLOTS:
                    copy_attn(h)

            for i, (first, src) in enumerate(((0, conv_out), (4, qT))):
                for p, (c0, c1) in enumerate(PIECES):
                    dve.wait_ge(mix_hi, 3 * i + p + 1)
                    nc.vector.tensor_tensor(act_lo[:, first:first + 4, c0:c1], src[:, :, c0:c1],
                                            f32(act_hi[:, first:first + 4, c0:c1]), ALU.subtract)\
                        .then_inc(mix_ready, 1)

            for p, (c0, c1) in enumerate(PIECES):
                for oc in range(KC):
                    m = M_OUT + 8 * p + oc
                    dve.wait_ge(x_again_in[oc], 16 * (p + 1))
                    dve.wait_ge(out_ready, m + 1)
                    nc.vector.tensor_tensor(xT[:, oc, c0:c1], out_bank[m % 4][:, 0:c1 - c0], x_again[:, oc, 0:c1 - c0],
                                            ALU.add).then_inc(out_freed, 1)
                    if p == 2 and oc % 2:
                        split_lo(W_OUT + 4 + oc // 2)

            def add_output(m, oc, piece, g=0):
                c0, c1 = piece
                dve.wait_ge(out_ready, g * GROUP_OUTS + (m + 1))
                nc.vector.tensor_tensor(xT[:, oc, c0:c1], out_bank[m % 4][:, 0:c1 - c0], xT[:, oc, c0:c1], ALU.add)\
                    .then_inc(out_freed, 1)

            def normed_passes(n, mb, w0, before_last=None):
                for p in range(3):
                    for oc in range(KC):
                        add_output(mb + 8 * p + oc, oc, PIECES[p])
                        if p and oc == 0:
                            norm_split_lo(n, p - 1, 2)
                            norm_split_lo(n, p - 1, 3)
                            norm_reduce(n, p - 1, 1)
                        if p == 2 and oc % 2:
                            split_lo(w0 + oc // 2)
                        if oc in (2, 4):
                            norm_split_lo(n, p, oc // 2 - 1)
                        if oc == 5:
                            norm_reduce(n, p, 0)
                        if p and oc == 6:
                            norm_rsqrt(n, p - 1)
                if before_last:
                    before_last()
                norm_split_lo(n, 2, 2)
                norm_split_lo(n, 2, 3)
                norm_reduce(n, 2, 1)

            normed_passes(1, M_OUT + 24, W_OUT + 8)

            def relu_scaled(layer, mb, g, q, p):
                m = mb + q
                c0, c1 = (PIECES, PIECES1)[layer][p]
                n = c1 - c0
                dve.wait_ge(out_ready, g * GROUP_OUTS + (m + 1))
                nc.vector.scalar_tensor_tensor(out=relu[:, q % 2, 0:n], in0=out_bank[m % 4][:, 0:n], scalar=0.0,
                                               in1=rs[:, c0:c1], op0=ALU.max, op1=ALU.mult).then_inc(out_freed, 1)

            def hidden_lo(layer, hb, g, q, p, chunk):
                n = (PIECES, PIECES1)[layer][p][1] - (PIECES, PIECES1)[layer][p][0]
                dve.wait_ge(hid_hi_done, g * UP_OUTS + (hb + q + 1))
                nc.vector.tensor_tensor(hid_lo[p][:, chunk, 0:n], sq[:, q % 2, 0:n], f32(hid_hi[p][:, chunk, 0:n]),
                                        ALU.subtract).then_inc(hid_ready, 1)

            def hidden(layer, mb, hb, g, q, p, chunk):
                relu_scaled(layer, mb, g, q, p)
                hidden_lo(layer, hb, g, q, p, chunk)

            def up(layer, mb, wb, hb, g, after=None):
                for u in range(2):
                    for p in range(3):
                        for i in range(2):
                            hidden(layer, mb, hb, g, 6 * u + 2 * p + i, p, 2 * u + i)
                        if after:
                            after(u, p)
                    for i in range(2):
                        split_lo(wb + 4 + 2 * u + i, g, 8)

            def down(layer, mb, wb, g):
                for p in range(3):
                    for oc in range(KC):
                        add_output(mb + UP_OUTS + 8 * p + oc, oc, (PIECES, PIECES1)[layer][p], g)
                        if p == 2 and oc % 2:
                            split_lo(wb + 8 + oc // 2, g, 8)

            def up_by_piece(mb, wb, hb):
                dve.wait_ge(stored_pool, 16 * N_STORES)
                for p in range(3):
                    for s in range(4):
                        if p == 2:
                            if s == 0:
                                norm_rsqrt(3, p)
                            hidden(1, mb, hb, 0, 4 * p + s, p, s)
                        elif s == 0:
                            pool_pair(p + 1, s)
                            norm_rsqrt(3, p)
                            relu_scaled(1, mb, 0, 4 * p, p)
                            norm_split_lo(3, p + 1, s)
                            hidden_lo(1, hb, 0, 4 * p, p, s)
                        else:
                            relu_scaled(1, mb, 0, 4 * p + s, p)
                            pool_pair(p + 1, s)
                            hidden_lo(1, hb, 0, 4 * p + s, p, s)
                            norm_split_lo(3, p + 1, s)
                            if s >= 2:
                                norm_reduce(3, p + 1, s - 2)
                        if p == 2:
                            split_lo(wb + 4 + s)

            def mlp(layer, mb, wb, hb, after):
                if layer == 0:
                    up(layer, mb, wb, hb, 0, after)
                else:
                    up_by_piece(mb, wb, hb)
                down(layer, mb, wb, 0)
                with dve.Fori(1, GROUPS - 1) as g:
                    up(layer, mb, wb, hb, g)
                    down(layer, mb, wb, g)
                last = GROUPS - 1
                up(layer, mb + GROUP_OUTS * last, wb + 8 * last, hb + UP_OUTS * last, 0)

            mlp(0, M_MLP0, W_MLP0, 0, lambda u, p: norm_rsqrt(1, 2) if (u, p) == (0, 0) else None)

            def scale_maps(p):
                c0, c1 = PIECES[p]
                n_pr = min(c1, NPR) - c0
                at_ = 0 if p == 0 else 16
                for oc in range(KC):
                    m = M_POOL + 8 * p + oc
                    acc = out_bank[m % 4]
                    dve.wait_ge(out_ready, m + 1)
                    ins_ = nc.vector.tensor_tensor(z[p][:, oc, at_:at_ + n_pr], acc[:, 0:n_pr], rs[:, c0:c0 + n_pr],
                                                   ALU.mult)
                    if p == 2:
                        smp = z_samples[:, oc, :].rearrange("p (b r) -> p b r", r=19)
                        ins_ = nc.vector.tensor_tensor(smp[:, :, PM:19],
                                                       acc[:, n_pr:n_pr + NS].rearrange("p (b t) -> p b t", t=T_S),
                                                       rs[:, NPR:NT].rearrange("p (b t) -> p b t", t=T_S), ALU.mult)
                    ins_.then_inc(out_freed, 1)
                dve.wait_ge(out_freed, M_POOL + 8 * (p + 1))
                if p < 2:
                    then(nc.vector.tensor_copy(z[p + 1][:, :, 0:16], z[p][:, :, PW - 16:PW]))

            def pool_pair(p, gi):
                ch = slice(2 * gi, 2 * gi + 2)
                parts = [(z[p][:, ch, :], 0)] + ([(z_samples[:, ch, :], 336)] if p == 2 else [])
                if p or gi:
                    dve.wait_ge(x_pooled, 4 * p + gi)
                for i in range(gi + 1):
                    shift = 2 ** i
                    lo = 2 * shift - 1
                    for zs, at_ in parts:
                        width = zs.shape[2]
                        src = zs if i == 0 else win[:, (i - 1) % 2, :, at_:at_ + width]
                        ins_ = nc.vector.tensor_tensor(win[:, i % 2, :, at_ + lo:at_ + width], src[:, :, lo:width],
                                                       src[:, :, lo - shift:width - shift], ALU.add)
                    then(ins_)
                sums, delta = win[:, gi % 2, :, :], win[:, (gi + 1) % 2, :, :]
                for zs, at_ in parts:
                    width = zs.shape[2]
                    ins_ = nc.vector.scalar_tensor_tensor(out=delta[:, :, at_ + PM:at_ + width],
                                                          in0=sums[:, :, at_ + PM:at_ + width],
                                                          scalar=1.0 / POOL_W[gi], in1=zs[:, :, PM:width],
                                                          op0=ALU.mult, op1=ALU.subtract)
                then(ins_)
                c0, c1 = PIECES1[p]
                n_pr = min(c1, NPR) - c0
                for c in range(2):
                    oc = 2 * gi + c
                    scale = prm[:, R_SCALE + oc:R_SCALE + oc + 1]
                    x = xT[:, oc, c0:c0 + n_pr]
                    ins_ = nc.vector.scalar_tensor_tensor(out=x, in0=delta[:, c, 16:16 + n_pr], scalar=scale, in1=x,
                                                          op0=ALU.mult, op1=ALU.add)
                    if p == 2:
                        x = xT[:, oc, NPR:NT].rearrange("p (b t) -> p b t", t=T_S)
                        smp = delta[:, c, 336:336 + 19 * NB_S].rearrange("p (b r) -> p b r", r=19)[:, :, PM:19]
                        ins_ = nc.vector.scalar_tensor_tensor(out=x, in0=smp, scalar=scale, in1=x, op0=ALU.mult,
                                                              op1=ALU.add)
                ins_.then_inc(x_pooled, 1)

            normed_passes(2, M_POOL - 24, W_POOL, lambda: scale_maps(0))
            scale_maps(1)
            norm_rsqrt(2, 2)
            for c in range(KC):
                ins_ = nc.vector.scalar_tensor_tensor(out=pool_tail[:, c, :], in0=xT[:, c, NPR - PM:NT],
                                                      scalar=gain(2, c), in1=rs[:, NPR - PM:NT], op0=ALU.mult,
                                                      op1=ALU.mult)
            ins_.then_inc(pool_gathered, 1)
            scale_maps(2)
            split_lo(W_MLP1 + 2)
            split_lo(W_MLP1 + 3)
            dve.wait_ge(states_placed, 2)
            for s in range(4):
                pool_pair(0, s)
                if s:
                    norm_split_lo(3, 0, s - 1)
            norm_split_lo(3, 0, 3)
            for half_ in range(2):
                norm_reduce(3, 0, half_)

            mlp(1, M_MLP1, W_MLP1, 96, None)

            def copy_y(t):
                n = P if t < 8 else NS
                dve.wait_ge(fin_turned, 2 * t + 1)
                nc.vector.tensor_copy(y_rows[0:n, t, 0:512], fin_bank[(2 * t) % 4][0:n, :]).then_inc(fin_dve, 1)

            mb = M_MLP1 + GROUP_OUTS * (GROUPS - 1) + UP_OUTS
            for p in range(3):
                for oc in range(KC):
                    add_output(mb + 8 * p + oc, oc, PIECES1[p])
                    if p == 1 and oc == 4:
                        copy_y(0)
                        copy_y(1)
                    if p == 2 and oc in (2, 4, 6):
                        copy_y(1 + oc // 2)
            for t in range(5, 9):
                copy_y(t)


N_STORES = 3 + 2 + 2 * NB_S + 2 + 1 + NB_S

_INS = ["x_prompt", "x_sample", "state_conv", "cache_k_win", "cache_v_win", "state_pool", "meta_tokens", "norm_mix",
        "norm_mlp", "w_in_even", "conv_w", "q_norm", "k_norm", "attn_sinks", "w_out_even", "w_pool", "pool_scale",
        "w_up", "w_down"]
_OUTS = [("y_prompt", (1, SEQ, D)), ("y_sample", (NB_S, T_S, D)), ("conv_prompt", (1, 1, 2, 512)),
         ("conv_sample", (1, NB_S, 2, 512)), ("k_prompt", (1, 1, W, N_KV, DH)), ("k_sample", (1, NB_S, W, N_KV, DH)),
         ("v_prompt", (1, 1, W, N_KV, DH)), ("v_sample", (1, NB_S, W, N_KV, DH)), ("pool_prompt", (1, 1, PM, D)),
         ("pool_sample", (1, NB_S, PM, D))]


def kernel(**inputs):
    import concourse.bacc as _bacc
    from concourse.bass_utils import run_bass_kernel_spmd as _run

    nc = _bacc.Bacc("TRN2", target_bir_lowering=False, num_devices=1)
    arrays = {n: np.ascontiguousarray(inputs[n]) for n in _INS}
    arrays["const"] = constants()
    ins = {n: nc.dram_tensor(f"in_{n}", a.shape, F32, kind="ExternalInput").ap() for n, a in arrays.items()}
    outs = {n: nc.dram_tensor(f"out_{n}", s, F32, kind="ExternalOutput").ap() for n, s in _OUTS}
    trunk_kernel(nc, ins, outs)
    r = _run(nc, [{f"in_{n}": a for n, a in arrays.items()}], core_ids=[0])
    return tuple(r.results[0][f"out_{n}"] for n, _ in _OUTS)
```

```python
from contextlib import ExitStack

import numpy as np

import concourse.bass as bass
from concourse import mybir

F32 = mybir.dt.float32
F32R = mybir.dt.float32r
ALU = mybir.AluOpType
ACT = mybir.ActivationFunctionType
AX_X = mybir.AxisListType.X

P = 128
D = 1024
KC = D // P
SEQ, N_META, NB_S, T_S = 1024, 16, 8, 4
NS = NB_S * T_S
NPR = N_META + SEQ
NT = NPR + NS
DH, N_HEADS, N_KV = 64, 8, 2
W = 128
EPS = 1e-6
QK_SCALE = DH ** -0.5
POOL_W = (2, 4, 8, 16)
PM = 15
D_FF = 4096
GROUPS = D_FF // 512

PIECES = ((0, 368), (368, 720), (720, NT))
PIECES1 = ((N_META, 368), (368, 720), (720, NT))
PW = 368

W_OUT, W_MLP0, W_POOL, W_MLP1, W_END = 18, 26, 90, 92, 156
M_OUT, M_MLP0, M_POOL, M_MLP1 = 54, 102, 390, 426
UP_OUTS, GROUP_OUTS = 12, 36

IN_COLS = [2048, 2176] + [1536 + P * c for c in range(4)]
for _j in range(4):
    IN_COLS += [P * _j, 512 + P * _j, 1024 + P * _j]

N_HALF, N_SAMPLE_HALF = 18, 2
HALVES = N_HALF + N_SAMPLE_HALF
SLOTS = 36
START = [3 + int(1.55 * h) for h in range(HALVES)]
T_LAG, PV_LAG = 2, 3
SK = 4 * W + 16


TILES = [(c0 + P * i, min(c0 + P * (i + 1), c1)) for c0, c1 in PIECES for i in range(3)]


def map_output(i, half):
    return M_POOL + (4 * i - 2 if i else 0) + half


def window_output(i, half):
    return M_POOL + min(4 * i + 4, 34) + half


def last_output(w, in_loop=False):
    if w < W_OUT:
        return 9 * (w // 3) + 6 + w % 3
    if w < W_MLP0:
        half, s = divmod(w - W_OUT, 4)
        return M_OUT + 24 * half + 16 + 2 * s + 1
    if W_POOL <= w < W_MLP1:
        return map_output(8, w - W_POOL)
    wb, mb = (W_MLP0, M_MLP0) if w < W_POOL else (W_MLP1, M_MLP1)
    g, s = divmod(w - wb, 8)
    if s < 4 and w >= W_MLP1 and g == 0 and not in_loop:
        return mb + 8 + s
    if s < 4:
        return mb + GROUP_OUTS * g + 6 * (s // 2) + 4 + s % 2
    return mb + GROUP_OUTS * g + UP_OUTS + 16 + 2 * (s - 4) + 1


def constants():
    ident = np.eye(P)
    mean_all = np.full((P, P), 1.0 / D)
    mean_head = np.kron(np.eye(2), np.full((DH, DH), 1.0 / DH))
    i, j = np.arange(P)[:, None], np.arange(P)[None, :]
    prompt = np.concatenate([np.where(j >= i, 0, -1e30), np.where(j <= i, 0, -1e30)], 1)
    b, t = (np.arange(P) % 16) // T_S, np.arange(P) % T_S
    cb, cs = np.arange(4 * W) // W, np.arange(4 * W) % W
    cache = np.where((cb[None] == b[:, None]) & (cs[None] >= t[:, None]), 0, -1e30)
    nb, nt = np.arange(16) // T_S, np.arange(16) % T_S
    new = np.where((nb[None] == b[:, None]) & (nt[None] <= t[:, None]), 0, -1e30)
    return np.concatenate([ident, mean_all, mean_head, prompt, cache, new], 1).astype(np.float32)


def bands():
    def band(dist, w):
        return np.where((dist >= 0) & (dist < w), 1.0 / w, 0.0) - (dist == 0)

    s, t = np.arange(P)[:, None], np.arange(P)[None, :]
    own = [band(t - s, w) for w in POOL_W]
    prev = [np.where(s < n, band(t[:, :16] + n - s, w), 0.0) for n in PREV_ROWS for w in POOL_W]
    b, q = np.arange(NS)[None, :] // T_S, np.arange(NS)[None, :] % T_S
    sb, sq_ = (s - 64) // T_S, (s - 64) % T_S
    new = [np.where((s >= 64) & (s < 64 + NS) & (sb == b), band(q - sq_, w), 0.0) for w in POOL_W]
    state = [np.where((s < NB_S * PM) & (s // PM == b), band(q + PM - s % PM, w), 0.0) for w in POOL_W]
    return np.concatenate(own + prev + new + state, 1).astype(np.float32)


PREV_ROWS = (128, 112, 96)
B_PREV, B_NEW = 4 * P, 4 * P + 4 * 16 * len(PREV_ROWS)
B_STATE = B_NEW + 4 * NS
B_COLS = B_STATE + 4 * NS

C_ID, C_MEAN, C_HEAD, C_MASK, C_SMASK = 0, 128, 256, 384, 640
C_COLS = C_SMASK + SK

R_NMIX, R_NMLP, R_CONV, R_SCALE, R_Q, R_K, R_ALL = 0, 16, 32, 44, 52, 53, 54


def trunk_kernel(nc, ins, outs):
    x_prompt, x_sample, meta = ins["x_prompt"], ins["x_sample"], ins["meta_tokens"]
    w_in, w_out = ins["w_in_even"], ins["w_out_even"]
    w_pool, w_up, w_down = ins["w_pool"], ins["w_up"], ins["w_down"]

    ctx = ExitStack()
    with ctx:
        def sem(name):
            return ctx.enter_context(nc.semaphore(name))

        base = (nc.sbuf_base + 63) // 64 * 64

        def place(name, shape, dtype, at):
            at = (at + 31) // 32 * 32
            n = 4
            for s in shape[1:]:
                n *= s
            return nc.alloc_sbuf_tensor_at(name, shape, dtype, offset=at), at + n

        xT, at = place("residual", [P, KC, NT], F32, base)
        act_hi, at = place("act_hi", [P, KC, NT], F32R, at)
        act_lo, at = place("act_lo", [P, KC, NT], F32R, at)
        w_hi, at = place("w_hi", [P, 4, D], F32R, at)
        w_lo, at = place("w_lo", [P, 4, D], F32R, at)
        raw, at = place("raw", [P, 2, D], F32, at)
        const, at = place("const", [P, C_COLS], F32, at)
        const_at = at - 4 * C_COLS
        prm, at = place("prm", [P, R_ALL + 2], F32, at)
        rs, shared = place("rs", [P, NT], F32, at)

        conv_out, _ = place("conv_out", [P, 4, NT], F32, base)
        n_keys = NT + NB_S * W
        kT, a = place("kT", [P, n_keys], F32, base + 4 * 4 * NT)
        kT_swapped, a = place("kT_swapped", [P, n_keys], F32, a)
        assert a <= base + 4 * KC * NT
        qT, a = place("qT", [P, 4, NT], F32, shared)
        x_again, a = place("x_again", [P, KC, PW], F32, a)
        scores_sb, a = place("scores_sb", [P, 2, D], F32, a)
        v_blocks, vb_at = place("v_blocks", [P, 11, P], F32, a)
        v_cache, a = place("v_cache", [P, NB_S, P], F32, vb_at)
        probsT, pt_end = place("probsT", [P, D], F32, a)
        U_S = 2 + NPR
        conv_u, a = place("conv_u", [P, U_S + NB_S * 6], F32, pt_end)
        xa_at = a
        xa_sb, a = place("xa_sb", [P, PW], F32, a)
        conv_y, a = place("conv_y", [P, PW], F32, a)
        sink, a = place("sink", [P, 2, 4], F32, a)
        sink_heads, a = place("sink_heads", [P, N_HEADS], F32, a)
        nsink, a = place("nsink", [P, 2, 4], F32, a)
        ssink, a = place("ssink", [P, 2], F32, a)
        conv_state, a = place("conv_state", [P, 4, 16], F32, a)
        conv_tail, a = place("conv_tail", [P, 4, 18], F32, a)
        q_samples, a = place("q_samples", [P, 2, 4, 16], F32, a)
        soft, a = place("soft", [P, 2, 6, 4], F32, a)
        MX, NM, DS, ES, RS, RC = range(6)
        assert a <= nc.sbuf_usable_end, (a, nc.sbuf_usable_end)
        x_rows, a = place("x_rows", [P, 9, D], F32, shared)
        assert a <= vb_at
        cache_rows, a = place("cache_rows", [P, NB_S, P], F32, shared + 4 * 4 * NT)
        rs_squared, a = place("rs_squared", [P, NT], F32, a)
        conv_rows, a = place("conv_rows", [P, 512], F32, a)
        k_tail, a = place("k_tail", [P, 2, P], F32, a)
        assert a <= shared + 4 * 4 * NT + 4 * KC * PW
        v_flat, _ = place("v_flat", [P, NT], F32, pt_end)
        param_rows, _ = place("param_rows", [P, P], F32, pt_end + 4 * 4 * PW)
        conv_tail_rows, a = place("conv_tail_rows", [P, 512], F32, shared + 4 * 4 * NT + 4 * D)

        norm_buf0, a = place("norm_buf0", [P, 4, PW], F32, vb_at - 4 * 11 * P)
        k_flat, a = place("k_flat", [P, NT], F32, a)
        head_sq, a = place("head_sq", [P, 2, PW], F32, a)
        assert a <= pt_end
        norm_sum0, a = place("norm_sum0", [P, 2, PW], F32, xa_at)
        assert a <= xa_at + 4 * 2 * PW + 64

        h_at = shared
        hid_hi, hid_lo = [], []
        for p in range(3):
            width = PIECES[p][1] - PIECES[p][0] if p == 2 else PW
            t, h_at = place(f"hid_hi{p}", [P, 4, width], F32R, h_at)
            hid_hi.append(t)
            t, h_at = place(f"hid_lo{p}", [P, 4, width], F32R, h_at)
            hid_lo.append(t)
        relu, a = place("relu", [P, 2, PW], F32, h_at)
        sq, a = place("sq", [P, 2, PW], F32, a)
        norm_buf_at = a
        norm_buf, a = place("norm_buf", [P, 4, PW], F32, a)
        pool_rows, _ = place("pool_rows", [P, D], F32, norm_buf_at)
        band, a = place("band", [P, B_COLS], F32, a)
        rs_rows, a = place("rs_rows", [P, 10], F32, a)
        pool_state, a = place("pool_state", [P, KC, NB_S * PM], F32, a)
        assert a <= nc.sbuf_usable_end, (a, nc.sbuf_usable_end)
        norm_sum, a = place("norm_sum", [P, 2, PW], F32, const_at + 4 * C_MASK)
        assert a <= const_at + 4 * C_COLS
        z, a = place("z", [P, 3, D], F32, shared)
        z_states, a = place("z_states", [P, D], F32, a)
        assert a <= h_at
        tail_rows, a = place("tail_rows", [P, D], F32, h_at)
        pool_tail, a = place("pool_tail", [P, KC, 47], F32, a)
        assert a <= h_at + 4 * 4 * PW
        y_rows, a = place("y_rows", [P, 9, D], F32, shared)
        assert a <= h_at + 4 * 4 * PW

        ident = const[:, C_ID:C_ID + P]

        out_bank = [ctx.enter_context(nc.psum_tensor(f"out{i}", [P, 512], F32)) for i in range(4)]
        scores = ctx.enter_context(nc.psum_tensor("scores", [P, 2, 512], F32))
        turned = ctx.enter_context(nc.psum_tensor("turned", [P, 512], F32))
        turned2 = ctx.enter_context(nc.psum_tensor("turned2", [P, 512], F32))
        fin_bank = [scores[:, 0, :], scores[:, 1, :], turned[:, :], turned2[:, :]]

        ident_in, mean_in = sem("ident_in"), sem("mean_in")
        params_in, params_rows_in = sem("params_in"), sem("params_rows_in")
        sinks_in = sem("sinks_in")
        x_in = [sem(f"x_in{t}") for t in range(9)]
        raw_in = [sem(f"raw_in{i}") for i in range(2)]
        kcache_in, vcache_in = sem("kcache_in"), sem("vcache_in")
        masks_in = sem("masks_in")
        conv_state_in, pool_state_in = sem("conv_state_in"), sem("pool_state_in")
        x_spilled = sem("x_spilled")
        x_again_in = [sem(f"x_again_in{c}") for c in range(KC)]
        k_moved, k_swapped = sem("k_moved"), sem("k_swapped")
        stored_pool, stored_sp = sem("stored_pool"), sem("stored_sp")
        w_hi_done, w_lo_done = sem("w_hi_done"), sem("w_lo_done")
        out_ready, out_freed = sem("out_ready"), sem("out_freed")
        prm_turned, prm_ready = sem("prm_turned"), sem("prm_ready")
        x_turned = [sem(f"x_turned{i}") for i in range(2)]
        xT_copied = [sem(f"xT_copied{i}") for i in range(2)]
        norm_sq, norm_summed, norm_mean = sem("norm_sq"), sem("norm_summed"), sem("norm_mean")
        norm_root, norm_rs_done = sem("norm_root"), sem("norm_rs_done")
        norm_hi = sem("norm_hi")
        act_ready = sem("act_ready")
        head_scaled = sem("head_scaled")
        head_sq_done, head_mean = sem("head_sq_done"), sem("head_mean")
        head_root, head_rs_done = sem("head_root"), sem("head_rs_done")
        eps_ready = sem("eps_ready")
        setup_turned, setup_copied = sem("setup_turned"), sem("setup_copied")
        q_packed = sem("q_packed")
        qk_ready, scores_read = sem("qk_ready"), sem("scores_read")
        soft_in, exp_done, probs_ready = sem("soft_in"), sem("exp_done"), sem("probs_ready")
        probs_turned = sem("probs_turned")
        probsT_ready = sem("probsT_ready")
        pv_ready, attn_copied = sem("pv_ready"), sem("attn_copied")
        tail_gathered, tail_turned, tail_copied = sem("tail_gathered"), sem("tail_turned"), sem("tail_copied")
        mix_hi, mix_ready = sem("mix_hi"), sem("mix_ready")
        hid_sq_done, hid_hi_done, hid_ready = sem("hid_sq_done"), sem("hid_hi_done"), sem("hid_ready")
        pool_state_turned, pool_state_copied = sem("pool_state_turned"), sem("pool_state_copied")
        bands_in = sem("bands_in")
        state_mapped, z_states_ready = sem("state_mapped"), sem("z_states_ready")
        pool_gathered, pool_turned, pool_copied = sem("pool_gathered"), sem("pool_turned"), sem("pool_copied")
        fin_turned = sem("fin_turned")
        fin_dve, fin_act = sem("fin_dve"), sem("fin_act")
        dve_step = sem("dve_step")
        act_step = sem("act_step")

        x_spill = nc.dram_tensor("x_spill", (P, KC, NT), F32, kind="Internal").ap()

        def norm_pieces(n):
            return PIECES if n < 3 else PIECES1

        def norm_tensors(n):
            return (norm_buf0, norm_sum0) if n == 0 else (norm_buf, norm_sum)

        def gain(n, c):
            row = (R_NMIX, R_NMLP, R_NMIX + KC, R_NMLP + KC)[n] + c
            return prm[:, row:row + 1]

        def half(h):
            n, kv = divmod(h, 2)
            q0 = 0 if n == 0 else N_META + W * (n - 1)
            nq = N_META if n == 0 else W
            k0 = (0, N_META)[n] if n < 2 else W
            return kv, q0, nq, q0 - k0, k0, nq

        def qk_count(h):
            return h + 1 + max(0, h - N_HALF + 1)

        def v_block(n):
            return v_blocks[0:N_META, 8, :] if n == 0 else v_blocks[:, n - 1, :]

        SETUPS = 7
        block = ctx.enter_context(nc.Block())

        @block.sync
        def _(sp):
            def load_x(t):
                if t == 0:
                    sp.dma_start(x_rows[0:N_META, 0, :], meta).then_inc(x_in[0], 16)
                    sp.dma_start(x_rows[N_META:P, 0, :], x_prompt[0, 0:P - N_META, :]).then_inc(x_in[0], 16)
                elif t < 8:
                    sp.dma_start(x_rows[:, t, :], x_prompt[0, P * t - N_META:P * (t + 1) - N_META, :])\
                        .then_inc(x_in[t], 16)
                else:
                    sp.dma_start(x_rows[0:N_META, 8, :], x_prompt[0, SEQ - N_META:SEQ, :]).then_inc(x_in[8], 16)
                    sp.dma_start(x_rows[N_META:N_META + NS, 8, :], x_sample.rearrange("b t d -> (b t) d"))\
                        .then_inc(x_in[8], 16)

            def load_step(src, w, g=0, per_group=0):
                if w >= 2:
                    sp.wait_ge(w_lo_done, g * per_group + (w - 1))
                if W_POOL + 2 <= w < W_POOL + 4 and per_group == 0:
                    sp.wait_ge(state_mapped, w - W_POOL - 1)
                n = src.shape[-1]
                sp.dma_start(raw[:, w % 2, :].rearrange("p (k n) -> p k n", n=n), src).then_inc(raw_in[w % 2], 16)

            def unit_src(weights, col):
                return weights[:, col].rearrange("(k p) n -> p k n", p=P)

            def load_in(w):
                load_step(unit_src(w_in[0], slice(IN_COLS[w], IN_COLS[w] + P)), w)

            for t in range(3):
                load_x(t)
            load_in(0)
            load_in(1)
            for t in range(3, 9):
                load_x(t)
            for w in range(2, W_OUT):
                load_in(w)
            for i in range(8):
                hh, s = divmod(i, 4)
                load_step(unit_src(w_out[0][512 * hh:512 * (hh + 1), :], slice(256 * s, 256 * (s + 1))), W_OUT + i)

            def load_group(layer, wb, g, first=0):
                at_ = (lambda n: slice(0, n)) if g is None else (lambda n: bass.ds(g * 512, n))
                for u in range(first, 4):
                    cols = slice(P * u, P * (u + 1)) if g is None else bass.ds(g * 512 + P * u, P)
                    load_step(unit_src(w_up[layer], cols), wb + u, 0 if g is None else g, 0 if g is None else 8)
                for s in range(4):
                    load_step(unit_src(w_down[layer][at_(512), :], slice(256 * s, 256 * (s + 1))),
                              wb + 4 + s, 0 if g is None else g, 0 if g is None else 8)

            def load_mlp(layer, wb, first):
                load_group(layer, wb, None, first)
                with sp.Fori(1, GROUPS) as g:
                    load_group(layer, wb, g)

            load_mlp(0, W_MLP0, 0)
            for i in range(2):
                load_step(w_pool[0].rearrange("g c e -> (g c) e")[512 * i:512 * (i + 1), :]
                          .rearrange("(k p) n -> p k n", p=P), W_POOL + i)
            for u in range(2):
                load_step(unit_src(w_up[1], slice(P * u, P * (u + 1))), W_MLP1 + u)
            load_mlp(1, W_MLP1, 2)

            for t in range(9):
                sp.wait_ge(fin_dve, t + 1)
                sp.wait_ge(fin_act, t + 1)
                if t < 8:
                    sp.dma_start(outs["y_prompt"][0, P * t:P * (t + 1), :], y_rows[:, t, :]).then_inc(stored_sp, 16)
                else:
                    sp.dma_start(outs["y_sample"].rearrange("b t d -> (b t) d"), y_rows[0:NS, 8, :])\
                        .then_inc(stored_sp, 16)
            sp.wait_ge(stored_sp, 16 * 9)

        @block.gpsimd
        def _(pool):
            n_stored = [0]

            def store(dst, src):
                pool.dma_start(dst, src).then_inc(stored_pool, 16)
                n_stored[0] += 1

            for r, name in ((R_Q, "q_norm"), (R_K, "k_norm")):
                for i in range(2):
                    pool.dma_start(param_rows[r:r + 1, DH * i:DH * (i + 1)], ins[name]).then_inc(params_in, 16)
            pool.dma_start(const[:, C_MEAN:C_MASK], ins["const"][:, C_MEAN:C_MASK]).then_inc(mean_in, 16)
            for p, (c0, c1) in enumerate(PIECES):
                tiles = (3, 6, 9)[p]
                pool.wait_ge(xT_copied[0], tiles)
                pool.wait_ge(xT_copied[1], tiles)
                pool.dma_start(x_spill[:, :, c0:c1], xT[:, :, c0:c1]).then_inc(x_spilled, 16)
            pool.dma_start(sink_heads[:, :], ins["attn_sinks"].broadcast_to([P, N_HEADS])).then_inc(sinks_in, 16)
            for kv in range(N_KV):
                for par in range(2):
                    h = 4 * kv + par
                    for j in range(2):
                        r = 32 * (2 * par + kv) + 16 * j
                        pool.dma_start(ssink[r:r + 16, 0:1],
                                       ins["attn_sinks"][0:1, h + 2 * j:h + 2 * j + 1].broadcast_to([16, 1]))\
                            .then_inc(sinks_in, 16)
            pool.dma_start(const[:, C_MASK:C_COLS], ins["const"][:, C_MASK:C_COLS]).then_inc(masks_in, 16)
            pool.dma_start(cache_rows[:, :, :], ins["cache_k_win"][0].rearrange("b s k d -> s b (k d)"))\
                .then_inc(kcache_in, 16)
            pool.dma_start(conv_rows[0:2 * NB_S, :], ins["state_conv"][0].rearrange("b r d -> (b r) d"))\
                .then_inc(conv_state_in, 16)
            store(outs["k_sample"][0, :, 0:W - T_S], ins["cache_k_win"][0, :, T_S:W])
            store(outs["v_sample"][0, :, 0:W - T_S], ins["cache_v_win"][0, :, T_S:W])
            store(outs["pool_sample"][0, :, 0:PM - T_S, :], ins["state_pool"][0, :, T_S:PM, :])
            pool.wait_ge(out_freed, 7)
            pool.wait_ge(norm_summed, 6)
            pool.wait_ge(act_ready, 12)
            pool.wait_ge(x_spilled, 48)
            pool.dma_start(kT[:, 0:NT], k_flat[:, :]).then_inc(k_moved, 16)
            for i in range(2):
                pool.dma_start(kT_swapped[DH * i:DH * (i + 1), 0:NT], k_flat[DH * (1 - i):DH * (2 - i), :])\
                    .then_inc(k_swapped, 16)
            pool.wait_ge(setup_copied, 2)
            for i in range(2):
                pool.dma_start(kT_swapped[DH * i:DH * (i + 1), NT:n_keys], kT[DH * (1 - i):DH * (2 - i), NT:n_keys])\
                    .then_inc(k_swapped, 16)
            pool.wait_ge(k_moved, 16)
            pool.wait_ge(k_swapped, 64)
            pool.dma_start(v_cache[:, :, :], ins["cache_v_win"][0].rearrange("b s k d -> s b (k d)"))\
                .then_inc(vcache_in, 16)
            pool.wait_ge(setup_copied, SETUPS)
            store(outs["v_prompt"][0, 0].rearrange("s k d -> s (k d)"), v_blocks[:, 7, :])
            store(outs["k_prompt"][0, 0].rearrange("s k d -> s (k d)"), k_tail[:, 0, :])
            for b in range(NB_S):
                store(outs["k_sample"][0, b, W - T_S:W].rearrange("t k d -> t (k d)"),
                      k_tail[T_S * b:T_S * (b + 1), 1, :])
                a, bb = divmod(b, 4)
                store(outs["v_sample"][0, b, W - T_S:W].rearrange("t k d -> t (k d)"),
                      v_blocks[T_S * bb:T_S * (bb + 1), 9 + a, :])
            for p, (c0, c1) in enumerate(PIECES):
                if p == 0:
                    pool.wait_ge(x_spilled, 48)
                    pool.wait_ge(stored_pool, 16 * n_stored[0])
                for oc in range(KC):
                    if p:
                        pool.wait_ge(out_freed, M_OUT + 8 * (p - 1) + oc + 1)
                    elif oc == 1:
                        pool.wait_ge(out_freed, 52)
                    pool.dma_start(x_again[:, oc, 0:c1 - c0], x_spill[:, oc, c0:c1]).then_inc(x_again_in[oc], 16)
            pool.wait_ge(tail_copied, 1)
            store(outs["conv_prompt"][0, 0], conv_tail_rows[0:2, :])
            store(outs["conv_sample"][0].rearrange("b r d -> (b r) d"), conv_tail_rows[2:18, :])
            pool.wait_ge(out_freed, M_MLP0)
            pool.wait_ge(norm_summed, 12)
            pool.wait_ge(stored_pool, 16 * n_stored[0])
            pool.dma_start(pool_rows[0:NB_S * PM, :], ins["state_pool"][0].rearrange("b r d -> (b r) d"))\
                .then_inc(pool_state_in, 16)
            pool.dma_start(band[:, :], ins["bands"]).then_inc(bands_in, 16)
            pool.wait_ge(pool_copied, 2)
            store(outs["pool_prompt"][0, 0], tail_rows[0:PM, :])
            for b in range(NB_S):
                store(outs["pool_sample"][0, b, PM - T_S:PM, :], tail_rows[PM + T_S * b:PM + T_S * (b + 1), :])
            pool.wait_ge(stored_pool, 16 * n_stored[0])

        @block.tensor
        def _(pe):
            def product(out, lhs, rhs, first, last):
                nc.tensor.matmul(out, lhs[0], rhs[0], start=first, stop=False)
                nc.tensor.matmul(out, lhs[0], rhs[1], start=False, stop=False)
                return nc.tensor.matmul(out, lhs[1], rhs[0], start=False, stop=last)

            def stationary(slot, at):
                return w_hi[:, slot, at:at + P], w_lo[:, slot, at:at + P]

            def acts(k, piece):
                c0, c1 = piece
                return act_hi[:, k, c0:c1], act_lo[:, k, c0:c1]

            def take_bank(m, g=0, per_group=0):
                if m >= 4:
                    pe.wait_ge(out_freed, g * per_group + (m - 3))
                return out_bank[m % 4]

            def wait_step(w, g=0, per_group=0):
                pe.wait_ge(w_lo_done, g * per_group + (w + 1))

            def unit_output(m, w, piece, g=0, normed_k=None, midway=None):
                out = take_bank(m, g, GROUP_OUTS)[:, 0:piece[1] - piece[0]]
                for k in range(KC):
                    if normed_k is not None and k % 2 == 0:
                        pe.wait_ge(act_ready, 4 * normed_k + k // 2 + 1)
                    if midway and k == KC // 2:
                        midway()
                    ins_ = product(out, stationary(w % 4, P * k), acts(k, piece), k == 0, k == KC - 1)
                ins_.then_inc(out_ready, 1)

            def down_output(m, w0, oc, n, rhs, g=0):
                out = take_bank(m, g, GROUP_OUTS)[:, 0:n]
                for k in range(4):
                    ins_ = product(out, stationary((w0 + oc // 2) % 4, 256 * k + P * (oc % 2)), rhs(k), k == 0, k == 3)
                ins_.then_inc(out_ready, 1)

            def norm_stats(n, p):
                k = 3 * n + p
                c0, c1 = norm_pieces(n)[p]
                pe.wait_ge(norm_summed, 2 * k + 2)
                if k:
                    pe.wait_ge(norm_root, k)
                if n == 2:
                    cols = [(3 * p + i, *TILES[3 * p + i]) for i in range(3)]
                    if p == 2:
                        cols.append((9, NPR - PM, NT))
                    for col, t0, t1 in cols:
                        for half_ in range(2):
                            ins_ = nc.tensor.matmul(turned2[0:t1 - t0, col:col + 1], norm_sum[:, half_, t0 - c0:t1 - c0],
                                                    const[:, C_MEAN:C_MEAN + 1], start=half_ == 0, stop=half_ == 1)
                    ins_.then_inc(norm_mean, 1)
                    return
                for half_ in range(2):
                    ins_ = nc.tensor.matmul(turned2[:, 0:c1 - c0], const[:, C_MEAN:C_MEAN + P],
                                            norm_tensors(n)[1][:, half_, 0:c1 - c0], start=half_ == 0, stop=half_ == 1)
                ins_.then_inc(norm_mean, 1)

            def head_stats(i):
                pe.wait_ge(head_sq_done, i + 1)
                if i:
                    pe.wait_ge(head_root, i)
                p = HEAD_NORMS[i][1]
                n = PIECES[p][1] - PIECES[p][0]
                nc.tensor.matmul(turned[:, 0:n], const[:, C_HEAD:C_HEAD + P], head_sq[:, i % 2, 0:n],
                                 start=True, stop=True).then_inc(head_mean, 1)

            pe.wait_ge(ident_in, 16)

            def turn_x(t):
                nr = P if t < 8 else N_META + NS
                pe.wait_ge(x_in[t], 32 if t in (0, 8) else 16)
                for half_ in range(2):
                    if t:
                        pe.wait_ge(xT_copied[half_], t)
                    for c in range(4):
                        cc = 4 * half_ + c
                        ins_ = nc.tensor.transpose(scores[:, half_, P * c:P * c + nr], x_rows[0:nr, t, P * cc:P * (cc + 1)],
                                                   ident[0:nr, 0:nr])
                    ins_.then_inc(x_turned[half_], 1)

            for t in range(3):
                turn_x(t)
            pe.wait_ge(params_rows_in, 16 * 4)
            pe.wait_ge(params_in, 16 * 4)
            nc.tensor.transpose(turned[:, 0:R_ALL], param_rows[0:R_ALL, :], ident[0:R_ALL, 0:R_ALL])\
                .then_inc(prm_turned, 1)
            pe.wait_ge(mean_in, 16)
            turn_x(3)

            HEAD_NORMS = [(m, (m % 9) // 3) for m in range(18) if m < 9 and m % 3 != 1 or m >= 9]

            def setup_round(r, turns):
                if r == 0:
                    pe.wait_ge(xT_copied[0], 9)
                    pe.wait_ge(xT_copied[1], 9)
                if r >= 2:
                    pe.wait_ge(setup_copied, r - 1)
                for at_, in_ in turns:
                    k, m_ = in_.partition_size(), in_.free_size()
                    ins_ = nc.tensor.transpose(scores[0:m_, r % 2, at_:at_ + k], in_, ident[0:k, 0:k])
                ins_.then_inc(setup_turned, 1)

            done_heads = 0
            for m in range(18):
                grp, p, i = m // 9, (m % 9) // 3, m % 3
                w = 3 * grp + i
                if p == 0:
                    wait_step(w)
                unit_output(m, w, PIECES[p], normed_k=p if m < 9 and i == 0 else None)
                if m in (3, 6):
                    norm_stats(0, p)
                while done_heads < len(HEAD_NORMS) and HEAD_NORMS[done_heads][0] < m - 1:
                    head_stats(done_heads)
                    done_heads += 1
                for t in ((4, 5), (6, 7), (8,))[m] if m < 3 else ():
                    turn_x(t)
                if m == 0:
                    norm_stats(0, 0)
                if m == 8:
                    pe.wait_ge(kcache_in, 16)
                    for r in range(2):
                        setup_round(r, [(P * b, cache_rows[:, 4 * r + b, :]) for b in range(4)])
                if m == 11:
                    pe.wait_ge(out_freed, 8)
                    for r in range(2):
                        setup_round(2 + r, [(P * b, v_flat[:, N_META + W * (4 * r + b):N_META + W * (4 * r + b + 1)])
                                            for b in range(4)])
                if m == 12:
                    pe.wait_ge(setup_copied, 3)
                    for at_, c in ((0, 0), (P, NPR), (2 * P, NPR + 16)):
                        ins_ = nc.tensor.transpose(scores[0:16, 0, at_:at_ + P], v_flat[:, c:c + 16], ident)
                    ins_.then_inc(setup_turned, 1)
                if m == 14:
                    pe.wait_ge(conv_state_in, 16)
                    pe.wait_ge(setup_copied, 4)
                    for c in range(4):
                        ins_ = nc.tensor.transpose(scores[:, 1, 16 * c:16 * (c + 1)], conv_rows[0:16, P * c:P * (c + 1)],
                                                   ident[0:16, 0:16])
                    ins_.then_inc(setup_turned, 1)
                if m == 16:
                    pe.wait_ge(setup_copied, 5)
                    pe.wait_ge(k_moved, 16)
                    nc.tensor.transpose(scores[:, 0, 0:P], kT[:, NPR - W:NPR], ident)
                    nc.tensor.transpose(scores[0:NS, 0, P:2 * P], kT[:, NPR:NT], ident).then_inc(setup_turned, 1)

            def keys(kv, par, c0, c1):
                return (kT if kv == par else kT_swapped)[DH * par:DH * (par + 1), c0:c1]

            def attn_scores(h):
                if h == 0:
                    pe.wait_ge(out_freed, 18)
                    pe.wait_ge(k_moved, 16)
                    pe.wait_ge(k_swapped, 64)
                    pe.wait_ge(setup_copied, SETUPS)
                else:
                    pe.wait_ge(scores_read, h)
                if h < N_HALF:
                    kv, q0, nq, key0, k0, k1 = half(h)
                    for par in range(2):
                        for j in range(2):
                            ins_ = nc.tensor.matmul(scores[0:nq, par, 256 * j:256 * j + k0 + k1],
                                                    qT[DH * par:DH * (par + 1), 2 * kv + j, q0:q0 + nq],
                                                    keys(kv, par, key0, key0 + k0 + k1), start=True, stop=True)
                    ins_.then_inc(qk_ready, 1)
                    return
                a = h - N_HALF
                if a == 0:
                    pe.wait_ge(q_packed, 1)
                new = NPR + 16 * a
                for par in range(2):
                    for kv in range(N_KV):
                        r = 32 * (2 * par + kv)
                        q = q_samples[DH * par:DH * (par + 1), a, 2 * kv:2 * kv + 2, :].rearrange("p c n -> p (c n)")
                        nc.tensor.matmul(scores[r:r + 32, 0, :], q, keys(kv, par, NT + 4 * W * a, NT + 4 * W * (a + 1)),
                                         start=True, stop=True)
                        ins_ = nc.tensor.matmul(scores[r:r + 32, 1, 0:16], q, keys(kv, par, new, new + 16),
                                                start=True, stop=True)
                    ins_.then_inc(qk_ready, 1)
                    if par == 0:
                        pe.wait_ge(qk_ready, qk_count(h - 1) + 1)

            def turn_probs(h):
                pe.wait_ge(probs_ready, h + 1)
                if h == 0:
                    pe.wait_ge(head_root, len(HEAD_NORMS))
                    pe.wait_ge(norm_root, 3)
                else:
                    pe.wait_ge(attn_copied, h)
                    pe.wait_ge(probsT_ready, h)
                if h < N_HALF:
                    kv, q0, nq, key0, k0, k1 = half(h)
                    for bank, at_, n in ((turned, 0, k0), (turned2, k0, k1)):
                        for e in range(4 if n else 0):
                            ins_ = nc.tensor.transpose(bank[0:n, e * nq:(e + 1) * nq],
                                                       scores_sb[0:nq, h % 2, 256 * e + at_:256 * e + at_ + n],
                                                       ident[0:nq, 0:nq])
                else:
                    for b in range(4):
                        nc.tensor.transpose(turned[:, P * b:P * (b + 1)], scores_sb[:, h % 2, P * b:P * (b + 1)], ident)
                    ins_ = nc.tensor.transpose(turned2[0:16, 0:P], scores_sb[:, h % 2, 4 * P:4 * P + 16], ident)
                ins_.then_inc(probs_turned, 1)

            def attn_values(h):
                pe.wait_ge(probsT_ready, h + 1)
                if h < N_HALF:
                    kv, q0, nq, key0, k0, k1 = half(h)
                    n = h // 2
                    for par in range(2):
                        parts = ([(v_block(n - 1), k0, 0)] if k0 else []) + [(v_block(n), k1, 512)]
                        for i, (vb, kn, at_) in enumerate(parts):
                            ins_ = nc.tensor.matmul(turned[DH * par:DH * (par + 1), 0:2 * nq],
                                                    vb[0:kn, DH * kv:DH * (kv + 1)],
                                                    probsT[0:kn, at_ + 2 * par * nq:at_ + 2 * (par + 1) * nq],
                                                    start=i == 0, stop=i == len(parts) - 1)
                else:
                    a = h - N_HALF
                    if a == 0:
                        pe.wait_ge(vcache_in, 16)
                    for par in range(2):
                        for kv in range(N_KV):
                            r = 32 * (2 * par + kv)
                            out = turned[DH * par:DH * (par + 1), 32 * kv:32 * (kv + 1)]
                            for b in range(4):
                                nc.tensor.matmul(out, v_cache[:, 4 * a + b, DH * kv:DH * (kv + 1)],
                                                 probsT[:, P * b + r:P * b + r + 32], start=b == 0, stop=False)
                            ins_ = nc.tensor.matmul(out, v_blocks[0:16, 9 + a, DH * kv:DH * (kv + 1)],
                                                    probsT[0:16, 512 + r:512 + r + 32], start=False, stop=True)
                ins_.then_inc(pv_ready, 1)

            for s in range(SLOTS):
                m = 18 + s
                w = 6 + 3 * (s // 9) + s % 3
                if (s % 9) // 3 == 0:
                    wait_step(w)

                def values():
                    for h in range(HALVES):
                        if START[h] + PV_LAG == s:
                            attn_values(h)

                unit_output(m, w, PIECES[(s % 9) // 3], midway=values)
                if s < 2:
                    head_stats(len(HEAD_NORMS) - 2 + s)
                for h in range(HALVES):
                    if START[h] == s + 1:
                        attn_scores(h)
                for h in range(HALVES):
                    if START[h] + T_LAG == s:
                        turn_probs(h)
            for h in range(HALVES):
                if START[h] + PV_LAG >= SLOTS:
                    attn_values(h)

            def w_out_half(half_, hook):
                for p, piece in enumerate(PIECES):
                    pe.wait_ge(mix_ready, 3 * half_ + p + 1)
                    for oc in range(KC):
                        m = M_OUT + 24 * half_ + 8 * p + oc
                        if p == 0 and oc % 2 == 0:
                            wait_step(W_OUT + 4 * half_ + oc // 2)
                        down_output(m, W_OUT + 4 * half_, oc, piece[1] - piece[0],
                                    lambda k: acts(4 * half_ + k, piece))
                        hook(p, oc)

            def conv_tail_turn(p, oc):
                if (p, oc) == (0, 7):
                    pe.wait_ge(tail_gathered, 4)
                    for c in range(4):
                        ins_ = nc.tensor.transpose(scores[0:18, 0, P * c:P * (c + 1)], conv_tail[:, c, :], ident)
                    ins_.then_inc(tail_turned, 1)

            w_out_half(0, conv_tail_turn)

            def stats_hook(n):
                def hook(p, oc):
                    if p and oc == 3:
                        norm_stats(n, p - 1)
                    if n == 2 and (p, oc) == (1, 5):
                        for i in range(2):
                            map_pool_state(i)
                return hook

            w_out_half(1, stats_hook(1))

            def turn_pool_state():
                pe.wait_ge(pool_state_in, 16)
                pe.wait_ge(tail_copied, 1)
                for half_ in range(2):
                    for c in range(4):
                        cc = 4 * half_ + c
                        ins_ = nc.tensor.transpose(scores[:, half_, 120 * c:120 * (c + 1)],
                                                   pool_rows[0:120, P * cc:P * (cc + 1)], ident[0:120, 0:120])
                    ins_.then_inc(pool_state_turned, 1)

            def map_pool_state(i):
                pe.wait_ge(raw_in[i], 16 * ((W_POOL + i) // 2 + 1))
                pe.wait_ge(pool_state_copied, 2)
                for g in range(2):
                    for k in range(2):
                        at_ = 512 * g + 256 * k
                        ins_ = nc.tensor.matmul(scores[0:NB_S * PM, i, 256 * g:256 * (g + 1)],
                                                pool_state[:, 4 * i + 2 * g + k, :], raw[:, i, at_:at_ + 256],
                                                start=k == 0, stop=k == 1)
                ins_.then_inc(state_mapped, 1)

            def up(layer, mb, wb, g, after=None, normed=None):
                pieces = (PIECES, PIECES1)[layer]
                for u in range(2):
                    for p, piece in enumerate(pieces):
                        for i in range(2):
                            if p == 0:
                                wait_step(wb + 2 * u + i, g, 8)
                            unit_output(mb + 6 * u + 2 * p + i, wb + 2 * u + i, piece, g,
                                        3 * normed + p if normed is not None and u == 0 and i == 0 else None)
                        if after:
                            after(u, p)

            def up_by_piece(mb, wb):
                for p, piece in enumerate(PIECES1):
                    for s in range(4):
                        if p == 0:
                            wait_step(wb + s)
                        unit_output(mb + 4 * p + s, wb + s, piece, 0, 9 + p if s == 0 else None)
                        if (p, s) == (1, 1):
                            norm_stats(3, 2)

            def down(layer, mb, wb, hb, g, hook=None, by_piece=False):
                pieces = (PIECES, PIECES1)[layer]
                for p, (c0, c1) in enumerate(pieces):
                    pe.wait_ge(hid_ready, g * UP_OUTS + (hb + (4 * p + 4 if by_piece else 6 + 2 * p + 2)))
                    for oc in range(KC):
                        if p == 0 and oc % 2 == 0:
                            wait_step(wb + 4 + oc // 2, g, 8)
                        down_output(mb + UP_OUTS + 8 * p + oc, wb + 4, oc, c1 - c0,
                                    lambda k: (hid_hi[p][:, k, 0:c1 - c0], hid_lo[p][:, k, 0:c1 - c0]), g)
                        if hook:
                            hook(p, oc)

            def at_group(mb, wb, hb, g):
                return mb + GROUP_OUTS * g, wb + 8 * g, hb + UP_OUTS * g

            def mlp(layer, mb, wb, hb, after, normed, hook):
                m0, w0, h0 = mb, wb, hb
                if layer == 0:
                    up(layer, m0, w0, 0, after, normed)
                else:
                    up_by_piece(m0, w0)
                down(layer, m0, w0, h0, 0, None, layer == 1)
                with pe.Fori(1, GROUPS - 1) as g:
                    up(layer, mb, wb, g)
                    down(layer, mb, wb, hb, g)
                m0, w0, h0 = at_group(mb, wb, hb, GROUPS - 1)
                up(layer, m0, w0, 0)
                down(layer, m0, w0, h0, 0, hook)

            def mlp0_hook(u, p):
                if (u, p) == (0, 1):
                    norm_stats(1, 2)
                if (u, p) == (1, 0):
                    turn_pool_state()

            mlp(0, M_MLP0, W_MLP0, 0, mlp0_hook, 1, stats_hook(2))

            def map_tile(i):
                t0, t1 = TILES[i]
                for half_ in range(2):
                    out = take_bank(map_output(i, half_))
                    if i == 0:
                        wait_step(W_POOL + half_)
                    slot = (W_POOL + half_) % 4
                    for g in range(2):
                        gi = 2 * half_ + g
                        pe.wait_ge(act_ready, 4 * (6 + i // 3) + gi + 1)
                        for k in range(2):
                            at_ = 512 * g + 256 * k
                            lhs = act_hi[:, 2 * gi + k, t0:t1], act_lo[:, 2 * gi + k, t0:t1]
                            rhs = w_hi[:, slot, at_:at_ + 256], w_lo[:, slot, at_:at_ + 256]
                            ins_ = product(out[0:t1 - t0, 256 * g:256 * (g + 1)], lhs, rhs, k == 0, k == 1)
                    ins_.then_inc(out_ready, 1)

            def window_tile(i):
                n = TILES[i][1] - TILES[i][0]
                n_own = 64 if i == 8 else n
                if i == 0:
                    pe.wait_ge(bands_in, 16)
                for half_ in range(2):
                    pe.wait_ge(out_freed, map_output(i, half_) + 1)
                    if i == 8:
                        pe.wait_ge(z_states_ready, half_ + 1)
                    out = take_bank(window_output(i, half_))
                    for cc in range(4):
                        c = 4 * half_ + cc
                        gi, at_ = c // 2, P * cc
                        own = z[0:n, i % 3, P * c:P * (c + 1)]
                        terms = [(own, band[0:n, P * gi:P * gi + n_own], 0, n_own, True)]
                        if i:
                            pn = TILES[i - 1][1] - TILES[i - 1][0]
                            b = B_PREV + 64 * PREV_ROWS.index(pn) + 16 * gi
                            terms.append((z[0:pn, (i - 1) % 3, P * c:P * (c + 1)], band[0:pn, b:b + 16], 0, 16, False))
                        if i == 8:
                            ns = NB_S * PM
                            terms.append((own, band[0:n, B_NEW + NS * gi:B_NEW + NS * (gi + 1)], n_own, NS, True))
                            terms.append((z_states[0:ns, P * c:P * (c + 1)],
                                          band[0:ns, B_STATE + NS * gi:B_STATE + NS * (gi + 1)], n_own, NS, False))
                        for j, (tokens, b, o, width, first) in enumerate(terms):
                            last = j + 1 == len(terms) or terms[j + 1][4]
                            ins_ = nc.tensor.matmul(out[:, at_ + o:at_ + o + width], tokens, b, start=first, stop=last)
                    ins_.then_inc(out_ready, 1)

            map_tile(0)
            for i in range(1, 9):
                map_tile(i)
                if i == 3:
                    norm_stats(2, 2)
                if i == 4:
                    pe.wait_ge(pool_gathered, 1)
                    pe.wait_ge(z_states_ready, 2)
                    for half_ in range(2):
                        for c in range(4):
                            ins_ = nc.tensor.transpose(scores[0:47, half_, P * c:P * (c + 1)],
                                                       pool_tail[:, 4 * half_ + c, :], ident)
                        ins_.then_inc(pool_turned, 1)
                if i == 7:
                    norm_stats(3, 0)
                window_tile(i - 1)
            window_tile(8)
            norm_stats(3, 1)

            def turn_y(t):
                c0 = N_META + P * t
                n = P if t < 8 else NS
                for half_ in range(2):
                    i = 2 * t + half_
                    if i >= 4:
                        pe.wait_ge((fin_dve, fin_act)[half_], t - 1)
                    if half_ == 0:
                        last_piece = 0 if c0 + n <= 368 else 1 if c0 + n <= 720 else 2
                        pe.wait_ge(out_freed, M_MLP1 + GROUP_OUTS * (GROUPS - 1) + UP_OUTS + 8 * (last_piece + 1))
                    for c in range(4):
                        cc = 4 * half_ + c
                        ins_ = nc.tensor.transpose(fin_bank[i % 4][0:n, P * c:P * (c + 1)], xT[:, cc, c0:c0 + n], ident)
                    ins_.then_inc(fin_turned, 1)

            def y_hook(p, oc):
                if oc == 3 and p == 1:
                    pe.wait_ge(norm_root, 12)
                    pe.wait_ge(pool_copied, 2)
                    turn_y(0)
                    turn_y(1)
                if p == 2 and oc in (1, 3, 5):
                    turn_y(2 + oc // 2)

            mlp(1, M_MLP1, W_MLP1, 96, None, None, y_hook)
            for t in range(5, 9):
                turn_y(t)

        @block.scalar
        def _(act):
            def split_hi(w, g=0, per_group=0, last=None):
                act.wait_ge(raw_in[w % 2], g * (8 * per_group) + 16 * (w // 2 + 1))
                if w >= 4:
                    act.wait_ge(out_ready, g * (GROUP_OUTS if per_group else 0)
                                + (last_output(w - 4, in_loop=per_group > 0) + 1))
                nc.scalar.activation(w_hi[:, w % 4, :], raw[:, w % 2, :], ACT.Copy).then_inc(w_hi_done, 1)

            def wait_residual(n, p, c):
                if n == 0:
                    act.wait_ge(xT_copied[c // 4], 3 * p + 3)
                elif n == 3:
                    act.wait_ge(out_freed, window_output(3 * p + 2, c // 4) + 1)
                else:
                    act.wait_ge(out_freed, {1: M_OUT + 24, 2: M_POOL - 24}[n] + 8 * p + c + 1)

            def norm_square(n, p, half_):
                i = 2 * (3 * n + p) + half_
                c0, c1 = norm_pieces(n)[p]
                wait_residual(n, p, 4 * half_ + 3)
                if i:
                    act.wait_ge(norm_summed, i)
                nc.scalar.activation(norm_tensors(n)[0][:, :, 0:c1 - c0], xT[:, 4 * half_:4 * half_ + 4, c0:c1],
                                     ACT.Square).then_inc(norm_sq, 1)

            def norm_sqrt(n, p):
                k = 3 * n + p
                c0, c1 = norm_pieces(n)[p]
                act.wait_ge(norm_mean, k + 1)
                if n == 2:
                    rows_ = TILES[3 * p + 2][1] - TILES[3 * p + 2][0]
                    parts = [(P, 3 * p, 2), (rows_, 3 * p + 2, 1)] + ([(47, 9, 1)] if p == 2 else [])
                    for rows_, col, w in parts:
                        ins_ = nc.scalar.activation(rs_rows[0:rows_, col:col + w], turned2[0:rows_, col:col + w],
                                                    ACT.Sqrt, bias=prm[0:rows_, R_ALL:R_ALL + 1])
                    ins_.then_inc(norm_root, 1)
                    return
                nc.scalar.activation(rs[:, c0:c1], turned2[:, 0:c1 - c0], ACT.Sqrt,
                                     bias=prm[:, R_ALL:R_ALL + 1]).then_inc(norm_root, 1)

            def norm_split_hi(n, p, pair):
                c0, c1 = norm_pieces(n)[p]
                wait_residual(n, p, 7 if n == 1 and pair >= 2 else 2 * pair + 1)
                for c in (2 * pair, 2 * pair + 1):
                    ins_ = nc.scalar.activation(act_hi[:, c, c0:c1], xT[:, c, c0:c1], ACT.Copy, scale=gain(n, c))
                ins_.then_inc(norm_hi, 1)

            def norm_splits(n, p):
                for pair in range(4):
                    norm_split_hi(n, p, pair)
                for half_ in range(2):
                    norm_square(n, p, half_)

            act.dma_start(const[:, 0:C_MEAN], ins["const"][:, 0:C_MEAN]).then_inc(ident_in, 16)
            rows = [(R_NMIX, ins["norm_mix"].rearrange("l (c p) -> (l c) p", p=P)),
                    (R_NMLP, ins["norm_mlp"].rearrange("l (c p) -> (l c) p", p=P)),
                    (R_CONV, ins["conv_w"][0].rearrange("j (c p) -> (j c) p", p=P)),
                    (R_SCALE, ins["pool_scale"].rearrange("l (c p) -> (l c) p", p=P))]
            for r, src in rows:
                act.dma_start(param_rows[r:r + src.shape[0], :], src).then_inc(params_rows_in, 16)

            def copy_x(t):
                nr = P if t < 8 else N_META + NS
                for half_ in range(2):
                    act.wait_ge(x_turned[half_], t + 1)
                    nc.scalar.activation(xT[:, 4 * half_:4 * half_ + 4, P * t:P * t + nr],
                                         scores[:, half_, :].rearrange("p (c n) -> p c n", c=4)[:, :, 0:nr], ACT.Copy)\
                        .then_inc(xT_copied[half_], 1)

            copy_x(0)
            copy_x(1)
            split_hi(0)
            copy_x(2)
            act.wait_ge(prm_turned, 1)
            nc.scalar.activation(prm[:, 0:R_ALL], turned[:, 0:R_ALL], ACT.Copy).then_inc(prm_ready, 1)
            act.wait_ge(prm_ready, 1)
            for pair in range(4):
                norm_split_hi(0, 0, pair)
            norm_square(0, 0, 0)
            split_hi(1)
            norm_square(0, 0, 1)
            copy_x(3)
            copy_x(4)
            copy_x(5)
            act.wait_ge(eps_ready, 1)
            norm_sqrt(0, 0)
            split_hi(2)

            def setup_copy(r, dst, src):
                act.wait_ge(setup_turned, r + 1)
                nc.scalar.activation(dst, src, ACT.Copy).then_inc(setup_copied, 1)

            head_outputs = [m for m in range(18) if m >= 9 or m % 3 != 1]

            def head_sqrt(i):
                m = head_outputs[i]
                n = PIECES[(m % 9) // 3][1] - PIECES[(m % 9) // 3][0]
                act.wait_ge(head_mean, i + 1)
                nc.scalar.activation(head_sq[:, i % 2, 0:n], turned[:, 0:n], ACT.Sqrt, bias=prm[:, R_ALL:R_ALL + 1])\
                    .then_inc(head_root, 1)

            i = 0
            for m in range(18):
                grp, p, part = m // 9, (m % 9) // 3, m % 3
                if m in (3, 6):
                    norm_sqrt(0, p)
                if m - 2 in head_outputs:
                    head_sqrt(head_outputs.index(m - 2))
                if m in head_outputs:
                    n = PIECES[p][1] - PIECES[p][0]
                    act.wait_ge(head_scaled, i + 1)
                    if i >= 2:
                        act.wait_ge(out_freed, head_outputs[i - 2] + 1)
                    nc.scalar.activation(head_sq[:, i % 2, 0:n], out_bank[m % 4][:, 0:n], ACT.Square)\
                        .then_inc(head_sq_done, 1)
                    i += 1
                if m < 3:
                    copy_x(m + 6)
                if m in (0, 3):
                    for pair in range(4):
                        norm_split_hi(0, p + 1, pair)
                if m in (1, 4):
                    for half_ in range(2):
                        norm_square(0, p + 1, half_)
                if m == 3:
                    split_hi(3)
                if p == 2:
                    split_hi(3 * grp + part + 4)
                if m == 8:
                    act.wait_ge(x_spilled, 48)
                    act.wait_ge(norm_summed, 6)
                    act.wait_ge(act_ready, 12)
                    for r in range(2):
                        setup_copy(r, kT[:, NT + 4 * W * r:NT + 4 * W * (r + 1)], scores[:, r, :])
                if m == 11:
                    act.wait_ge(act_ready, 12)
                    for r in range(2):
                        setup_copy(2 + r, v_blocks[:, 4 * r:4 * (r + 1), :],
                                   scores[:, r, :].rearrange("p (b n) -> p b n", b=4))
                if m == 12:
                    setup_copy(4, v_blocks[0:16, 8:11, :], scores[0:16, 0, 0:3 * P].rearrange("p (b n) -> p b n", b=3))
                if m == 14:
                    setup_copy(5, conv_state[:, :, :], scores[:, 1, 0:64].rearrange("p (c n) -> p c n", c=4))
                if m == 16:
                    act.wait_ge(setup_turned, SETUPS)
                    nc.scalar.activation(k_tail[0:NS, 1, :], scores[0:NS, 0, P:2 * P], ACT.Copy).then_inc(act_step, 1)
                    act.wait_ge(act_step, 1)
                    nc.scalar.activation(k_tail[:, 0, :], scores[:, 0, 0:P], ACT.Copy).then_inc(setup_copied, 1)

            head_sqrt(len(head_outputs) - 2)
            head_sqrt(len(head_outputs) - 1)

            def exps(h):
                act.wait_ge(soft_in, h + 1)
                s = soft[:, h % 2]
                if h < N_HALF:
                    kv, q0, nq, key0, k0, k1 = half(h)
                    for e in range(4):
                        pr = scores_sb[0:nq, h % 2, 256 * e:256 * e + k0 + k1]
                        nc.scalar.activation(pr, pr, ACT.Exp, bias=s[0:nq, NM, e:e + 1],
                                             accum_out=s[0:nq, RS, e:e + 1])
                    nc.scalar.activation(s[0:nq, ES, :], s[0:nq, DS, :], ACT.Exp).then_inc(exp_done, 1)
                else:
                    pr = scores_sb[:, h % 2, 0:SK]
                    nc.scalar.activation(pr, pr, ACT.Exp, bias=s[:, NM, 0:1], accum_out=s[:, RS, 0:1])
                    nc.scalar.activation(s[:, ES, 0:1], s[:, DS, 0:1], ACT.Exp).then_inc(exp_done, 1)

            def copy_probs(h):
                act.wait_ge(probs_turned, h + 1)
                if h >= 2:
                    rows, cols = (half(h)[4], 4 * W) if h < N_HALF else (P, 512)
                    nc.scalar.activation(probsT[0:rows, 0:cols], turned[0:rows, 0:cols], ACT.Copy)
                if h < N_HALF:
                    kv, q0, nq, key0, k0, k1 = half(h)
                    nc.scalar.activation(probsT[0:k1, 512:512 + 4 * nq], turned2[0:k1, 0:4 * nq], ACT.Copy)\
                        .then_inc(probsT_ready, 1)
                else:
                    nc.scalar.activation(probsT[0:16, 512:512 + P], turned2[0:16, 0:P], ACT.Copy).then_inc(probsT_ready, 1)

            def conv_mix_hi(p):
                c0, c1 = PIECES[p]
                act.wait_ge(out_freed, 45 + 3 * p + 3)
                nc.scalar.activation(act_hi[:, 0:4, c0:c1], conv_out[:, :, c0:c1], ACT.Copy).then_inc(mix_hi, 1)

            for s in range(SLOTS):
                if s in (31, 34):
                    conv_mix_hi((s - 31) // 3)
                for h in range(HALVES):
                    if START[h] == s:
                        exps(h)
                if (s % 9) // 3 == 2:
                    split_hi(6 + 3 * (s // 9) + s % 3 + 4)
                for h in range(HALVES):
                    if START[h] + T_LAG == s:
                        copy_probs(h)

            conv_mix_hi(2)
            act.wait_ge(attn_copied, HALVES)
            for c0, c1 in PIECES:
                nc.scalar.activation(act_hi[:, 4:8, c0:c1], qT[:, :, c0:c1], ACT.Copy).then_inc(mix_hi, 1)
            def splits_half0():
                for s in range(4):
                    split_hi(W_OUT + 4 + s)

            splits_half0()
            act.wait_ge(tail_turned, 1)
            act.wait_ge(out_freed, M_OUT + 24)
            nc.scalar.activation(conv_tail_rows[0:18, :], scores[0:18, 0, :], ACT.Copy).then_inc(tail_copied, 1)

            def normed_pass_hi(n, p, w0):
                for what in ("w0", "n0", "w1", "n1", "s0", "r", "w2", "w3", "n2", "n3", "s1"):
                    if what[0] == "w":
                        if w0 is not None:
                            split_hi(w0 + int(what[1]))
                    elif what == "r":
                        if p:
                            norm_sqrt(n, p - 1)
                    elif what[0] == "s":
                        norm_square(n, p, int(what[1]))
                    else:
                        norm_split_hi(n, p, int(what[1]))

            normed_pass_hi(1, 0, None)
            normed_pass_hi(1, 1, None)
            normed_pass_hi(1, 2, W_OUT + 8)

            def hidden(layer, mb, hb, g, q, p, chunk):
                m = mb + q
                c0, c1 = (PIECES, PIECES1)[layer][p]
                n = c1 - c0
                act.wait_ge(out_freed, g * GROUP_OUTS + (m + 1))
                if hb + q >= 2:
                    act.wait_ge(hid_ready, g * UP_OUTS + (hb + q - 1))
                nc.scalar.activation(sq[:, q % 2, 0:n], relu[:, q % 2, 0:n], ACT.Square).then_inc(hid_sq_done, 1)
                act.wait_ge(hid_sq_done, g * UP_OUTS + (hb + q + 1))
                nc.scalar.activation(hid_hi[p][:, chunk, 0:n], sq[:, q % 2, 0:n], ACT.Copy)\
                    .then_inc(hid_hi_done, 1)

            def up(layer, mb, wb, hb, g, after=None):
                for u in range(2):
                    for p in range(3):
                        for i in range(2):
                            hidden(layer, mb, hb, g, 6 * u + 2 * p + i, p, 2 * u + i)
                        if after:
                            after(u, p)
                    for i in range(2):
                        split_hi(wb + 4 + 2 * u + i, g, 8)

            def up_by_piece(mb, wb, hb):
                for p in range(3):
                    for s in range(4):
                        if (p, s) == (0, 0):
                            norm_sqrt(3, 1)
                        if (p, s) == (1, 2):
                            norm_sqrt(3, 2)
                        hidden(1, mb, hb, 0, 4 * p + s, p, s)
                        if p == 2:
                            split_hi(wb + 4 + s)

            def down_splits(wb, g):
                for s in range(4):
                    split_hi(wb + 8 + s, g, 8)

            def mlp(layer, mb, wb, hb, after):
                if layer == 0:
                    up(layer, mb, wb, hb, 0, after)
                else:
                    up_by_piece(mb, wb, hb)
                down_splits(wb, 0)
                with act.Fori(1, GROUPS - 1) as g:
                    up(layer, mb, wb, hb, g)
                    down_splits(wb, g)
                last = GROUPS - 1
                up(layer, mb + GROUP_OUTS * last, wb + 8 * last, hb + UP_OUTS * last, 0)

            def mlp0_extras(u, p):
                if (u, p) == (0, 1):
                    norm_sqrt(1, 2)
                if (u, p) == (1, 0):
                    for half_ in range(2):
                        act.wait_ge(pool_state_turned, half_ + 1)
                        nc.scalar.activation(pool_state[:, 4 * half_:4 * (half_ + 1), :],
                                             scores[:, half_, 0:480].rearrange("p (c n) -> p c n", c=4), ACT.Copy)\
                            .then_inc(pool_state_copied, 1)

            act.wait_ge(stored_pool, 16 * (N_STORES - 1 - NB_S))
            mlp(0, M_MLP0, W_MLP0, 0, mlp0_extras)

            for p in range(3):
                normed_pass_hi(2, p, W_POOL if p == 2 else None)
            for i in range(9):
                act.wait_ge(out_ready, map_output(i, 1) + 1)
                if i == 3:
                    norm_sqrt(2, 2)
                if i == 1:
                    act.wait_ge(out_ready, M_POOL)
                    for half_ in range(2):
                        act.wait_ge(state_mapped, half_ + 1)
                        nc.scalar.activation(z_states[0:NB_S * PM, 512 * half_:512 * (half_ + 1)],
                                             scores[0:NB_S * PM, half_, :], ACT.Copy).then_inc(z_states_ready, 1)
                if i in (4, 7):
                    p = i // 3 - 1
                    for pair in range(4):
                        norm_split_hi(3, p, pair)
                    norm_square(3, p, 0)
                if i in (5, 8):
                    norm_square(3, i // 3 - 1, 1)
                if i == 4:
                    act.wait_ge(norm_rs_done, 9)
                    for half_ in range(2):
                        act.wait_ge(pool_turned, half_ + 1)
                        nc.scalar.activation(tail_rows[0:47, 512 * half_:512 * (half_ + 1)], scores[0:47, half_, :],
                                             ACT.Copy, scale=rs_rows[0:47, 9:10]).then_inc(pool_copied, 1)
                if i == 7:
                    norm_sqrt(3, 0)
            split_hi(W_MLP1 + 2)
            split_hi(W_MLP1 + 3)
            norm_splits(3, 2)

            mlp(1, M_MLP1, W_MLP1, 96, None)

            for t in range(9):
                n = P if t < 8 else NS
                act.wait_ge(fin_turned, 2 * t + 2)
                nc.scalar.activation(y_rows[0:n, t, 512:1024], fin_bank[(2 * t + 1) % 4][0:n, :], ACT.Copy)\
                    .then_inc(fin_act, 1)

        @block.vector
        def _(dve):
            steps = [0]

            def then(ins_):
                ins_.then_inc(dve_step, 1)
                steps[0] += 1
                dve.wait_ge(dve_step, steps[0])

            def f32(t):
                return t.bitcast(F32)

            def split_lo(w, g=0, per_group=0):
                dve.wait_ge(w_hi_done, g * per_group + (w + 1))
                nc.vector.tensor_tensor(w_lo[:, w % 4, :], raw[:, w % 2, :], f32(w_hi[:, w % 4, :]), ALU.subtract)\
                    .then_inc(w_lo_done, 1)

            def norm_reduce(n, p, half_):
                i = 2 * (3 * n + p) + half_
                c0, c1 = norm_pieces(n)[p]
                buf, total = norm_tensors(n)
                dve.wait_ge(norm_sq, i + 1)
                if i >= 2:
                    dve.wait_ge(norm_mean, i // 2)
                nc.vector.tensor_reduce(total[:, half_, 0:c1 - c0], buf[:, :, 0:c1 - c0].rearrange("p c n -> p n c"),
                                        AX_X, ALU.add).then_inc(norm_summed, 1)

            def norm_rsqrt(n, p):
                k = 3 * n + p
                c0, c1 = norm_pieces(n)[p]
                dve.wait_ge(norm_root, k + 1)
                if n == 2:
                    rows_ = TILES[3 * p + 2][1] - TILES[3 * p + 2][0]
                    parts = [(P, 3 * p, 2), (rows_, 3 * p + 2, 1)] + ([(47, 9, 1)] if p == 2 else [])
                    for rows_, col, w in parts:
                        ins_ = nc.vector.reciprocal(rs_rows[0:rows_, col:col + w], rs_rows[0:rows_, col:col + w])
                    ins_.then_inc(norm_rs_done, 1)
                    dve.wait_ge(norm_rs_done, k + 1)
                    return
                nc.vector.reciprocal(rs[:, c0:c1], rs[:, c0:c1]).then_inc(norm_rs_done, 1)
                dve.wait_ge(norm_rs_done, k + 1)

            def norm_split_lo(n, p, pair):
                c0, c1 = norm_pieces(n)[p]
                dve.wait_ge(norm_hi, 4 * (3 * n + p) + pair + 1)
                for c in (2 * pair, 2 * pair + 1):
                    ins_ = nc.vector.scalar_tensor_tensor(out=act_lo[:, c, c0:c1], in0=xT[:, c, c0:c1],
                                                          scalar=gain(n, c), in1=f32(act_hi[:, c, c0:c1]),
                                                          op0=ALU.mult, op1=ALU.subtract)
                ins_.then_inc(act_ready, 1)

            def norm_splits(n, p):
                for pair in range(4):
                    norm_split_lo(n, p, pair)
                for half_ in range(2):
                    norm_reduce(n, p, half_)

            nc.vector.memset(prm[:, R_ALL:R_ALL + 1], EPS).then_inc(eps_ready, 1)

            split_lo(0)
            dve.wait_ge(prm_ready, 1)
            for pair in range(4):
                norm_split_lo(0, 0, pair)
            norm_reduce(0, 0, 0)
            split_lo(1)
            norm_reduce(0, 0, 1)
            norm_rsqrt(0, 0)
            split_lo(2)

            heads = [m for m in range(18) if m >= 9 or m % 3 != 1]

            def head_finish(m):
                i = heads.index(m)
                grp, p, part = m // 9, (m % 9) // 3, m % 3
                c0, c1 = PIECES[p]
                head_rs = head_sq[:, i % 2, 0:c1 - c0]
                dve.wait_ge(head_root, i + 1)
                nc.vector.reciprocal(head_rs, head_rs).then_inc(head_rs_done, 1)
                dve.wait_ge(head_rs_done, i + 1)
                if (grp, part) == (0, 0):
                    dst, row = k_flat[:, c0:c1], R_K
                else:
                    dst, row = qT[:, 0 if grp == 0 else part + 1, c0:c1], R_Q
                nc.vector.scalar_tensor_tensor(out=dst, in0=out_bank[m % 4][:, 0:c1 - c0], scalar=prm[:, row:row + 1],
                                               in1=head_rs, op0=ALU.mult, op1=ALU.mult).then_inc(out_freed, 1)

            def finish(m):
                if m in heads:
                    head_finish(m)
                    return
                c0, c1 = PIECES[(m % 9) // 3]
                dve.wait_ge(out_ready, m + 1)
                nc.vector.tensor_tensor(v_flat[:, c0:c1], out_bank[m % 4][:, 0:c1 - c0], rs[:, c0:c1], ALU.mult)\
                    .then_inc(out_freed, 1)

            for m in range(18):
                grp, p, part = m // 9, (m % 9) // 3, m % 3
                c0, c1 = PIECES[p]
                n = c1 - c0
                acc = out_bank[m % 4][:, 0:n]
                if m in (3, 6):
                    norm_rsqrt(0, p)
                if m in heads:
                    dve.wait_ge(out_ready, m + 1)
                    nc.vector.tensor_tensor(acc, acc, rs[:, c0:c1], ALU.mult).then_inc(head_scaled, 1)
                    dve.wait_ge(head_scaled, heads.index(m) + 1)
                if m >= 2:
                    finish(m - 2)
                if m in (0, 3):
                    for pair in range(4):
                        norm_split_lo(0, p + 1, pair)
                if m in (1, 4):
                    for half_ in range(2):
                        norm_reduce(0, p + 1, half_)
                if m == 3:
                    split_lo(3)
                if p == 2 and m < 17:
                    split_lo(3 * grp + part + 4)
                if m == 12:
                    then(nc.vector.tensor_tensor(rs_squared[:, :], rs[:, :], rs[:, :], ALU.mult))
            finish(16)
            finish(17)
            split_lo(9)

            dve.wait_ge(sinks_in, 16 * 9)
            dve.wait_ge(out_freed, 18)
            nc.vector.tensor_copy(q_samples[:, :, :, :].rearrange("p a c n -> p c a n"),
                                  qT[:, :, NPR:NT].rearrange("p c (a n) -> p c a n", a=2)).then_inc(q_packed, 1)
            by_e = sink_heads[:, :].rearrange("p (k j r) -> p k r j", k=2, j=2)
            for kv in range(N_KV):
                nc.vector.tensor_copy(sink[:, kv, :].rearrange("p (r j) -> p r j", r=2), by_e[:, kv])
                nc.vector.tensor_scalar(nsink[:, kv, :].rearrange("p (r j) -> p r j", r=2), by_e[:, kv], -1.0, None,
                                        ALU.mult)
            then(nc.vector.tensor_scalar(ssink[:, 1:2], ssink[:, 0:1], -1.0, None, ALU.mult))
            dve.wait_ge(masks_in, 16)
            dve.wait_ge(setup_copied, SETUPS)
            then(nc.vector.memset(conv_u[:, 0:2], 0.0))

            def mask_and_max(h):
                dve.wait_ge(qk_ready, qk_count(h))
                s = soft[:, h % 2]
                if h >= 2:
                    dve.wait_ge(probs_turned, h - 1)
                if h < N_HALF:
                    kv, q0, nq, key0, k0, k1 = half(h)
                    kn = k0 + k1
                    sv = scores_sb[0:nq, h % 2, :].rearrange("p (e n) -> p e n", e=4)[:, :, 0:kn]
                    ps = scores[0:nq].rearrange("p a (j n) -> p (a j) n", j=2)[:, :, 0:kn]
                    mask = const[0:nq, C_MASK + W - k0:C_MASK + W + k1].unsqueeze(1).to_broadcast([nq, 4, kn])
                    ne, nsk, sk = 4, nsink[0:nq, kv, :], sink[0:nq, kv, :]
                else:
                    nq, ne = P, 1
                    sv, ps = scores_sb[:, h % 2, 0:SK], scores.rearrange("p a n -> p (a n)")[:, 0:SK]
                    mask = const[:, C_SMASK:C_SMASK + SK]
                    nsk, sk = ssink[:, 1:2], ssink[:, 0:1]
                nc.vector.scalar_tensor_tensor(out=sv, in0=ps, scalar=QK_SCALE, in1=mask, op0=ALU.mult, op1=ALU.add)\
                    .then_inc(scores_read, 1)
                dve.wait_ge(scores_read, h + 1)
                then(nc.vector.tensor_reduce(s[0:nq, MX, 0:ne], sv, AX_X, ALU.max))
                then(nc.vector.scalar_tensor_tensor(out=s[0:nq, NM, 0:ne], in0=s[0:nq, MX, 0:ne], scalar=-1.0, in1=nsk,
                                                    op0=ALU.mult, op1=ALU.min))
                nc.vector.tensor_tensor(s[0:nq, DS, 0:ne], sk, s[0:nq, NM, 0:ne], ALU.add).then_inc(soft_in, 1)

            def normalise(h):
                s = soft[:, h % 2]
                nq, ne = (half(h)[2], 4) if h < N_HALF else (P, 1)
                dve.wait_ge(exp_done, h + 1)
                then(nc.vector.tensor_tensor(s[0:nq, RC, 0:ne], s[0:nq, RS, 0:ne], s[0:nq, ES, 0:ne], ALU.add))
                then(nc.vector.reciprocal(s[0:nq, RC, 0:ne], s[0:nq, RC, 0:ne]))
                for e in range(ne):
                    kn = sum(half(h)[4:6]) if h < N_HALF else SK
                    pr = scores_sb[0:nq, h % 2, 256 * e:256 * e + kn]
                    ins_ = nc.vector.tensor_scalar(pr, pr, s[0:nq, RC, e:e + 1], None, ALU.mult)
                ins_.then_inc(probs_ready, 1)

            def copy_attn(h):
                dve.wait_ge(pv_ready, h + 1)
                if h < N_HALF:
                    kv, q0, nq = half(h)[:3]
                    dst = qT[:, 2 * kv:2 * kv + 2, q0:q0 + nq]
                    src = turned[:, 0:2 * nq].rearrange("p (j n) -> p j n", j=2)
                else:
                    a = h - N_HALF
                    dst = qT[:, :, NPR + 16 * a:NPR + 16 * (a + 1)]
                    src = turned[:, 0:64].rearrange("p (c n) -> p c n", c=4)
                nc.vector.tensor_copy(dst, src).then_inc(attn_copied, 1)

            def sample_u(first, n):
                return conv_u[:, U_S:U_S + 6 * NB_S].rearrange("p (b r) -> p b r", r=6)[:, :, first:first + n]

            def conv(s):
                j, p, part = s // 9, (s % 9) // 3, s % 3
                c0, c1 = PIECES[p]
                n = c1 - c0
                acc = out_bank[(18 + s) % 4][:, 0:n]
                n_pr = min(c1, NPR) - c0
                parts = [(slice(0, n_pr), None)] + ([(slice(n_pr, n), True)] if n > n_pr else [])

                def rows(sl, samples, ap):
                    v = ap[:, sl]
                    return v.rearrange("p (b t) -> p b t", t=T_S) if samples else v

                dve.wait_ge(out_ready, 18 + s + 1)
                if part == 0:
                    if p == 0:
                        nc.vector.tensor_copy(sample_u(0, 2), conv_state[:, j, :].rearrange("p (b r) -> p b r", r=2))
                    nc.vector.tensor_tensor(xa_sb[:, 0:n], acc, rs_squared[:, c0:c1], ALU.mult).then_inc(out_freed, 1)
                    dve.wait_ge(out_freed, 18 + s + 1)
                elif part == 1:
                    for sl, samples in parts:
                        dst = sample_u(2, T_S) if samples else conv_u[:, 2 + c0:2 + c0 + n_pr]
                        ins_ = nc.vector.tensor_tensor(dst, rows(sl, samples, acc), rows(sl, samples, xa_sb), ALU.mult)
                    ins_.then_inc(out_freed, 1)
                    dve.wait_ge(out_freed, 18 + s + 1)
                    for tap in range(3):
                        row = R_CONV + 4 * tap + j
                        wt = prm[:, row:row + 1]
                        for sl, samples in parts:
                            src = sample_u(tap, T_S) if samples else conv_u[:, c0 + tap:c0 + tap + n_pr]
                            y = rows(sl, samples, conv_y)
                            if tap == 0:
                                ins_ = nc.vector.tensor_scalar(y, src, wt, None, ALU.mult)
                            else:
                                ins_ = nc.vector.scalar_tensor_tensor(out=y, in0=src, scalar=wt, in1=y, op0=ALU.mult,
                                                                      op1=ALU.add)
                        then(ins_)
                    then(nc.vector.tensor_tensor(conv_y[:, 0:n], conv_y[:, 0:n], rs[:, c0:c1], ALU.mult))
                    if p == 2:
                        nc.vector.tensor_copy(conv_tail[:, j, 0:2], conv_u[:, 2 + NPR - 2:2 + NPR])
                        nc.vector.tensor_copy(conv_tail[:, j, 2:18].rearrange("p (b r) -> p b r", r=2), sample_u(4, 2))\
                            .then_inc(tail_gathered, 1)
                else:
                    nc.vector.tensor_tensor(conv_out[:, j, c0:c1], acc, conv_y[:, 0:n], ALU.mult).then_inc(out_freed, 1)
                if p == 2:
                    split_lo(6 + 3 * j + part + 4)

            def mix_lo(i):
                first, src = ((0, conv_out), (4, qT))[i // 3]
                c0, c1 = PIECES[i % 3]
                dve.wait_ge(mix_hi, i + 1)
                nc.vector.tensor_tensor(act_lo[:, first:first + 4, c0:c1], src[:, :, c0:c1],
                                        f32(act_hi[:, first:first + 4, c0:c1]), ALU.subtract).then_inc(mix_ready, 1)

            for s in range(SLOTS):
                for h in range(HALVES):
                    if START[h] == s:
                        mask_and_max(h)
                for h in range(HALVES):
                    if START[h] + PV_LAG == s:
                        copy_attn(h)
                conv(s)
                for h in range(HALVES):
                    if START[h] + T_LAG - 1 == s:
                        normalise(h)
                if s in (31, 34):
                    mix_lo((s - 31) // 3)
            for h in range(HALVES):
                if START[h] + PV_LAG >= SLOTS:
                    copy_attn(h)

            mix_lo(2)
            for i in range(3, 6):
                mix_lo(i)

            for p, (c0, c1) in enumerate(PIECES):
                for oc in range(KC):
                    m = M_OUT + 8 * p + oc
                    dve.wait_ge(x_again_in[oc], 16 * (p + 1))
                    dve.wait_ge(out_ready, m + 1)
                    nc.vector.tensor_tensor(xT[:, oc, c0:c1], out_bank[m % 4][:, 0:c1 - c0], x_again[:, oc, 0:c1 - c0],
                                            ALU.add).then_inc(out_freed, 1)
                    if p == 2 and oc % 2:
                        split_lo(W_OUT + 4 + oc // 2)

            def add_output(m, oc, piece, g=0):
                c0, c1 = piece
                dve.wait_ge(out_ready, g * GROUP_OUTS + (m + 1))
                nc.vector.tensor_tensor(xT[:, oc, c0:c1], out_bank[m % 4][:, 0:c1 - c0], xT[:, oc, c0:c1], ALU.add)\
                    .then_inc(out_freed, 1)

            def normed_passes(n, mb, w0, before_last=None):
                for p in range(3):
                    for oc in range(KC):
                        add_output(mb + 8 * p + oc, oc, PIECES[p])
                        if p and oc == 0:
                            norm_split_lo(n, p - 1, 2)
                            norm_split_lo(n, p - 1, 3)
                            norm_reduce(n, p - 1, 1)
                        if p == 2 and oc % 2:
                            split_lo(w0 + oc // 2)
                        if oc in (2, 4):
                            norm_split_lo(n, p, oc // 2 - 1)
                        if oc == 5:
                            norm_reduce(n, p, 0)
                        if p and oc == 6:
                            norm_rsqrt(n, p - 1)
                if before_last:
                    before_last()
                norm_split_lo(n, 2, 2)
                norm_split_lo(n, 2, 3)
                norm_reduce(n, 2, 1)

            normed_passes(1, M_OUT + 24, W_OUT + 8)

            def relu_scaled(layer, mb, g, q, p):
                m = mb + q
                c0, c1 = (PIECES, PIECES1)[layer][p]
                n = c1 - c0
                dve.wait_ge(out_ready, g * GROUP_OUTS + (m + 1))
                nc.vector.scalar_tensor_tensor(out=relu[:, q % 2, 0:n], in0=out_bank[m % 4][:, 0:n], scalar=0.0,
                                               in1=rs[:, c0:c1], op0=ALU.max, op1=ALU.mult).then_inc(out_freed, 1)

            def hidden_lo(layer, hb, g, q, p, chunk):
                n = (PIECES, PIECES1)[layer][p][1] - (PIECES, PIECES1)[layer][p][0]
                dve.wait_ge(hid_hi_done, g * UP_OUTS + (hb + q + 1))
                nc.vector.tensor_tensor(hid_lo[p][:, chunk, 0:n], sq[:, q % 2, 0:n], f32(hid_hi[p][:, chunk, 0:n]),
                                        ALU.subtract).then_inc(hid_ready, 1)

            def hidden(layer, mb, hb, g, q, p, chunk):
                relu_scaled(layer, mb, g, q, p)
                hidden_lo(layer, hb, g, q, p, chunk)

            def up(layer, mb, wb, hb, g, after=None):
                for u in range(2):
                    for p in range(3):
                        for i in range(2):
                            hidden(layer, mb, hb, g, 6 * u + 2 * p + i, p, 2 * u + i)
                        if after:
                            after(u, p)
                    for i in range(2):
                        split_lo(wb + 4 + 2 * u + i, g, 8)

            def down(layer, mb, wb, g):
                for p in range(3):
                    for oc in range(KC):
                        add_output(mb + UP_OUTS + 8 * p + oc, oc, (PIECES, PIECES1)[layer][p], g)
                        if p == 2 and oc % 2:
                            split_lo(wb + 8 + oc // 2, g, 8)

            def up_by_piece(mb, wb, hb):
                dve.wait_ge(stored_pool, 16 * N_STORES)
                for p in range(3):
                    for s in range(4):
                        if (p, s) == (0, 0):
                            norm_rsqrt(3, 1)
                        if (p, s) == (1, 2):
                            norm_rsqrt(3, 2)
                        hidden(1, mb, hb, 0, 4 * p + s, p, s)
                        if p == 2:
                            split_lo(wb + 4 + s)

            def mlp(layer, mb, wb, hb, after):
                if layer == 0:
                    up(layer, mb, wb, hb, 0, after)
                else:
                    up_by_piece(mb, wb, hb)
                down(layer, mb, wb, 0)
                with dve.Fori(1, GROUPS - 1) as g:
                    up(layer, mb, wb, hb, g)
                    down(layer, mb, wb, g)
                last = GROUPS - 1
                up(layer, mb + GROUP_OUTS * last, wb + 8 * last, hb + UP_OUTS * last, 0)

            mlp(0, M_MLP0, W_MLP0, 0, lambda u, p: norm_rsqrt(1, 2) if (u, p) == (0, 1) else None)

            def scale_map(i):
                n = TILES[i][1] - TILES[i][0]
                for half_ in range(2):
                    m = map_output(i, half_)
                    dve.wait_ge(out_ready, m + 1)
                    nc.vector.tensor_scalar(z[0:n, i % 3, 512 * half_:512 * (half_ + 1)], out_bank[m % 4][0:n, :],
                                            rs_rows[0:n, i:i + 1], None, ALU.mult).then_inc(out_freed, 1)

            def add_windows(i):
                t0, t1 = TILES[i]
                skip = N_META if i == 0 else 0
                for half_ in range(2):
                    m = window_output(i, half_)
                    dve.wait_ge(out_ready, m + 1)
                    for cc in range(4):
                        c = 4 * half_ + cc
                        x = xT[:, c, t0 + skip:t1]
                        ins_ = nc.vector.scalar_tensor_tensor(out=x, in0=out_bank[m % 4][:, P * cc + skip:P * cc + t1 - t0],
                                                              scalar=prm[:, R_SCALE + c:R_SCALE + c + 1], in1=x,
                                                              op0=ALU.mult, op1=ALU.add)
                    ins_.then_inc(out_freed, 1)

            normed_passes(2, M_POOL - 24, W_POOL, 
                          lambda: (scale_map(0), scale_map(1), add_windows(0), scale_map(2)))
            for c in range(KC):
                ins_ = nc.vector.tensor_scalar(pool_tail[:, c, :], xT[:, c, NPR - PM:NT], gain(2, c), None, ALU.mult)
            ins_.then_inc(pool_gathered, 1)
            dve.wait_ge(pool_gathered, 1)
            for i in range(2, 9):
                if i > 2:
                    scale_map(i)
                if i in (5, 8):
                    norm_reduce(3, i // 3 - 1, 0)
                add_windows(i - 1)
                if i == 3:
                    norm_rsqrt(2, 2)
                if i in (4, 7):
                    for pair in range(4):
                        norm_split_lo(3, i // 3 - 1, pair)
                if i in (5, 8):
                    norm_reduce(3, i // 3 - 1, 1)
                if i == 8:
                    norm_rsqrt(3, 0)
            add_windows(8)
            split_lo(W_MLP1 + 2)
            split_lo(W_MLP1 + 3)
            norm_splits(3, 2)

            mlp(1, M_MLP1, W_MLP1, 96, None)

            def copy_y(t):
                n = P if t < 8 else NS
                dve.wait_ge(fin_turned, 2 * t + 1)
                nc.vector.tensor_copy(y_rows[0:n, t, 0:512], fin_bank[(2 * t) % 4][0:n, :]).then_inc(fin_dve, 1)

            mb = M_MLP1 + GROUP_OUTS * (GROUPS - 1) + UP_OUTS
            for p in range(3):
                for oc in range(KC):
                    add_output(mb + 8 * p + oc, oc, PIECES1[p])
                    if p == 1 and oc == 4:
                        copy_y(0)
                        copy_y(1)
                    if p == 2 and oc in (2, 4, 6):
                        copy_y(1 + oc // 2)
            for t in range(5, 9):
                copy_y(t)


N_STORES = 3 + 2 + 2 * NB_S + 2 + 1 + NB_S

_INS = ["x_prompt", "x_sample", "state_conv", "cache_k_win", "cache_v_win", "state_pool", "meta_tokens", "norm_mix",
        "norm_mlp", "w_in_even", "conv_w", "q_norm", "k_norm", "attn_sinks", "w_out_even", "w_pool", "pool_scale",
        "w_up", "w_down"]
_OUTS = [("y_prompt", (1, SEQ, D)), ("y_sample", (NB_S, T_S, D)), ("conv_prompt", (1, 1, 2, 512)),
         ("conv_sample", (1, NB_S, 2, 512)), ("k_prompt", (1, 1, W, N_KV, DH)), ("k_sample", (1, NB_S, W, N_KV, DH)),
         ("v_prompt", (1, 1, W, N_KV, DH)), ("v_sample", (1, NB_S, W, N_KV, DH)), ("pool_prompt", (1, 1, PM, D)),
         ("pool_sample", (1, NB_S, PM, D))]


def kernel(**inputs):
    import concourse.bacc as _bacc
    from concourse.bass_utils import run_bass_kernel_spmd as _run

    nc = _bacc.Bacc("TRN2", target_bir_lowering=False, num_devices=1)
    arrays = {n: np.ascontiguousarray(inputs[n]) for n in _INS}
    arrays["const"] = constants()
    arrays["bands"] = bands()
    ins = {n: nc.dram_tensor(f"in_{n}", a.shape, F32, kind="ExternalInput").ap() for n, a in arrays.items()}
    outs = {n: nc.dram_tensor(f"out_{n}", s, F32, kind="ExternalOutput").ap() for n, s in _OUTS}
    trunk_kernel(nc, ins, outs)
    r = _run(nc, [{f"in_{n}": a for n, a in arrays.items()}], core_ids=[0])
    return tuple(r.results[0][f"out_{n}"] for n, _ in _OUTS)
```
